# Optimizing a Trainium2 kernel written in Bass

```python
import math
import jax, jax.numpy as jnp
from jax import lax
import numpy as np

D_MODEL = 1024
BATCH = 1
SEQ = 256
DEPTH = 2

N_MIXERS = 2
N_RWKV_LAYERS = (DEPTH + N_MIXERS - 1) // N_MIXERS
N_DIFF_LAYERS = DEPTH // N_MIXERS
NORM_EPS = 1e-6

RW_HEAD = 64
RW_HEADS = D_MODEL // RW_HEAD
RW_WIDTH = RW_HEADS * RW_HEAD
RW_N_PROJ = 4
RW_N_MIX = 6
DECAY_LORA = max(32, int(round(1.8 * D_MODEL ** 0.5 / 32)) * 32)
ICLR_LORA = max(32, int(round(1.8 * D_MODEL ** 0.5 / 32)) * 32)
GN_EPS = 64e-5

DA_HEADS = 8
DA_QK_DIM = D_MODEL // DA_HEADS // 2
DA_V_DIM = 2 * DA_QK_DIM
DA_WIDTH = DA_HEADS * DA_V_DIM
DA_SUBLN_EPS = 1e-5
ROPE_THETA = 10000.0
Q_BLOCK = 128

PLE_DIM = 256


def rms_norm(x, g, eps=NORM_EPS):
    xf = x.astype(jnp.float32)
    y = xf * lax.rsqrt(jnp.mean(xf * xf, axis=-1, keepdims=True) + eps)
    return (y * g.astype(jnp.float32)).astype(x.dtype)

def token_shift(x):
    return jnp.pad(x, ((0, 0), (1, 0), (0, 0)))[:, :-1]

def rwkv7_mixer(h, mu, w_in, w0, w1, w2, a0, a1, a2, k_k, k_a, r_k, ln_w, ln_b, w_out):
    B, S, _ = h.shape
    H, N = RW_HEADS, RW_HEAD
    f32 = jnp.float32
    dx = token_shift(h) - h
    xm = h[:, :, None, :] + dx[:, :, None, :] * mu[:RW_N_PROJ]
    proj = jnp.einsum('bsgd,dgc->bsgc', xm, w_in.reshape(D_MODEL, RW_N_PROJ, RW_WIDTH))
    r, k, v, gate = proj[:, :, 0], proj[:, :, 1], proj[:, :, 2], proj[:, :, 3]
    xw = h + dx * mu[4]
    xa = h + dx * mu[5]
    w_log = -jax.nn.softplus(-(w0 + jnp.tanh(xw @ w1) @ w2).astype(f32)) - 0.5
    decay = jnp.exp(-jnp.exp(w_log))
    a = jax.nn.sigmoid((a0 + (xa @ a1) @ a2).astype(f32))
    kk = (k * k_k).reshape(B, S, H, N).astype(f32)
    kk = kk / jnp.maximum(jnp.sqrt(jnp.sum(kk * kk, axis=-1, keepdims=True)), 1e-12)
    k = k.astype(f32) * (1.0 + (a - 1.0) * k_a.astype(f32))

    def heads(t):
        return t.reshape(B, S, H, N).astype(f32)

    rh, kh, vh, wh, ah = heads(r), heads(k), heads(v), heads(decay), heads(a)
    bh = kk * ah

    def step(state, inp):
        r_t, w_t, k_t, v_t, kk_t, b_t = inp
        sa = jnp.einsum('bhij,bhj->bhi', state, kk_t)
        state = (state * w_t[:, :, None, :] - sa[..., None] * b_t[:, :, None, :]
                 + v_t[..., None] * k_t[:, :, None, :])
        y_t = jnp.einsum('bhij,bhj->bhi', state, r_t)
        return state, y_t

    seq_first = lambda t: jnp.swapaxes(t, 0, 1)
    s0 = jnp.zeros((B, H, N, N), f32)
    _, y = lax.scan(step, s0, (seq_first(rh), seq_first(wh), seq_first(kh),
                               seq_first(vh), seq_first(kk), seq_first(bh)))
    y = jnp.swapaxes(y, 0, 1)
    mean = jnp.mean(y, axis=-1, keepdims=True)
    var = jnp.mean(jnp.square(y - mean), axis=-1, keepdims=True)
    y = ((y - mean) * lax.rsqrt(var + GN_EPS) * ln_w.reshape(H, N).astype(f32)
         + ln_b.reshape(H, N).astype(f32))
    bonus = jnp.sum(rh * kh * r_k.astype(f32), axis=-1, keepdims=True) * vh
    y = (y + bonus).reshape(B, S, RW_WIDTH).astype(h.dtype)
    return (y * jax.nn.silu(gate)) @ w_out

def rope(x, cos, sin):
    half = x.shape[-1] // 2
    x1, x2 = x[..., :half], x[..., half:]
    rot = jnp.concatenate([-x2, x1], axis=-1)
    return (x * cos + rot * sin).astype(x.dtype)

def diff_attn_mixer(h, w_in, lq1, lk1, lq2, lk2, subln, w_out, lambda_init):
    B, S, _ = h.shape
    H, dk, dv = DA_HEADS, DA_QK_DIM, DA_V_DIM
    f32 = jnp.float32
    nb = S // Q_BLOCK
    proj = h @ w_in
    q, k, v, gate = jnp.split(proj, [2 * H * dk, 4 * H * dk, 4 * H * dk + H * dv], axis=-1)
    q = q.reshape(B, S, H, 2, dk)
    k = k.reshape(B, S, H, 2, dk)
    v = v.reshape(B, S, H, dv)
    pos = jnp.arange(S, dtype=f32)
    inv_freq = 1.0 / (ROPE_THETA ** (jnp.arange(0, dk, 2, dtype=f32) / dk))
    ang = pos[:, None] * inv_freq[None, :]
    ang = jnp.concatenate([ang, ang], axis=-1)
    cos = jnp.cos(ang)[:, None, None, :]
    sin = jnp.sin(ang)[:, None, None, :]
    q = rope(q, cos, sin)
    k = rope(k, cos, sin)
    lam = (jnp.exp(jnp.sum(lq1.astype(f32) * lk1.astype(f32)))
           - jnp.exp(jnp.sum(lq2.astype(f32) * lk2.astype(f32))) + lambda_init)
    scale = dk ** -0.5
    qb = q.reshape(B, nb, Q_BLOCK, H, 2, dk).transpose(1, 0, 3, 4, 2, 5)
    kt = k.transpose(0, 2, 3, 1, 4)
    vt = v.transpose(0, 2, 1, 3)
    key_pos = jnp.arange(S)

    def block(args):
        i, qi = args
        s = jnp.einsum('bhcqd,bhckd->bhcqk', qi, kt).astype(f32) * scale
        q_pos = i * Q_BLOCK + jnp.arange(Q_BLOCK)
        s = jnp.where(key_pos[None, :] <= q_pos[:, None], s, -jnp.inf)
        pr = jax.nn.softmax(s, axis=-1)
        att = pr[:, :, 0] - lam * pr[:, :, 1]
        return jnp.einsum('bhqk,bhkd->bhqd', att.astype(vt.dtype), vt)

    o = lax.map(block, (jnp.arange(nb), qb))
    o = o.transpose(1, 0, 3, 2, 4).reshape(B, S, H, dv)
    o = rms_norm(o, subln, DA_SUBLN_EPS) * (1.0 - lambda_init)
    o = o.reshape(B, S, DA_WIDTH)
    return (o * jax.nn.silu(gate)) @ w_out

def first_inputs(seed: int = 0) -> dict:
    key = jax.random.key(seed)
    ks = iter(jax.random.split(key, 40))
    nrm = lambda shape, s: jax.random.normal(next(ks), shape, jnp.float32) * s
    NA, NB, D, C = N_RWKV_LAYERS, N_DIFF_LAYERS, D_MODEL, RW_WIDTH
    lin = jnp.linspace(0.0, 1.0, C, dtype=jnp.float32)
    return {
        'x': nrm((BATCH, SEQ, D), 1.0),
        'p': nrm((DEPTH, BATCH, SEQ, PLE_DIM), 1.0),
        'rw_norm': 1.0 + nrm((NA, D), 0.05),
        'rw_mu': jax.random.uniform(next(ks), (NA, RW_N_MIX, D), jnp.float32),
        'rw_w_in': nrm((NA, D, RW_N_PROJ * C), D ** -0.5),
        'rw_w0': (-7.0 + 5.0 * lin ** 0.85 + 0.5)[None, :] + nrm((NA, C), 0.1),
        'rw_w1': nrm((NA, D, DECAY_LORA), D ** -0.5),
        'rw_w2': nrm((NA, DECAY_LORA, C), 0.1 * DECAY_LORA ** -0.5),
        'rw_a0': nrm((NA, C), 0.1),
        'rw_a1': nrm((NA, D, ICLR_LORA), D ** -0.5),
        'rw_a2': nrm((NA, ICLR_LORA, C), 0.3 * ICLR_LORA ** -0.5),
        'rw_k_k': 0.85 + nrm((NA, C), 0.05),
        'rw_k_a': 1.0 + nrm((NA, C), 0.05),
        'rw_r_k': nrm((NA, RW_HEADS, RW_HEAD), 0.1),
        'rw_ln_w': 1.0 + nrm((NA, C), 0.05),
        'rw_ln_b': nrm((NA, C), 0.02),
        'rw_w_out': nrm((NA, C, D), C ** -0.5),
        'da_norm': 1.0 + nrm((NB, D), 0.05),
        'da_w_in': nrm((NB, D, 4 * DA_HEADS * DA_QK_DIM + 2 * DA_WIDTH), D ** -0.5),
        'da_lq1': nrm((NB, DA_QK_DIM), 0.1),
        'da_lk1': nrm((NB, DA_QK_DIM), 0.1),
        'da_lq2': nrm((NB, DA_QK_DIM), 0.1),
        'da_lk2': nrm((NB, DA_QK_DIM), 0.1),
        'da_subln': 1.0 + nrm((NB, DA_V_DIM), 0.05),
        'da_w_out': nrm((NB, DA_WIDTH, D), DA_WIDTH ** -0.5),
        'pe_norm': 1.0 + nrm((DEPTH, D), 0.05),
        'pe_w_gate': nrm((DEPTH, D, D), D ** -0.5),
        'pe_w_proj': nrm((DEPTH, PLE_DIM, D), PLE_DIM ** -0.5),
        'final_norm': 1.0 + nrm((D,), 0.05),
    }

def first_block(x, p, rw_norm, rw_mu, rw_w_in, rw_w0, rw_w1, rw_w2, rw_a0, rw_a1, rw_a2,
              rw_k_k, rw_k_a, rw_r_k, rw_ln_w, rw_ln_b, rw_w_out,
              da_norm, da_w_in, da_lq1, da_lk1, da_lq2, da_lk2, da_subln, da_w_out,
              pe_norm, pe_w_gate, pe_w_proj, final_norm):
    h = x
    for i in range(DEPTH):
        j = i // N_MIXERS
        if i % N_MIXERS == 0:
            h = h + rwkv7_mixer(rms_norm(h, rw_norm[j]), rw_mu[j], rw_w_in[j], rw_w0[j], rw_w1[j],
                                rw_w2[j], rw_a0[j], rw_a1[j], rw_a2[j], rw_k_k[j], rw_k_a[j],
                                rw_r_k[j], rw_ln_w[j], rw_ln_b[j], rw_w_out[j])
        else:
            lambda_init = 0.8 - 0.6 * math.exp(-0.3 * i)
            h = h + diff_attn_mixer(rms_norm(h, da_norm[j]), da_w_in[j], da_lq1[j], da_lk1[j],
                                    da_lq2[j], da_lk2[j], da_subln[j], da_w_out[j], lambda_init)
        g = jax.nn.sigmoid(rms_norm(h, pe_norm[i]) @ pe_w_gate[i])
        h = h + g * (p[i] @ pe_w_proj[i])
    return rms_norm(h, final_norm)


N_A_LAYERS = DEPTH // 2
N_B_LAYERS = DEPTH - N_A_LAYERS
D_FF = 2816
FFN_HALF = 0.5
SSM_EXPAND = 2
SSM_D_INNER = SSM_EXPAND * D_MODEL
SSM_HEAD_DIM = 64
SSM_HEADS = SSM_D_INNER // SSM_HEAD_DIM
SSM_GROUPS = 4
SSM_STATE = 128
SSM_CONV = 4
SSM_CHUNK = 256
SSM_CONV_DIM = SSM_D_INNER + 2 * SSM_GROUPS * SSM_STATE
SSM_IN_DIM = SSM_D_INNER + SSM_CONV_DIM + SSM_HEADS
ATT_HEAD_DIM = 64
ATT_HEADS = D_MODEL // ATT_HEAD_DIM
ATT_KV_HEADS = ATT_HEADS // 8
ATT_GROUP = ATT_HEADS // ATT_KV_HEADS
ATT_WINDOW = 128
ATT_BLOCK = ATT_WINDOW
REL_BUCKETS = 32
REL_MAX_DIST = ATT_WINDOW
EPS = 1e-6


def rmsnorm(x, g):
    xf = x.astype(jnp.float32)
    y = xf * lax.rsqrt(jnp.mean(xf * xf, axis=-1, keepdims=True) + EPS)
    return (y * g.astype(jnp.float32)).astype(x.dtype)

def swiglu_half_step(h, g, w1, w3, w2):
    u = rmsnorm(h, g)
    return h + FFN_HALF * ((jax.nn.silu(u @ w1) * (u @ w3)) @ w2)

def causal_depthwise_conv(x, w, b):
    c = x.shape[-1]
    y = lax.conv_general_dilated(
        x, w.astype(x.dtype)[:, None, :], window_strides=(1,),
        padding=[(SSM_CONV - 1, 0)], dimension_numbers=('NWC', 'WIO', 'NWC'),
        feature_group_count=c)
    return y + b.astype(x.dtype)

def ssd_chunked_scan(x, dt, a, b_in, c_in):
    bsz, t, h, p = x.shape
    g, n = b_in.shape[2], b_in.shape[3]
    r = h // g
    L = SSM_CHUNK
    nc = -(-t // L)
    pad = nc * L - t
    f32 = jnp.float32

    def chunks(z):
        z = z.astype(f32)
        z = jnp.pad(z, [(0, 0), (0, pad)] + [(0, 0)] * (z.ndim - 2))
        z = z.reshape((bsz, nc, L) + z.shape[2:])
        return jnp.moveaxis(z, 1, 0)

    xc = chunks(x.reshape(bsz, t, g, r, p))
    dtc = chunks(dt.reshape(bsz, t, g, r))
    bc = chunks(b_in)
    cc = chunks(c_in)
    a_gr = a.astype(f32).reshape(g, r)
    causal = jnp.tril(jnp.ones((L, L), bool))[:, :, None, None]

    def step(state, inp):
        xk, dtk, bk, ck = inp
        acum = jnp.cumsum(dtk * a_gr, axis=1)
        seg = acum[:, :, None] - acum[:, None, :]
        decay = jnp.exp(jnp.where(causal, seg, -jnp.inf))
        cb = jnp.einsum('blgn,bsgn->blsg', ck, bk)
        scores = cb[..., None] * decay
        y_diag = jnp.einsum('blsgr,bsgr,bsgrp->blgrp', scores, dtk, xk)
        y_off = jnp.einsum('blgn,bgrpn,blgr->blgrp', ck, state, jnp.exp(acum))
        w_end = jnp.exp(acum[:, -1:] - acum) * dtk
        state = (state * jnp.exp(acum[:, -1])[..., None, None]
                 + jnp.einsum('bsgn,bsgr,bsgrp->bgrpn', bk, w_end, xk))
        return state, y_diag + y_off

    state0 = jnp.zeros((bsz, g, r, p, n), f32)
    _, y = lax.scan(step, state0, (xc, dtc, bc, cc))
    y = jnp.moveaxis(y, 0, 1).reshape(bsz, nc * L, h, p)[:, :t]
    return y.astype(x.dtype)

def mamba2_mixer(u, w_in, conv_w, conv_b, dt_bias, a_log, d_skip, gate_norm, w_out):
    bsz, t, _ = u.shape
    zxbcdt = u @ w_in
    z, xbc, dt = jnp.split(zxbcdt, [SSM_D_INNER, SSM_D_INNER + SSM_CONV_DIM], axis=-1)
    xbc = jax.nn.silu(causal_depthwise_conv(xbc, conv_w, conv_b))
    xs, b_in, c_in = jnp.split(xbc, [SSM_D_INNER, SSM_D_INNER + SSM_GROUPS * SSM_STATE], axis=-1)
    xs = xs.reshape(bsz, t, SSM_HEADS, SSM_HEAD_DIM)
    b_in = b_in.reshape(bsz, t, SSM_GROUPS, SSM_STATE)
    c_in = c_in.reshape(bsz, t, SSM_GROUPS, SSM_STATE)
    dt = jax.nn.softplus((dt + dt_bias).astype(jnp.float32))
    a = -jnp.exp(a_log.astype(jnp.float32))
    y = ssd_chunked_scan(xs, dt, a, b_in, c_in) + d_skip[:, None].astype(xs.dtype) * xs
    y = y.reshape(bsz, t, SSM_D_INNER) * jax.nn.silu(z)
    y = rmsnorm(y.reshape(bsz, t, SSM_GROUPS, SSM_D_INNER // SSM_GROUPS),
                gate_norm.reshape(SSM_GROUPS, SSM_D_INNER // SSM_GROUPS))
    return y.reshape(bsz, t, SSM_D_INNER) @ w_out

def shared_kv(h, kv_norm, w_kv, k_norm):
    bsz, t, _ = h.shape
    kv = rmsnorm(h, kv_norm) @ w_kv
    k, v = jnp.split(kv, 2, axis=-1)
    k = rmsnorm(k.reshape(bsz, t, ATT_KV_HEADS, ATT_HEAD_DIM), k_norm)
    v = v.reshape(bsz, t, ATT_KV_HEADS, ATT_HEAD_DIM)
    return k, v

def t5_bucket(dist):
    n = jnp.maximum(dist, 0)
    max_exact = REL_BUCKETS // 2
    nf = jnp.maximum(n, 1).astype(jnp.float32)
    large = max_exact + (jnp.log(nf / max_exact) / math.log(REL_MAX_DIST / max_exact)
                         * (REL_BUCKETS - max_exact)).astype(jnp.int32)
    large = jnp.minimum(large, REL_BUCKETS - 1)
    return jnp.where(n < max_exact, n, large)

def sliding_window_attention(u, k, v, w_q, q_norm, sinks, rel_bias, w_o):
    bsz, t, _ = u.shape
    blk = ATT_BLOCK
    nb = t // blk
    q = rmsnorm((u @ w_q).reshape(bsz, t, ATT_KV_HEADS, ATT_GROUP, ATT_HEAD_DIM), q_norm)
    qb = jnp.moveaxis(q.reshape(bsz, nb, blk, ATT_KV_HEADS, ATT_GROUP, ATT_HEAD_DIM), 1, 0)

    def band(z):
        prev = jnp.pad(z, [(0, 0), (blk, 0), (0, 0), (0, 0)])[:, :t]
        zz = jnp.concatenate([prev.reshape(bsz, nb, blk, ATT_KV_HEADS, ATT_HEAD_DIM),
                              z.reshape(bsz, nb, blk, ATT_KV_HEADS, ATT_HEAD_DIM)], axis=2)
        return jnp.moveaxis(zz, 1, 0)

    kb, vb = band(k), band(v)
    qi = jnp.arange(blk)[:, None] + blk
    kj = jnp.arange(2 * blk)[None, :]
    dist = qi - kj
    in_window = (dist >= 0) & (dist < ATT_WINDOW)
    bias = rel_bias[t5_bucket(dist)]
    bias = jnp.transpose(bias.reshape(blk, 2 * blk, ATT_KV_HEADS, ATT_GROUP),
                         (2, 3, 0, 1)).astype(jnp.float32)
    sink = sinks.reshape(ATT_KV_HEADS, ATT_GROUP)[None, :, :, None, None].astype(jnp.float32)
    scale = ATT_HEAD_DIM ** -0.5

    def block(args):
        qk, kk, vk, bi = args
        s = jnp.einsum('bqkrd,bskd->bkrqs', qk, kk).astype(jnp.float32) * scale + bias
        valid = in_window & ((bi > 0) | (kj >= blk))
        s = jnp.where(valid, s, -jnp.inf)
        m = jnp.maximum(jnp.max(s, axis=-1, keepdims=True), sink)
        p = jnp.exp(s - m)
        denom = jnp.sum(p, axis=-1, keepdims=True) + jnp.exp(sink - m)
        return jnp.einsum('bkrqs,bskd->bqkrd', (p / denom).astype(vk.dtype), vk)

    o = lax.map(block, (qb, kb, vb, jnp.arange(nb)))
    o = jnp.moveaxis(o, 0, 1).reshape(bsz, t, ATT_HEADS * ATT_HEAD_DIM)
    return o @ w_o

def second_inputs(seed: int = 0) -> dict:
    key = jax.random.key(seed)
    ks = jax.random.split(key, 24)
    nrm = jax.random.normal
    f32 = jnp.float32
    x = nrm(ks[0], (BATCH, SEQ, D_MODEL), f32)
    ffn_norm = 1.0 + 0.05 * nrm(ks[1], (DEPTH, 2, D_MODEL), f32)
    ffn_w1 = nrm(ks[2], (DEPTH, 2, D_MODEL, D_FF), f32) * D_MODEL ** -0.5
    ffn_w3 = nrm(ks[3], (DEPTH, 2, D_MODEL, D_FF), f32) * D_MODEL ** -0.5
    ffn_w2 = nrm(ks[4], (DEPTH, 2, D_FF, D_MODEL), f32) * D_FF ** -0.5
    ssm_norm = 1.0 + 0.05 * nrm(ks[5], (N_A_LAYERS, D_MODEL), f32)
    ssm_w_in = nrm(ks[6], (N_A_LAYERS, D_MODEL, SSM_IN_DIM), f32) * D_MODEL ** -0.5
    ssm_conv_w = nrm(ks[7], (N_A_LAYERS, SSM_CONV, SSM_CONV_DIM), f32) * SSM_CONV ** -0.5
    ssm_conv_b = 0.01 * nrm(ks[8], (N_A_LAYERS, SSM_CONV_DIM), f32)
    dt0 = jnp.exp(jax.random.uniform(ks[9], (N_A_LAYERS, SSM_HEADS), f32,
                                     math.log(1e-3), math.log(1e-1)))
    ssm_dt_bias = dt0 + jnp.log(-jnp.expm1(-dt0))
    ssm_a_log = jnp.log(jax.random.uniform(ks[10], (N_A_LAYERS, SSM_HEADS), f32, 1.0, 16.0))
    ssm_d = 1.0 + 0.1 * nrm(ks[11], (N_A_LAYERS, SSM_HEADS), f32)
    ssm_gate_norm = 1.0 + 0.05 * nrm(ks[12], (N_A_LAYERS, SSM_D_INNER), f32)
    ssm_w_out = nrm(ks[13], (N_A_LAYERS, SSM_D_INNER, D_MODEL), f32) * SSM_D_INNER ** -0.5
    kv_norm = 1.0 + 0.05 * nrm(ks[14], (D_MODEL,), f32)
    w_kv = nrm(ks[15], (D_MODEL, 2 * ATT_KV_HEADS * ATT_HEAD_DIM), f32) * D_MODEL ** -0.5
    k_norm = 1.0 + 0.05 * nrm(ks[16], (ATT_HEAD_DIM,), f32)
    attn_norm = 1.0 + 0.05 * nrm(ks[17], (N_B_LAYERS, D_MODEL), f32)
    w_q = nrm(ks[18], (N_B_LAYERS, D_MODEL, ATT_HEADS * ATT_HEAD_DIM), f32) * D_MODEL ** -0.5
    q_norm = 1.0 + 0.05 * nrm(ks[19], (N_B_LAYERS, ATT_HEAD_DIM), f32)
    sinks = 0.5 * nrm(ks[20], (N_B_LAYERS, ATT_HEADS), f32)
    w_o = nrm(ks[21], (N_B_LAYERS, ATT_HEADS * ATT_HEAD_DIM, D_MODEL), f32) * (ATT_HEADS * ATT_HEAD_DIM) ** -0.5
    rel_bias = 0.5 * nrm(ks[22], (REL_BUCKETS, ATT_HEADS), f32)
    return {'x': x, 'ffn_norm': ffn_norm, 'ffn_w1': ffn_w1, 'ffn_w3': ffn_w3, 'ffn_w2': ffn_w2,
            'ssm_norm': ssm_norm, 'ssm_w_in': ssm_w_in, 'ssm_conv_w': ssm_conv_w,
            'ssm_conv_b': ssm_conv_b, 'ssm_dt_bias': ssm_dt_bias, 'ssm_a_log': ssm_a_log,
            'ssm_d': ssm_d, 'ssm_gate_norm': ssm_gate_norm, 'ssm_w_out': ssm_w_out,
            'kv_norm': kv_norm, 'w_kv': w_kv, 'k_norm': k_norm,
            'attn_norm': attn_norm, 'w_q': w_q, 'q_norm': q_norm, 'sinks': sinks, 'w_o': w_o,
            'rel_bias': rel_bias}

def second_block(x, ffn_norm, ffn_w1, ffn_w3, ffn_w2,
              ssm_norm, ssm_w_in, ssm_conv_w, ssm_conv_b, ssm_dt_bias, ssm_a_log,
              ssm_d, ssm_gate_norm, ssm_w_out,
              kv_norm, w_kv, k_norm,
              attn_norm, w_q, q_norm, sinks, w_o,
              rel_bias):
    h = x
    k_shared, v_shared = None, None
    for layer in range(DEPTH):
        h = swiglu_half_step(h, ffn_norm[layer, 0], ffn_w1[layer, 0], ffn_w3[layer, 0], ffn_w2[layer, 0])
        if layer < N_A_LAYERS:
            i = layer
            h = h + mamba2_mixer(rmsnorm(h, ssm_norm[i]), ssm_w_in[i], ssm_conv_w[i], ssm_conv_b[i],
                                 ssm_dt_bias[i], ssm_a_log[i], ssm_d[i], ssm_gate_norm[i], ssm_w_out[i])
        else:
            j = layer - N_A_LAYERS
            h = h + sliding_window_attention(rmsnorm(h, attn_norm[j]), k_shared, v_shared,
                                             w_q[j], q_norm[j], sinks[j], rel_bias, w_o[j])
        h = swiglu_half_step(h, ffn_norm[layer, 1], ffn_w1[layer, 1], ffn_w3[layer, 1], ffn_w2[layer, 1])
        if layer == N_A_LAYERS - 1:
            k_shared, v_shared = shared_kv(h, kv_norm, w_kv, k_norm)
    return h


def setup_inputs(seed=0):
    out = dict(first_inputs(seed))
    for name, value in second_inputs(seed + 1).items():
        if name != "x":
            out[name + "_2"] = value
    return out


def reference(
    x, p, rw_norm, rw_mu, rw_w_in, rw_w0, rw_w1, rw_w2, rw_a0, rw_a1, rw_a2, rw_k_k, rw_k_a,
    rw_r_k, rw_ln_w, rw_ln_b, rw_w_out, da_norm, da_w_in, da_lq1, da_lk1, da_lq2, da_lk2,
    da_subln, da_w_out, pe_norm, pe_w_gate, pe_w_proj, final_norm, ffn_norm_2, ffn_w1_2,
    ffn_w3_2, ffn_w2_2, ssm_norm_2, ssm_w_in_2, ssm_conv_w_2, ssm_conv_b_2, ssm_dt_bias_2,
    ssm_a_log_2, ssm_d_2, ssm_gate_norm_2, ssm_w_out_2, kv_norm_2, w_kv_2, k_norm_2,
    attn_norm_2, w_q_2, q_norm_2, sinks_2, w_o_2, rel_bias_2,
):
    x = first_block(
        x, p, rw_norm, rw_mu, rw_w_in, rw_w0, rw_w1, rw_w2, rw_a0, rw_a1, rw_a2, rw_k_k, rw_k_a,
        rw_r_k, rw_ln_w, rw_ln_b, rw_w_out, da_norm, da_w_in, da_lq1, da_lk1, da_lq2, da_lk2,
        da_subln, da_w_out, pe_norm, pe_w_gate, pe_w_proj, final_norm,
    )
    return second_block(
        x, ffn_norm_2, ffn_w1_2, ffn_w3_2, ffn_w2_2, ssm_norm_2, ssm_w_in_2, ssm_conv_w_2,
        ssm_conv_b_2, ssm_dt_bias_2, ssm_a_log_2, ssm_d_2, ssm_gate_norm_2, ssm_w_out_2,
        kv_norm_2, w_kv_2, k_norm_2, attn_norm_2, w_q_2, q_norm_2, sinks_2, w_o_2, rel_bias_2,
    )


_drawn_inputs = setup_inputs


def setup_inputs(seed=0):
    import zlib

    import numpy as np

    out = dict(_drawn_inputs(seed))
    spreads = {}
    factors = {'rw_w1': 8.0,
     'rw_w2': 8.0,
     'rw_k_k': 2.859,
     'rw_ln_b': 4.516,
     'da_lq1': 5.737,
     'da_lk1': 8.0,
     'da_lq2': 4.596,
     'da_lk2': 7.792,
     'pe_norm': 3.29,
     'ssm_conv_b_2': 5.06,
     'kv_norm_2': 5.269,
     'k_norm_2': 8.0,
     'attn_norm_2': 8.0,
     'q_norm_2': 8.0,
     'sinks_2': 36.324}
    for name, (base, spread) in spreads.items():
        noise = np.random.default_rng([zlib.crc32(name.encode()), seed]).standard_normal(out[name].shape)
        drawn = base * np.exp(spread * noise) if base else spread * noise
        out[name] = __import__('jax').numpy.asarray(drawn.astype(out[name].dtype))
    for name, factor in factors.items():
        out[name] = (out[name] * factor).astype(out[name].dtype)
    return out
```

```python
from contextlib import ExitStack
import math

import numpy as np
import concourse.bass as bass
from concourse import mybir

F32 = mybir.dt.float32
F32R = mybir.dt.float32r
ALU = mybir.AluOpType
ACT = mybir.ActivationFunctionType
X = mybir.AxisListType.X

P = 128
T = 256
TT = T // P
D = 1024
KD = D // P
FF = 2816
KF = FF // P
COLS = 512
SLAB_K = 4
BANKS = 8
RAW_SLOTS, PART_SLOTS = 3, 3
ROW_SLOTS = 2
DECAY = math.exp(-0.5)
NEG = -1.0e30
LAMBDA_INIT = 0.8 - 0.6 * math.exp(-0.3)

SSM_H = 32
CONV_ORDER = (4, 5, 0, 1, 2, 3)
BIAS_N = 3 * P

STAGES = ["rw", "ple0", "da", "ple1", "final", "ffn0", "ssm", "ffn1", "kv", "ffn2", "swa", "ffn3"]


def column_blocks(n):
    return [(c, min(COLS, n - c)) for c in range(0, n, COLS)]


CONST_COLS = [
    ("ident", P),
    ("flip", P),
    ("strict_incl", 2 * P),
    ("levels", 7 * P),
    ("level0_t", P),
    ("cum", P),
    ("cumx", P),
    ("ends", 2),
    ("causal", 2 * P),
    ("cos", TT * 64), ("sin", TT * 64),
    ("tri", 2 * P),
]
CONST_AT, N_CONST = {}, 0
for _name, _n in CONST_COLS:
    CONST_AT[_name] = (N_CONST, N_CONST + _n)
    N_CONST += _n


def constants():
    f = np.float32
    a, b = np.arange(P)[:, None], np.arange(P)[None, :]
    levels = []
    for l in range(7):
        m = 1 << l
        levels.append((a // (2 * m) == b // (2 * m)) & ((a // m) % 2 == 1) & ((b // m) % 2 == 0))
    half = 64 // 2
    inv_freq = 1.0 / (10000.0 ** (np.arange(0, 64, 2, dtype=f) / f(64)))
    ang = np.arange(T, dtype=f)[:, None] * inv_freq[None, :].astype(f)
    ang = np.concatenate([ang, ang], 1)
    sign = np.concatenate([-np.ones(half), np.ones(half)])[None, :]

    def tiles(x):
        return x.reshape(TT, P, 64).transpose(1, 0, 2).reshape(P, TT * 64)

    parts = {
        "ident": a == b, "flip": a + b == P - 1, "strict_incl": np.concatenate([a < b, a <= b], 1),
        "levels": np.concatenate(levels, 1), "level0_t": levels[0].T,
        "cum": -DECAY * ((a <= b) * 1.0 - (a < 64)), "cumx": -DECAY * ((a < b) * 1.0 - (a < 64)),
        "ends": np.concatenate([-DECAY * (a >= 64), -DECAY * (a < 64)], 1),
        "causal": np.concatenate([np.zeros((P, P)), np.where(b > a, NEG, 0.0)], 1),
        "cos": tiles(np.cos(ang)), "sin": tiles(np.sin(ang) * sign),
        "tri": np.concatenate([a <= b, np.ones((P, P))], 1),
    }
    return np.ascontiguousarray(np.concatenate([parts[n].astype(f) for n, _ in CONST_COLS], 1))


def bias_picks():
    f = np.float32
    dist = np.arange(BIAS_N) - 127
    n = np.maximum(dist, 0)
    large = 16 + (np.log(np.maximum(n, 1).astype(f) / f(16)) / f(math.log(128 / 16)) * f(16)).astype(np.int32)
    bucket = np.where(n < 16, n, np.minimum(large, 31))
    inside = (dist >= 0) & (dist < 128)
    picks = np.zeros((33, BIAS_N), f)
    picks[bucket, np.arange(BIAS_N)] = inside
    picks[32] = np.where(inside, 0.0, NEG)
    return picks


class Order:

    def __init__(self, eng, sem):
        self.eng, self.sem, self.n = eng, sem, 0
        self.last = None

    def step(self, ins):
        ins.then_inc(self.sem, 1)
        self.n += 1
        self.last = (self.sem, self.n)

    def settle(self):
        self.eng.wait_ge(*self.last)


class Plan:

    def __init__(self):
        self.jobs = {}
        self.slabs = []
        self.gemms = {}
        self.used = 0

    def job(self, *name):
        assert name not in self.jobs, name
        self.jobs[name] = len(self.jobs)

    def gemm_by_channel(self, name, w, c0):
        first = len(self.slabs)
        for k0 in range(0, KD, SLAB_K):
            self.slabs.append((w, k0, SLAB_K, c0, COLS, ("job", (name, 1))))
        self.gemms[name] = (first, len(self.slabs), COLS)
        for j in range(2):
            self.job(name, j)

    def gemm(self, name, w, k_tiles, c0, cols):
        first = len(self.slabs)
        for k0 in range(0, k_tiles, SLAB_K):
            kn = min(SLAB_K, k_tiles - k0)
            last = k0 + kn == k_tiles
            if not last:
                self.used += 1
            release = ("job", (name, TT - 1)) if last else ("used", self.used)
            self.slabs.append((w, k0, kn, c0, cols, release))
        self.gemms[name] = (first, len(self.slabs), cols)
        for t in range(TT):
            self.job(name, t)


def ffn_blocks():
    return column_blocks(FF)


def build_plan(W):
    p = Plan()

    def turned(tag, n=4):
        for i in range(n):
            p.job(tag, "turn", i)

    for s in STAGES:
        if s == "rw":
            turned(s)
            for x in "wa":
                p.job(s, "lora_in", x)
                for b in range(2):
                    for t in range(TT):
                        p.job(s, "lora_out", x, b, t)
            for i, x in enumerate("rkvg"):
                for b in range(2):
                    p.gemm((s, x, b), W["rw_w_in"], KD, i * D + b * COLS, COLS)
            for b in range(2):
                for w in range(2):
                    p.job(s, "cum", b, w)
                    p.job(s, "cumx", b, w)
            p.job(s, "carry")
            for w in range(2):
                for gg in range(2):
                    for g in (2 * gg, 2 * gg + 1):
                        for pp in range(2):
                            p.job(s, "ct", w, g, pp)
                        for par in range(2):
                            p.job(s, "ab", w, g, par)
                            p.job(s, "ak", w, g, par)
                            p.job(s, "a0", w, g, par)
                    for l in range(1, 7):
                        for g in (2 * gg, 2 * gg + 1):
                            p.job(s, "x", w, g, l)
                        for g in (2 * gg, 2 * gg + 1):
                            if l < 6:
                                p.job(s, "tx", w, g, l)
                            p.job(s, "xt", w, g, l)
                    for g in (2 * gg, 2 * gg + 1):
                        p.job(s, "rhs", w, g)
                    for g in (2 * gg, 2 * gg + 1):
                        p.job(s, "u", w, g)
                    for g in (2 * gg, 2 * gg + 1):
                        p.job(s, "y", w, g)
                        if w == 0:
                            p.job(s, "s", w, g)
            turned("rwo")
            for b in range(2):
                p.gemm((s, "o", b), W["rw_w_out"], KD, b * COLS, COLS)
        elif s in ("ple0", "ple1"):
            i = int(s[-1])
            for j in range(1):
                p.job(s, "turn_p", j)
            for b in range(2):
                p.gemm((s, "p", b), W["pe_w_proj%d" % i], 2, b * COLS, COLS)
            turned(s)
            for b in range(2):
                p.gemm((s, "g", b), W["pe_w_gate%d" % i], KD, b * COLS, COLS)
        elif s == "da":
            turned(s)
            for i in range(8):
                p.gemm((s, i), W["da_w_in"], KD, i * COLS, COLS)
            for i in range(8):
                p.job(s, "qk", i)
            for hd in range(8):
                for qt in range(2):
                    for c in range(2):
                        p.job(s, "s", hd, qt, c)
                if hd:
                    p.job(s, "at", hd - 1)
                    p.job(s, "o", hd - 1)
            p.job(s, "at", 7)
            p.job(s, "o", 7)
            turned("dao")
            for b in range(2):
                p.gemm((s, "out", b), W["da_w_out"], KD, b * COLS, COLS)
        elif s == "ssm":
            turned(s)
            p.gemm((s, "dt"), W["ssm_w_in"], KD, 5 * D, SSM_H)
            p.job(s, "acum")
            for i in range(4):
                p.gemm((s, "z", i), W["ssm_w_in"], KD, i * COLS, COLS)
            before = None
            for i in CONV_ORDER:
                p.gemm_by_channel((s, "xb", i), W["ssm_w_in"], 2 * D + i * COLS)
                if before is not None and before < 4:
                    for j in range(2):
                        p.job(s, "xt", before, j)
                before = i
            for j in range(2):
                p.job(s, "xt", before, j)
            for g in range(4):
                p.job(s, "cb", g)
            for u in range(SSM_H // 2 + 2):
                if u < SSM_H // 2:
                    p.job(s, "seg", u)
                if u >= 2:
                    p.job(s, "y", u - 2)
            turned("ssmo", 8)
            for b in range(2):
                p.gemm((s, "out", b), W["ssm_w_out"], 2 * KD, b * COLS, COLS)
        elif s == "kv":
            p.job(s, "bias")
            turned(s)
            p.gemm((s, "kv"), W["w_kv"], KD, 0, 256)
            p.job(s, "vt")
            p.job(s, "kt")
        elif s == "swa":
            turned(s)
            for b in range(2):
                p.gemm((s, "q", b), W["w_q"], KD, b * COLS, COLS)
            for i in range(4):
                p.job(s, "qt", i)
            for pr in range(8):
                for qt in range(2):
                    for par in range(2):
                        p.job(s, "s", pr, qt, par)
                if pr:
                    for par in range(2):
                        p.job(s, "at", pr - 1, par)
                    p.job(s, "o", pr - 1)
            for par in range(2):
                p.job(s, "at", 7, par)
            p.job(s, "o", 7)
            turned("swao")
            for b in range(2):
                p.gemm((s, "out", b), W["w_o"], KD, b * COLS, COLS)
        elif s == "final":
            pass
        elif s.startswith("ffn"):
            turned(s)
            n = len(ffn_blocks())
            for b, (c0, cols) in enumerate(ffn_blocks()):
                p.gemm((s, "u", b), W["w1_" + s[-1]], KD, c0, cols)
                if b:
                    for i in range(2):
                        p.job(s, "gt", b - 1, i)
                p.gemm((s, "v", b), W["w3_" + s[-1]], KD, c0, cols)
            p.job(s, "gt", n - 1, 0)
            for b in range(2):
                p.gemm((s, "d", b), W["w2_" + s[-1]], KF, b * COLS, COLS)
    return p


ROW_SOURCES = {
    "rw": ["rw_norm", "rw_k_k", "rw_k_a", "rw_r_k", "rw_ln_w", "rw_ln_b"],
    "ple0": ["pe_norm0"], "ple1": ["pe_norm1"], "da": ["da_norm"], "final": ["final_norm"],
    "ffn0": ["ffn_norm0"], "ffn1": ["ffn_norm1"], "ffn2": ["ffn_norm2"], "ffn3": ["ffn_norm3"],
    "ssm": ["ssm_norm", "gate_norm0", "gate_norm1"], "kv": ["kv_norm"], "swa": ["attn_norm"],
}


def program(nc, A, out):
    W = {"rw_w_in": A["rw_w_in"][0], "rw_w_out": A["rw_w_out"][0], "da_w_in": A["da_w_in"][0],
         "da_w_out": A["da_w_out"][0], "ssm_w_in": A["ssm_w_in_2"][0], "ssm_w_out": A["ssm_w_out_2"][0],
         "w_kv": A["w_kv_2"], "w_q": A["w_q_2"][0], "w_o": A["w_o_2"][0]}
    for i in range(2):
        W["pe_w_gate%d" % i] = A["pe_w_gate"][i]
        W["pe_w_proj%d" % i] = A["pe_w_proj"][i]
    for i in range(4):
        for m in (1, 2, 3):
            W["w%d_%d" % (m, i)] = A["ffn_w%d_2" % m][i // 2, i % 2]
    R = {"rw_norm": A["rw_norm"][0], "rw_k_k": A["rw_k_k"][0], "rw_k_a": A["rw_k_a"][0],
         "rw_r_k": A["rw_r_k"][0].rearrange("h n -> (h n)"), "rw_ln_w": A["rw_ln_w"][0],
         "rw_ln_b": A["rw_ln_b"][0], "pe_norm0": A["pe_norm"][0], "pe_norm1": A["pe_norm"][1],
         "da_norm": A["da_norm"][0], "final_norm": A["final_norm"], "ssm_norm": A["ssm_norm_2"][0],
         "gate_norm0": A["ssm_gate_norm_2"][0, 0:D], "gate_norm1": A["ssm_gate_norm_2"][0, D:2 * D],
         "kv_norm": A["kv_norm_2"], "attn_norm": A["attn_norm_2"][0]}
    for i in range(4):
        R["ffn_norm%d" % i] = A["ffn_norm_2"][i // 2, i % 2]

    plan = build_plan(W)
    jobs, slabs, gemms = plan.jobs, plan.slabs, plan.gemms
    rows = [(s, r) for s in STAGES for r in ROW_SOURCES[s]]
    row_at = {key: n for n, key in enumerate(rows)}

    with ExitStack() as ctx:
        def sb(name, shape, dt=F32, scope=ctx):
            return scope.enter_context(nc.sbuf_tensor(name, shape, dt))

        def sem(name):
            return ctx.enter_context(nc.semaphore(name))

        bank = [ctx.enter_context(nc.psum_tensor("bank%d" % i, [P, COLS], F32)) for i in range(BANKS)]

        h = sb("h", [P, TT, D])
        xn = sb("xn", [P, TT, D])
        raw = sb("raw", [P, RAW_SLOTS, SLAB_K, COLS])
        w_hi = sb("w_hi", [P, PART_SLOTS, SLAB_K, COLS], F32R)
        w_lo = sb("w_lo", [P, PART_SLOTS, SLAB_K, COLS], F32R)
        row = sb("row", [P, ROW_SLOTS, D])
        const = sb("const", [P, N_CONST])
        stat = sb("stat", [P, 8])
        first_half = ExitStack()
        p_tok = sb("p_tok", [P, TT, TT, 256], scope=first_half)
        first_half.close()
        kv_k = sb("kv_k", [P, 2, T])
        kv_v = sb("kv_v", [P, TT, P])
        rest_of_p_tok = sb("rest_of_p_tok", [P, 256])
        minus_half = sb("minus_half", [P, 32])

        core = ExitStack()
        ct = sb("ct", [P, 2, 2, 4, P], scope=core)
        ab = sb("ab", [P, 2, 4, 4, P], scope=core)
        inv = sb("inv", [P, 2, 2, 4, P], scope=core)
        core.close()
        x_hi = [sb("x_hi0", [P, KD, T], F32R)]
        x_lo = [sb("x_lo0", [P, KD, T], F32R)]

        rw = ExitStack()
        x_hi.append(sb("x_hi1", [P, KD, T], F32R, rw))
        x_lo.append(sb("x_lo1", [P, KD, T], F32R, rw))
        rw_r = sb("rw_r", [P, TT, D], scope=rw)
        rw_k = sb("rw_k", [P, TT, D], scope=rw)
        rw_v = sb("rw_v", [P, TT, D], scope=rw)
        rw_gate = sb("rw_gate", [P, TT, D], scope=rw)
        rw_sig = sb("rw_sig", [P, TT, D], scope=rw)
        rw_a = sb("rw_a", [P, TT, D], scope=rw)
        rw_kap = sb("rw_kap", [P, TT, D], scope=rw)
        rhs_sb = sb("rhs_sb", [P, 2, 2, P], scope=rw)
        un_sb = sb("un_sb", [P, 2, 2, P], scope=rw)
        state = sb("state", [P, 8, P], scope=rw)
        carry = sb("carry", [P, 8], scope=rw)
        bonus = sb("bonus", [P, TT, 16], scope=rw)
        hstat = sb("hstat", [P, 3, TT, 16], scope=rw)
        mu = sb("mu", [P, 6, KD], scope=rw)
        xn_ch = rw_gate[:, :, :].rearrange("p t (k c) -> p (t k) c", c=T)
        dx_ch = xn[:, :, :].rearrange("p t (k c) -> p (t k) c", c=T)
        mix_v = rw_v[:, :, :].rearrange("p t (k c) -> p (t k) c", c=T)
        mix_k = rw_k[:, :, :].rearrange("p t (k c) -> p (t k) c", c=T)
        x_mask = rw_sig[:, 0, :].rearrange("p (g i c) -> p g i c", g=2, i=4)
        lora_w1 = rw_r[:, 0, :].rearrange("p (x k c) -> p x k c", x=2, k=KD)
        lora_t = rw_r[:, 1, 0:2 * T].rearrange("p (x t) -> p x t", x=2)
        rw.close()
        decays = [[ab[:, i, :, :, :].rearrange("p a b c -> p (a b c)")[:, j * COLS:(j + 1) * COLS]
                   for j in range(3)] for i in range(2)]
        ff = ExitStack()
        g_hi = sb("g_hi", [P, KF, T], F32R, ff)
        g_lo = sb("g_lo", [P, KF, T], F32R, ff)
        g_tok = sb("g_tok", [P, 2, TT, COLS], scope=ff)
        silu = sb("silu", [P, TT, COLS], scope=ff)
        bias = sb("bias", [P, 16, T], scope=ff)
        bias_rows = sb("bias_rows", [16, BIAS_N], scope=ff)
        rel = sb("rel", [33, 16], scope=ff)
        picks = sb("picks", [33, BIAS_N], scope=ff)
        ff.close()
        bias_dram = nc.dram_tensor("bias_dram", [16, BIAS_N], F32, kind="Internal").ap()
        sw = ExitStack()
        sq_tok = sb("sq_tok", [P, TT, D], scope=sw)
        sq_ch = sb("sq_ch", [P, KD, T], scope=sw)
        s_sc = sb("s_sc", [P, 2, 2, T], scope=sw)
        s_pr = sb("s_pr", [P, 2, TT, 2, T], scope=sw)
        s_at = sb("s_at", [P, 2, 3, P], scope=sw)
        s_sm = sb("s_sm", [P, 16, 8], scope=sw)
        sinks = sb("sinks", [P, 16], scope=sw)
        q_norm = sb("q_norm", [P, 64], scope=sw)
        k_norm = sb("k_norm", [P, 64], scope=sw)
        k_tmp = sb("k_tmp", [P, TT, 2, 2, 64], scope=sw)
        v_tmp = sb("v_tmp", [P, TT, P], scope=sw)
        k_sq = sb("k_sq", [P, TT, 2, 64], scope=sw)
        sw_stat = sb("sw_stat", [P, 2, 32], scope=sw)
        sw.close()
        late = ExitStack()
        y_hi = sb("y_hi", [P, 2 * KD, T], F32R, late)
        y_lo = sb("y_lo", [P, 2 * KD, T], F32R, late)
        late.close()
        ss = ExitStack()
        z_tok = sb("z_tok", [P, TT, 2 * D], scope=ss)
        xs_tok = sb("xs_tok", [P, TT, 2 * D], scope=ss)
        y_tok = sb("y_tok", [P, TT, 2 * D], scope=ss)
        bc = sb("bc", [P, 8, T], scope=ss)
        conv_in = sb("conv_in", [P, 2, 2, T + 4], scope=ss)
        conv_sum = sb("conv_sum", [P, 2, 2, T], scope=ss)
        cb = sb("cb", [P, 4, 3 * P], scope=ss)
        seg = sb("seg", [P, 2, 2, 3 * P], scope=ss)
        conv_w = sb("conv_w", [P, 24, 4], scope=ss)
        conv_b = sb("conv_b", [P, 24], scope=ss)
        per_head_in = sb("per_head_in", [P, 3, SSM_H], scope=ss)
        dts = sb("dts", [P, 8, TT, SSM_H], scope=ss)
        ss_stat = sb("ss_stat", [P, 2, 8], scope=ss)
        ss.close()
        da = ExitStack()
        q_tok = sb("q_tok", [P, TT, D], scope=da)
        k_tok = sb("k_tok", [P, TT, D], scope=da)
        v_tok = sb("v_tok", [P, TT, D], scope=da)
        gate = sb("gate", [P, TT, D], scope=da)
        rot = sb("rot", [P, TT, D], scope=da)
        q_ch = sb("q_ch", [P, KD, T], scope=da)
        k_ch = sb("k_ch", [P, KD, T], scope=da)
        scores = sb("scores", [P, 2, 2, T], scope=da)
        expo = sb("expo", [P, 2, 2, T], scope=da)
        att = sb("att", [P, 2, TT, T], scope=da)
        att_ch = sb("att_ch", [P, 2, 3, P], scope=da)
        sm = sb("sm", [P, 8 * TT, 8], scope=da)
        lq = sb("lq", [P, 4, 64], scope=da)
        lam = sb("lam", [P, 6], scope=da)
        subln = sb("subln", [P, P], scope=da)
        da_stat = sb("da_stat", [P, 2, 16], scope=da)
        da.close()
        pl = ExitStack()
        p_hi = sb("p_hi", [P, 2, T], F32R, pl)
        p_lo = sb("p_lo", [P, 2, T], F32R, pl)
        p_out = sb("p_out", [P, TT, D], scope=pl)
        sig = sb("sig", [P, TT, D], scope=pl)
        pl.close()

        ld_const, ld_mu, ld_lora, ld_p = sem("ld_const"), sem("ld_mu"), sem("ld_lora"), sem("ld_p")
        ld_bias = sem("ld_bias")
        ld_da, ld_ssm, ld_kv, ld_swa = sem("ld_da"), sem("ld_ssm"), sem("ld_kv"), sem("ld_swa")
        lora_ready_for_load = sem("lora_ready_for_load")
        slab_loaded = [sem("slab_loaded%d" % i) for i in range(RAW_SLOTS)]
        row_loaded = [sem("row_loaded%d" % i) for i in range(ROW_SLOTS)]
        row_used = sem("row_used")
        slab_hi, slab_lo, slab_used = sem("slab_hi"), sem("slab_lo"), sem("slab_used")
        psum_ready = sem("psum_ready")
        bank_free = [sem("bank_free%d" % i) for i in range(BANKS)]
        turned_hi = sem("turned_hi")
        vec_step, act_step, pool_step = sem("vec_step"), sem("act_step"), sem("pool_step")
        stored = sem("stored")
        named = {}

        def event(*name):
            key = "_".join(map(str, name))
            if key not in named:
                named[key] = sem(key)
            return named[key]

        def ready(eng, *name):
            eng.wait_ge(psum_ready, jobs[name] + 1)

        def consumed(eng, *name):
            j = jobs[name]
            eng.wait_ge(bank_free[j % BANKS], j // BANKS + 1)

        def B(*name):
            return bank[jobs[name] % BANKS]

        def frees(ins, *name):
            ins.then_inc(bank_free[jobs[name] % BANKS], 1)

        def slab_released(eng, n):
            kind, what = slabs[n][5]
            if kind == "job":
                eng.wait_ge(psum_ready, jobs[what] + 1)
            else:
                eng.wait_ge(slab_used, what)

        def C(name, part=slice(0, P)):
            lo_, hi_ = CONST_AT[name]
            return const[part, lo_:hi_]

        ident = C("ident")
        stage_before = dict(zip(STAGES[1:], STAGES))

        def h_done(eng, s):
            if s is None:
                eng.wait_ge(ld_const, 32)
            elif s == "rw":
                consumed(eng, (s, "o", 1), TT - 1)
            elif s in ("ple0", "ple1"):
                eng.wait_ge(event(s, "added"), 2 * TT)
            elif s in ("da", "swa", "ssm"):
                consumed(eng, (s, "out", 1), TT - 1)
            elif s == "final":
                eng.wait_ge(event(s, "scaled"), TT)
            elif s.startswith("ffn"):
                consumed(eng, (s, "d", 1), TT - 1)
            elif s == "kv":
                consumed(eng, s, "turn", 3)

        turned_no = {}
        for name in jobs:
            if name[1] in ("turn", "turn_p", "gt") and name[0] != "rw":
                turned_no[name] = len(turned_no) + 1

        block = ctx.enter_context(nc.Block())

        @block.sync
        def _(sp):
            sp.dma_start(h[:, :, :], A["x"][0].rearrange("(t p) d -> p t d", p=P)).then_inc(ld_const, 16)
            sp.dma_start(const[:, :], A["constants"]).then_inc(ld_const, 16)
            nrow = [0]

            def load_rows(upto):
                while nrow[0] < upto:
                    n = nrow[0]
                    if n >= ROW_SLOTS:
                        sp.wait_ge(row_used, n - ROW_SLOTS + 1)
                    sp.dma_start(row[:, n % ROW_SLOTS, :], R[rows[n][1]].partition_broadcast(P)) \
                        .then_inc(row_loaded[n % ROW_SLOTS], 16)
                    nrow[0] += 1

            def load_slabs(lo_, hi_):
                for n in range(lo_, hi_):
                    w, k0, kn, c0, cols, _ = slabs[n]
                    if n >= RAW_SLOTS:
                        sp.wait_ge(slab_lo, n - RAW_SLOTS + 1)
                    sp.dma_start(raw[:, n % RAW_SLOTS, 0:kn, 0:cols],
                                 w[k0 * P:(k0 + kn) * P, c0:c0 + cols].rearrange("(k p) c -> p k c", p=P)) \
                        .then_inc(slab_loaded[n % RAW_SLOTS], 16)

            def load_extras(s):
                if s == "ssm":
                    h_done(sp, stage_before.get(s))
                    sp.dma_start(conv_w[:, :, :], A["ssm_conv_w_2"]).then_inc(ld_ssm, 16)
                    sp.dma_start(conv_b[:, :], A["ssm_conv_b_2"]).then_inc(ld_ssm, 16)
                    for i, n in enumerate(("ssm_dt_bias_2", "ssm_a_log_2", "ssm_d_2")):
                        sp.dma_start(per_head_in[:, i, :], A[n][0].partition_broadcast(P)).then_inc(ld_ssm, 16)
                if s == "kv":
                    h_done(sp, stage_before.get(s))
                    sp.dma_start(rel[0:32, :], A["rel_bias_2"]).then_inc(ld_kv, 16)
                    sp.dma_start(picks[:, :], A["bias_picks"]).then_inc(ld_kv, 16)
                    sp.dma_start(k_norm[:, :], A["k_norm_2"].partition_broadcast(P)).then_inc(ld_kv, 16)
                if s == "swa":
                    h_done(sp, stage_before.get(s))
                    sp.dma_start(sinks[:, :], A["sinks_2"][0].partition_broadcast(P)).then_inc(ld_swa, 16)
                    sp.dma_start(q_norm[:, :], A["q_norm_2"][0].partition_broadcast(P)).then_inc(ld_swa, 16)
                if s == "da":
                    h_done(sp, stage_before.get(s))
                    for i, n in enumerate(("da_lq1", "da_lk1", "da_lq2", "da_lk2")):
                        sp.dma_start(lq[:, i, :], A[n][0].partition_broadcast(P)).then_inc(ld_da, 16)
                    sp.dma_start(subln[:, :], A["da_subln"][0].partition_broadcast(P)).then_inc(ld_da, 16)
                if s == "rw":
                    sp.dma_start(mu[:, :, :], A["rw_mu"]).then_inc(ld_mu, 16)
                    for i, (w1, w2, w0) in enumerate((("rw_w1", "rw_w2", "rw_w0"), ("rw_a1", "rw_a2", "rw_a0"))):
                        sp.dma_start(lora_w1[:, i], A[w1][0].rearrange("(k p) c -> p k c", p=P)).then_inc(ld_lora, 16)
                        sp.dma_start(rw_kap[0:64, i, :], A[w2][0]).then_inc(ld_lora, 16)
                        sp.dma_start(rw_kap[64:65, i, :], A[w0]).then_inc(ld_lora, 16)

            sp.dma_start(p_tok[:, :, :, :], A["p"][:, 0].rearrange("i (t p) c -> p i t c", p=P)).then_inc(ld_p, 16)
            for s in STAGES:
                here = [n for n, (st, _) in enumerate(rows) if st == s]
                mine = [g for g in gemms if g[0] == s]
                load_rows(here[0] + min(len(here), ROW_SLOTS))
                load_extras(s)
                for g in mine:
                    if g == mine[max(0, len(mine) - 2)]:
                        load_rows(here[-1] + 1)
                    load_slabs(gemms[g][0], gemms[g][1])
                if not mine:
                    load_rows(here[-1] + 1)
            h_done(sp, STAGES[-1])
            sp.dma_start(out[0].rearrange("(t p) d -> p t d", p=P), h[:, :, :]).then_inc(stored, 16)
            sp.wait_ge(stored, 16)

        @block.gpsimd
        def _(pool):
            O = Order(pool, pool_step)

            def power(s, what, dst, src, n):
                pool.wait_ge(event(s, what + "_mean"), 1)
                pool.tensor_tensor(dst, src, minus_half[:, 0:n], ALU.pow).then_inc(event(s, what + "_rstd"), 1)

            O.step(pool.memset(minus_half[:, :], -0.5))
            O.settle()
            for s in STAGES:
                power(s, "norm", stat[:, 4:6], stat[:, 2:4], 2)
                if s == "rw":
                    power(s, "kap", hstat[:, 1, :, :].rearrange("p t h -> p (t h)"),
                          hstat[:, 0, :, :].rearrange("p t h -> p (t h)"), 32)
                    power(s, "group", hstat[:, 1, :, :].rearrange("p t h -> p (t h)"),
                          hstat[:, 2, :, :].rearrange("p t h -> p (t h)"), 32)
                if s == "da":
                    power(s, "head", da_stat[:, 1, :], da_stat[:, 0, :], 16)
                if s == "ssm":
                    power(s, "group", ss_stat[:, 1, :], ss_stat[:, 0, :], 8)
                if s == "kv":
                    power(s, "head", sw_stat[:, 1, 0:4], sw_stat[:, 0, 0:4], 4)
                    consumed(pool, s, "bias")
                    pool.dma_start(bias_dram, bias_rows[:, :]).then_inc(ld_bias, 16)
                    pool.wait_ge(ld_bias, 16)
                    pool.dma_start(bias[:, :, :], bass.AP(bias_dram.tensor, 0, [[1, P], [BIAS_N, 16], [1, T]])) \
                        .then_inc(ld_bias, 16)
                if s == "swa":
                    power(s, "head", sw_stat[:, 1, :], sw_stat[:, 0, :], 32)

        @block.scalar
        def _(act):
            O = Order(act, act_step)
            split = [0]

            def hi_parts(name, count=99):
                while split[0] < min(gemms[name][1], gemms[name][0] + count):
                    n = split[0]
                    _, _, kn, _, cols, _ = slabs[n]
                    act.wait_ge(slab_loaded[n % RAW_SLOTS], 16 * (n // RAW_SLOTS + 1))
                    if n >= PART_SLOTS:
                        slab_released(act, n - PART_SLOTS)
                    act.activation(w_hi[:, n % PART_SLOTS, 0:kn, 0:cols], raw[:, n % RAW_SLOTS, 0:kn, 0:cols],
                                   ACT.Copy).then_inc(slab_hi, 1)
                    split[0] += 1

            def squares(s):
                h_done(act, stage_before.get(s))
                for t in range(TT):
                    act.activation(xn[:, t, :], h[:, t, :], ACT.Square, accum_out=stat[:, t:t + 1]) \
                        .then_inc(event(s, "squares"), 1)

            def take_hi(*name):
                ready(act, *name)
                i = name[-1]
                hi = {"turn": x_hi[0], "turn_p": p_hi, "gt": g_hi}[name[1]]
                if name[0] == "ssmo":
                    hi = y_hi
                b_ = i if name[1] != "gt" else 2 * name[2] + i
                act.activation(hi[:, 2 * b_:2 * b_ + 2, :], B(*name)[:, :].rearrange("p (k t) -> p k t", k=2),
                               ACT.Copy).then_inc(turned_hi, 1)

            def activations(s, tag=None, n=4):
                for i in range(n):
                    take_hi(tag or s, "turn", i)

            def evacuate(name, dst, func=ACT.Copy):
                for t in range(TT):
                    ready(act, name, t)
                    frees(act.activation(dst(t), B(name, t)[:, 0:gemms[name][2]], func), name, t)

            def rwkv(s):
                hi_parts((s, "r", 0))
                for i in range(4):
                    ready(act, s, "turn", i)
                    frees(act.activation(xn_ch[:, 2 * i:2 * i + 2, :],
                                         B(s, "turn", i)[:, :].rearrange("p (k t) -> p k t", k=2), ACT.Copy),
                          s, "turn", i)
                for i, (x, func) in enumerate((("w", ACT.Tanh), ("a", ACT.Copy))):
                    ready(act, s, "lora_in", x)
                    frees(act.activation(lora_t[0:64, i, :], B(s, "lora_in", x)[0:64, 0:T], func), s, "lora_in", x)
                    for b in range(2):
                        for t in range(TT):
                            ready(act, s, "lora_out", x, b, t)
                            frees(act.activation((rw_sig, rw_a)[i][:, t, b * COLS:(b + 1) * COLS],
                                                 B(s, "lora_out", x, b, t)[:, :], ACT.Sigmoid),
                                  s, "lora_out", x, b, t)

                def mix_hi(i):
                    act.wait_ge(event(s, "mixed"), i + 1)
                    if i >= 2:
                        ready(act, (s, "rkvg"[i - 2], 1), TT - 1)
                    act.activation(x_hi[i % 2][:, :, :], (mix_v, mix_k, mix_v, xn_ch)[i], ACT.Copy) \
                        .then_inc(event(s, "mix_hi"), 1)

                mix_hi(0)
                for i, x in enumerate("rkvg"):
                    hi_parts((s, x, 1))
                    if i < 3:
                        mix_hi(i + 1)
                        hi_parts((s, "rkvg"[i + 1], 0))
                    for b in range(2):
                        evacuate((s, x, b), lambda t: (rw_r, rw_k, rw_v, rw_gate)[i][:, t, b * COLS:(b + 1) * COLS],
                                 ACT.Silu if x == "g" else ACT.Copy)
                for b in range(2):
                    for w in range(TT):
                        i = 2 * b + w
                        ready(act, s, "cum", b, w)
                        if i >= 2:
                            act.wait_ge(event(s, "decayed"), i - 1)
                        e = decays[i % 2]
                        act.activation(e[0], B(s, "cum", b, w)[:, :], ACT.Exp).then_inc(event(s, "exp_p"), 1)
                        frees(act.activation(e[1], B(s, "cum", b, w)[:, :], ACT.Exp, scale=-1.0), s, "cum", b, w)
                        ready(act, s, "cumx", b, w)
                        frees(act.activation(e[2], B(s, "cumx", b, w)[:, :], ACT.Exp), s, "cumx", b, w)
                ready(act, s, "carry")
                frees(act.activation(carry[:, :], B(s, "carry")[:, 0:8], ACT.Exp), s, "carry")
                for w in range(TT):
                    for gg in range(2):
                        pair = (2 * gg, 2 * gg + 1)
                        for g in pair:
                            for pp in range(2):
                                ready(act, s, "ct", w, g, pp)
                                frees(act.activation(ct[:, g % 2, pp, :, :],
                                                     B(s, "ct", w, g, pp)[:, :].rearrange("p (i c) -> p i c", i=4),
                                                     ACT.Copy), s, "ct", w, g, pp)
                        for what, dst, sign in (("rhs", rhs_sb, 1.0), ("u", un_sb, -1.0)):
                            for g in pair:
                                ready(act, s, what, w, g)
                                frees(act.activation(dst[:, g % 2, :, :],
                                                     B(s, what, w, g)[:, 0:2 * P].rearrange("p (i c) -> p i c", i=2),
                                                     ACT.Copy, scale=sign), s, what, w, g)
                        for g in pair:
                            ready(act, s, "y", w, g)
                            frees(act.activation(xn[:, w, g * 2 * P:(g + 1) * 2 * P], B(s, "y", w, g)[:, 0:2 * P],
                                                 ACT.Copy), s, "y", w, g)
                            if w == 0:
                                ready(act, s, "s", w, g)
                                act.wait_ge(event(s, "state_zeroed"), 1)
                                consumed(act, s, "carry")
                                o = B(s, "s", w, g)
                                for pp in range(2):
                                    for par in range(2):
                                        r_, c_ = slice(64 * par, 64 * par + 64), pp * P + 64 * par
                                        ins = act.activation(state[r_, 2 * g + pp, 64 * par:64 * par + 64],
                                                             o[r_, c_:c_ + 64], ACT.Copy,
                                                             scale=carry[r_, 2 * g + pp:2 * g + pp + 1])
                                frees(ins, s, "s", w, g)
                hi_parts((s, "o", 0))
                activations(s, "rwo")
                hi_parts((s, "o", 1))

            for s in STAGES:
                squares(s)
                if s == "rw":
                    rwkv(s)
                elif s in ("ple0", "ple1"):
                    hi_parts((s, "p", 0))
                    take_hi(s, "turn_p", 0)
                    hi_parts((s, "p", 1))
                    for b in range(2):
                        evacuate((s, "p", b), lambda t: p_out[:, t, b * COLS:(b + 1) * COLS])
                    activations(s)
                    for b in range(2):
                        hi_parts((s, "g", b))
                        if b:
                            evacuate((s, "g", 0), lambda t: sig[:, t, 0:COLS], ACT.Sigmoid)
                    evacuate((s, "g", 1), lambda t: sig[:, t, COLS:D], ACT.Sigmoid)
                elif s == "da":
                    activations(s)
                    dst = [q_tok, q_tok, k_tok, k_tok, v_tok, v_tok, gate, gate]
                    hi_parts((s, 0))
                    for i in range(8):
                        if i < 7:
                            hi_parts((s, i + 1))
                        evacuate((s, i), lambda t: dst[i][:, t, (i % 2) * COLS:(i % 2 + 1) * COLS],
                                 ACT.Silu if i >= 6 else ACT.Copy)
                    act.wait_ge(event(s, "lq_dots"), 1)
                    act.activation(lam[:, 2:4], lam[:, 0:2], ACT.Exp).then_inc(event(s, "lq_exp"), 1)
                    for i in range(8):
                        ready(act, s, "qk", i)
                        dst_ch = (q_ch if i < 4 else k_ch)[:, 2 * (i % 4):2 * (i % 4) + 2, :]
                        frees(act.activation(dst_ch, B(s, "qk", i)[:, :].rearrange("p (k t) -> p k t", k=2),
                                             ACT.Copy), s, "qk", i)

                    def weigh_values(hd):
                        ready(act, s, "at", hd)
                        frees(act.activation(att_ch[:, hd % 2, :, :],
                                             B(s, "at", hd)[:, 0:3 * P].rearrange("p (i q) -> p i q", i=3),
                                             ACT.Copy), s, "at", hd)
                        ready(act, s, "o", hd)
                        frees(act.activation(xn[:, :, hd * P:(hd + 1) * P],
                                             B(s, "o", hd)[:, 0:T].rearrange("p (t c) -> p t c", t=TT),
                                             ACT.Copy), s, "o", hd)

                    for hd in range(8):
                        for qt in range(TT):
                            u, n = hd * TT + qt, (qt + 1) * P
                            act.wait_ge(event(s, "max"), u + 1)
                            if u >= 2:
                                act.wait_ge(event(s, "att"), u - 1)
                            for c in range(2):
                                act.activation(expo[:, u % 2, c, 0:n], scores[:, u % 2, c, 0:n], ACT.Exp,
                                               bias=sm[:, u, 2 + c:3 + c], scale=64 ** -0.5,
                                               accum_out=sm[:, u, 4 + c:5 + c]).then_inc(event(s, "exp"), 1)
                        if hd:
                            weigh_values(hd - 1)
                    weigh_values(7)
                    for b in range(2):
                        hi_parts((s, "out", b))
                        if b == 0:
                            activations(s, "dao")
                elif s == "ssm":
                    hi_parts((s, "dt"))
                    activations(s)
                    act.wait_ge(ld_ssm, 16 * 5)
                    act.activation(per_head_in[:, 1, :], per_head_in[:, 1, :], ACT.Exp) \
                        .then_inc(event(s, "a"), 1)
                    act.wait_ge(event(s, "dt_minus_abs"), 1)
                    O.step(act.activation(dts[:, 2], dts[:, 1], ACT.Exp))
                    O.settle()
                    act.activation(dts[:, 3], dts[:, 2], ACT.Ln, bias=1.0).then_inc(event(s, "dt_log"), 1)
                    hi_parts((s, "z", 0))
                    for i in range(4):
                        hi_parts((s, "z", i + 1) if i < 3 else (s, "xb", CONV_ORDER[0]))
                        evacuate((s, "z", i), lambda t: z_tok[:, t, i * COLS:(i + 1) * COLS], ACT.Silu)

                    def conv_out(i, j):
                        m = 2 * i + j
                        n = CONV_ORDER.index(i) * 2 + j
                        act.wait_ge(event(s, "convolved"), n + 1)
                        for c in range(2):
                            tile_ = 4 * i + 2 * j + c
                            dst = bc[:, tile_ - 16, :] if i >= 4 else conv_sum[:, n % 2, c, :]
                            act.activation(dst, conv_sum[:, n % 2, c, :], ACT.Silu,
                                           bias=conv_b[:, tile_:tile_ + 1]).then_inc(event(s, "conv_out"), 1)

                    def take_tokens(i):
                        for j in range(2):
                            ready(act, s, "xt", i, j)
                            c = i * COLS + j * 256
                            frees(act.activation(xs_tok[:, :, c:c + 256],
                                                 B(s, "xt", i, j)[:, :].rearrange("p (t c) -> p t c", t=TT),
                                                 ACT.Copy), s, "xt", i, j)

                    for n, i in enumerate(CONV_ORDER):
                        if n < 5:
                            hi_parts((s, "xb", CONV_ORDER[n + 1]), 1)
                        for j in range(2):
                            ready(act, (s, "xb", i), j)
                            if 2 * n + j >= 2:
                                act.wait_ge(event(s, "convolved"), 2 * n + j - 1)
                            frees(act.activation(conv_in[:, j, :, 3:3 + T],
                                                 B((s, "xb", i), j)[:, :].rearrange("p (c t) -> p c t", c=2),
                                                 ACT.Copy), (s, "xb", i), j)
                            conv_out(i, j)
                        if n < 5:
                            hi_parts((s, "xb", CONV_ORDER[n + 1]))
                        if i < 4:
                            if i:
                                take_tokens(i - 1)
                    take_tokens(3)
                    for u in range(SSM_H // 2 + 2):
                        if u < SSM_H // 2:
                            act.wait_ge(event(s, "seg"), u + 1)
                            act.activation(seg[:, u % 2, :, :], seg[:, u % 2, :, :], ACT.Exp) \
                                .then_inc(event(s, "seg_exp"), 1)
                        if u >= 2:
                            ready(act, s, "y", u - 2)
                            frees(act.activation(y_tok[:, :, (u - 2) * P:(u - 1) * P],
                                                 B(s, "y", u - 2)[:, 0:T].rearrange("p (t c) -> p t c", t=TT),
                                                 ACT.Copy), s, "y", u - 2)
                    hi_parts((s, "out", 0), 2)
                    activations(s, "ssmo", 8)
                    for b in range(2):
                        hi_parts((s, "out", b))
                elif s == "kv":
                    hi_parts((s, "kv"))
                    activations(s)
                    ready(act, (s, "kv"), TT - 1)
                    ready(act, s, "vt")
                    frees(act.activation(kv_v[:, :, :], B(s, "vt")[:, 0:2 * P].rearrange("p (t c) -> p t c", t=TT),
                                         ACT.Copy), s, "vt")
                    ready(act, s, "kt")
                    frees(act.activation(kv_k[:, :, :], B(s, "kt")[:, :].rearrange("p (h t) -> p h t", h=2),
                                         ACT.Copy), s, "kt")
                elif s == "swa":
                    hi_parts((s, "q", 0))
                    activations(s)
                    for b in range(2):
                        if b == 0:
                            hi_parts((s, "q", 1))
                        evacuate((s, "q", b), lambda t: sq_tok[:, t, b * COLS:(b + 1) * COLS])
                    for i in range(4):
                        ready(act, s, "qt", i)
                        frees(act.activation(sq_ch[:, 2 * i:2 * i + 2, :],
                                             B(s, "qt", i)[:, :].rearrange("p (k t) -> p k t", k=2), ACT.Copy),
                              s, "qt", i)

                    def window_values(pr):
                        for par in range(2):
                            ready(act, s, "at", pr, par)
                            frees(act.activation(s_at[:, par, :, :],
                                                 B(s, "at", pr, par)[:, 0:3 * P].rearrange("p (i q) -> p i q", i=3),
                                                 ACT.Copy), s, "at", pr, par)
                        ready(act, s, "o", pr)
                        frees(act.activation(xn[:, :, pr * P:(pr + 1) * P],
                                             B(s, "o", pr)[:, 0:T].rearrange("p (t c) -> p t c", t=TT),
                                             ACT.Copy), s, "o", pr)

                    for pr in range(8):
                        for qt in range(TT):
                            u, n = pr * TT + qt, (qt + 1) * P
                            act.wait_ge(event(s, "max"), u + 1)
                            if pr >= 2:
                                ready(act, s, "at", pr - 2, 1)
                            for c in range(2):
                                act.activation(s_pr[:, pr % 2, qt, c, 0:n], s_sc[:, u % 2, c, 0:n], ACT.Exp,
                                               bias=s_sm[:, u, 2 + c:3 + c],
                                               accum_out=s_sm[:, u, 4 + c:5 + c]).then_inc(event(s, "exp"), 1)
                            act.activation(s_sm[:, u, 0:2], s_sm[:, u, 0:2], ACT.Exp).then_inc(event(s, "exp"), 1)
                        if pr:
                            window_values(pr - 1)
                    window_values(7)
                    hi_parts((s, "out", 0))
                    activations(s, "swao")
                    hi_parts((s, "out", 1))
                elif s.startswith("ffn"):
                    activations(s)
                    blocks = ffn_blocks()

                    def gated_hi(b):
                        for i in range(blocks[b][1] // 256):
                            take_hi(s, "gt", b, i)

                    for b, (_, cols) in enumerate(blocks):
                        hi_parts((s, "u", b))
                        hi_parts((s, "v", b))
                        if b:
                            gated_hi(b - 1)
                            act.wait_ge(bank_free[jobs[(s, "v", b - 1), 1] % BANKS],
                                        jobs[(s, "v", b - 1), 1] // BANKS + 1)
                        evacuate((s, "u", b), lambda t: silu[:, t, 0:cols], ACT.Silu)
                    hi_parts((s, "d", 0), 2)
                    gated_hi(len(blocks) - 1)
                    for b in range(2):
                        hi_parts((s, "d", b))

        @block.vector
        def _(dve):
            O = Order(dve, vec_step)
            split = [0]

            def lo_parts(name, count=99):
                while split[0] < min(gemms[name][1], gemms[name][0] + count):
                    n = split[0]
                    _, _, kn, _, cols, _ = slabs[n]
                    dve.wait_ge(slab_hi, n + 1)
                    hi = w_hi[:, n % PART_SLOTS, 0:kn, 0:cols]
                    dve.tensor_tensor(w_lo[:, n % PART_SLOTS, 0:kn, 0:cols], raw[:, n % RAW_SLOTS, 0:kn, 0:cols],
                                      hi.bitcast(F32), ALU.subtract).then_inc(slab_lo, 1)
                    split[0] += 1

            def use_row(s, r):
                n = row_at[(s, r)]
                dve.wait_ge(row_loaded[n % ROW_SLOTS], 16 * (n // ROW_SLOTS + 1))
                return row[:, n % ROW_SLOTS, :]

            def release_row():
                O.settle()
                dve.sem_inc(row_used, 1)

            def signal(ins, sem_, value):
                ins.then_inc(sem_, 1)
                O.last = (sem_, value)

            def frees_bank(ins, *name):
                frees(ins, *name)
                O.last = (bank_free[jobs[name] % BANKS], jobs[name] // BANKS + 1)

            def norm(s, dst=None):
                dve.wait_ge(event(s, "squares"), TT)
                signal(dve.tensor_scalar(stat[:, 2:4], stat[:, 0:2], 1.0 / D, 1e-6, ALU.mult, ALU.add),
                       event(s, "norm_mean"), 1)
                gain = use_row(s, ROW_SOURCES[s][0])
                dve.wait_ge(event(s, "norm_rstd"), 1)
                for t in range(TT):
                    signal(dve.scalar_tensor_tensor(out=(dst or xn)[:, t, :], in0=h[:, t, :],
                                                    scalar=stat[:, 4 + t:5 + t], in1=gain, op0=ALU.mult,
                                                    op1=ALU.mult), event(s, "scaled"), t + 1)
                release_row()

            def take_lo(*name):
                dve.wait_ge(turned_hi, turned_no[name])
                i = name[-1]
                hi, lo_ = {"turn": (x_hi[0], x_lo[0]), "turn_p": (p_hi, p_lo), "gt": (g_hi, g_lo)}[name[1]]
                if name[0] == "ssmo":
                    hi, lo_ = y_hi, y_lo
                b_ = i if name[1] != "gt" else 2 * name[2] + i
                frees_bank(dve.tensor_tensor(lo_[:, 2 * b_:2 * b_ + 2, :],
                                             B(*name)[:, :].rearrange("p (k t) -> p k t", k=2),
                                             hi[:, 2 * b_:2 * b_ + 2, :].bitcast(F32), ALU.subtract), *name)

            def activations(s, tag=None, n=4):
                for i in range(n):
                    take_lo(tag or s, "turn", i)

            def add_to_h(name, c0, scale=1.0):
                cols = gemms[name][2]
                for t in range(TT):
                    ready(dve, name, t)
                    dst = h[:, t, c0:c0 + cols]
                    frees_bank(dve.scalar_tensor_tensor(out=dst, in0=B(name, t)[:, 0:cols], scalar=scale, in1=dst,
                                                        op0=ALU.mult, op1=ALU.add), name, t)

            def over(x, n):
                return x.unsqueeze(1).broadcast_to([P, n, x.shape[1]])

            def rwkv(s):
                norm(s)
                O.step(dve.memset(lora_t[64:65, :, :], 1.0))
                signal(dve.memset(state[:, :, :], 0.0), event(s, "state_zeroed"), 1)
                for i in range(4):
                    consumed(dve, s, "turn", i)
                dve.wait_ge(ld_mu, 16)
                O.step(dve.tensor_scalar(dx_ch[:, :, 0:1], xn_ch[:, :, 0:1], -1.0, None, ALU.mult))
                O.step(dve.tensor_tensor(dx_ch[:, :, 1:T], xn_ch[:, :, 0:T - 1], xn_ch[:, :, 1:T], ALU.subtract))
                O.settle()

                def mix(dst, m, sem_, value):
                    for k in range(KD):
                        ins = dve.scalar_tensor_tensor(out=dst[:, k, :], in0=dx_ch[:, k, :], scalar=mu[:, m, k:k + 1],
                                                       in1=xn_ch[:, k, :], op0=ALU.mult, op1=ALU.add)
                        if k < KD - 1:
                            O.step(ins)
                    signal(ins, sem_, value)

                def mix_projection(i):
                    mix((mix_v, mix_k, mix_v, xn_ch)[i], i, event(s, "mixed"), i + 1)

                def mix_lo(i):
                    dve.wait_ge(event(s, "mix_hi"), i + 1)
                    signal(dve.tensor_tensor(x_lo[i % 2][:, :, :], (mix_v, mix_k, mix_v, xn_ch)[i],
                                             x_hi[i % 2][:, :, :].bitcast(F32), ALU.subtract),
                           event(s, "mix_lo"), i + 1)

                mix(mix_v, 4, event(s, "lora_mixed"), 1)
                mix(mix_k, 5, event(s, "lora_mixed"), 2)
                lo_parts((s, "r", 0))
                ready(dve, s, "lora_in", "w")
                mix_projection(0)
                mix_lo(0)
                ready(dve, s, "lora_in", "a")
                for i, x in enumerate("rkvg"):
                    lo_parts((s, x, 1))
                    if i < 3:
                        mix_projection(i + 1)
                        mix_lo(i + 1)
                        lo_parts((s, "rkvg"[i + 1], 0))

                heads32 = [P, 2 * 16, 64]

                def by_head(x):
                    return x[:, :, :].rearrange("p t (h c) -> p (t h) c", c=64)

                def per_head(x):
                    return x.rearrange("p t h -> p (t h)").unsqueeze(2).broadcast_to(heads32)

                def row_op(dst, a_, r_, op):
                    for t in range(TT):
                        O.step(dve.tensor_tensor(dst[:, t, :], a_[:, t, :], r_, op))

                for b in range(2):
                    consumed(dve, (s, "k", b), TT - 1)
                ready(dve, s, "lora_out", "a", 1, 1)
                row_op(rw_kap, rw_k, use_row(s, "rw_k_k"), ALU.mult)
                release_row()
                O.step(dve.tensor_tensor(xn[:, :, :], rw_kap[:, :, :], rw_kap[:, :, :], ALU.mult))
                O.settle()
                O.step(dve.tensor_reduce(hstat[:, 0, :, :].rearrange("p t h -> p (t h)"), by_head(xn), X, ALU.add))
                O.settle()
                signal(dve.tensor_scalar(hstat[:, 0, :, :], hstat[:, 0, :, :], 1e-24, None, ALU.max),
                       event(s, "kap_mean"), 1)
                consumed(dve, s, "lora_out", "a", 1, 1)
                ka = use_row(s, "rw_k_a")
                for t in range(TT):
                    O.step(dve.scalar_tensor_tensor(out=xn[:, t, :], in0=rw_a[:, t, :], scalar=-1.0, in1=ka,
                                                    op0=ALU.add, op1=ALU.mult))
                release_row()
                for t in range(TT):
                    O.step(dve.scalar_tensor_tensor(out=rw_k[:, t, :], in0=xn[:, t, :], scalar=1.0, in1=rw_k[:, t, :],
                                                    op0=ALU.add, op1=ALU.mult))
                O.settle()
                dve.wait_ge(event(s, "kap_rstd"), 1)
                O.step(dve.tensor_tensor(by_head(rw_kap), by_head(rw_kap), per_head(hstat[:, 1, :, :]), ALU.mult))
                O.step(dve.tensor_tensor(xn[:, :, :], rw_r[:, :, :], rw_k[:, :, :], ALU.mult))
                O.settle()
                row_op(xn, xn, use_row(s, "rw_r_k"), ALU.mult)
                release_row()
                O.step(dve.tensor_reduce(bonus[:, :, :].rearrange("p t h -> p (t h)"), by_head(xn), X, ALU.add))
                O.step(dve.tensor_tensor(rw_a[:, :, :], rw_kap[:, :, :], rw_a[:, :, :], ALU.mult))
                O.settle()
                for b in range(2):
                    for w in range(TT):
                        consumed(dve, s, "cumx", b, w)
                        e, c = decays[(2 * b + w) % 2], slice(b * COLS, (b + 1) * COLS)
                        for x, i in ((rw_r, 0), (rw_k, 1), (rw_a, 1)):
                            O.step(dve.tensor_tensor(x[:, w, c], x[:, w, c], e[i], ALU.mult))
                        signal(dve.tensor_tensor(rw_kap[:, w, c], rw_kap[:, w, c], e[2], ALU.mult),
                               event(s, "decayed"), 2 * b + w + 1)

                O.settle()
                for w in range(TT):
                    for gg in range(2):
                        pair = (2 * gg, 2 * gg + 1)
                        for g in pair:
                            a_, x_, t_ = ab[:, g % 2], x_mask[:, g % 2], inv[:, g % 2]
                            for par in range(2):
                                it = slice(2 * par, 2 * par + 2)
                                for what, j in (("ab", 0), ("ak", 2)):
                                    ready(dve, s, what, w, g, par)
                                    frees_bank(dve.tensor_tensor(
                                        a_[:, it, j:j + 2, :].rearrange("p i j c -> p i (j c)"),
                                        B(s, what, w, g, par)[:, :].rearrange("p (i c) -> p i c", i=2),
                                        over(C("strict_incl"), 2), ALU.mult), s, what, w, g, par)
                                ready(dve, s, "a0", w, g, par)
                                frees_bank(dve.tensor_tensor(
                                    x_[:, it, :], B(s, "a0", w, g, par)[:, 0:2 * P].rearrange("p (i c) -> p i c", i=2),
                                    over(C("levels")[:, 0:P], 2), ALU.mult), s, "a0", w, g, par)
                            O.settle()
                            O.step(dve.tensor_tensor(t_[:, 1], a_[:, :, 0, :], over(C("level0_t"), 4), ALU.mult))
                            O.step(dve.tensor_tensor(t_[:, 0], over(ident, 4), x_, ALU.subtract))
                            O.settle()
                            signal(dve.tensor_tensor(t_[:, 1], over(ident, 4), t_[:, 1], ALU.subtract),
                                   event(s, "inverse_begun"), 4 * w + g + 1)
                        for l in range(1, 7):
                            for g in pair:
                                ready(dve, s, "x", w, g, l)
                                frees_bank(dve.tensor_tensor(
                                    x_mask[:, g % 2], B(s, "x", w, g, l)[:, :].rearrange("p (i c) -> p i c", i=4),
                                    over(C("levels")[:, l * P:(l + 1) * P], 4), ALU.mult), s, "x", w, g, l)
                            for g in pair:
                                for j, what in enumerate(("tx", "xt")):
                                    if l == 6 and what == "tx":
                                        continue
                                    ready(dve, s, what, w, g, l)
                                    t_ = inv[:, g % 2, j]
                                    frees_bank(dve.tensor_tensor(
                                        t_, t_, B(s, what, w, g, l)[:, :].rearrange("p (i c) -> p i c", i=4),
                                        ALU.subtract), s, what, w, g, l)

                for w in range(TT):
                    for g in range(4):
                        consumed(dve, s, "y", w, g)
                lo_parts((s, "o", 0))
                mean, rstd, var = (hstat[:, i, :, :] for i in range(3))
                O.step(dve.tensor_reduce(mean.rearrange("p t h -> p (t h)"), by_head(xn), X, ALU.add))
                O.settle()
                O.step(dve.tensor_scalar(mean, mean, 1.0 / 64, None, ALU.mult))
                O.settle()
                O.step(dve.tensor_tensor(by_head(xn), by_head(xn), per_head(mean), ALU.subtract))
                O.settle()
                O.step(dve.tensor_tensor(rw_r[:, :, :], xn[:, :, :], xn[:, :, :], ALU.mult))
                O.settle()
                O.step(dve.tensor_reduce(var.rearrange("p t h -> p (t h)"), by_head(rw_r), X, ALU.add))
                O.settle()
                signal(dve.tensor_scalar(var, var, 1.0 / 64, 64e-5, ALU.mult, ALU.add), event(s, "group_mean"), 1)
                O.step(dve.tensor_tensor(by_head(rw_r), by_head(rw_v), per_head(bonus[:, :, :]), ALU.mult))
                dve.wait_ge(event(s, "group_rstd"), 1)
                O.settle()
                O.step(dve.tensor_tensor(by_head(xn), by_head(xn), per_head(rstd), ALU.mult))
                O.settle()
                row_op(xn, xn, use_row(s, "rw_ln_w"), ALU.mult)
                release_row()
                row_op(xn, xn, use_row(s, "rw_ln_b"), ALU.add)
                release_row()
                O.step(dve.tensor_tensor(xn[:, :, :], xn[:, :, :], rw_r[:, :, :], ALU.add))
                O.settle()
                signal(dve.tensor_tensor(xn[:, :, :], xn[:, :, :], rw_gate[:, :, :], ALU.mult), event(s, "gated"), 1)
                activations(s, "rwo")
                lo_parts((s, "o", 1))
                for b in range(2):
                    add_to_h((s, "o", b), b * COLS)

            for s in STAGES:
                if s == "rw":
                    rwkv(s)
                elif s in ("ple0", "ple1"):
                    lo_parts((s, "p", 0))
                    take_lo(s, "turn_p", 0)
                    norm(s)
                    lo_parts((s, "p", 1))
                    activations(s)
                    lo_parts((s, "g", 0))
                    for b in range(2):
                        lo_parts((s, "g", b))
                        for t in range(TT):
                            c = slice(b * COLS, (b + 1) * COLS)
                            consumed(dve, (s, "g", b), t)
                            O.step(dve.tensor_tensor(sig[:, t, c], sig[:, t, c], p_out[:, t, c], ALU.mult))
                            O.settle()
                            signal(dve.tensor_tensor(h[:, t, c], h[:, t, c], sig[:, t, c], ALU.add),
                                   event(s, "added"), b * TT + t + 1)
                elif s == "final":
                    norm(s, h)
                elif s == "da":
                    norm(s)
                    activations(s)
                    for i in range(8):
                        lo_parts((s, i))
                    dve.wait_ge(ld_da, 16 * 5)
                    O.step(dve.tensor_tensor(lq[:, 0:4:2, :], lq[:, 0:4:2, :], lq[:, 1:4:2, :], ALU.mult))
                    O.settle()
                    signal(dve.tensor_reduce(lam[:, 0:2], lq[:, 0:4:2, :], X, ALU.add), event(s, "lq_dots"), 1)
                    O.step(dve.tensor_scalar(subln[:, :], subln[:, :], 1.0 - LAMBDA_INIT, None, ALU.mult))
                    dve.wait_ge(event(s, "lq_exp"), 1)
                    O.step(dve.tensor_tensor(lam[:, 4:5], lam[:, 2:3], lam[:, 3:4], ALU.subtract))
                    O.settle()
                    O.step(dve.tensor_scalar(lam[:, 5:6], lam[:, 4:5], -1.0, -LAMBDA_INIT, ALU.mult, ALU.add))

                    for i, x in enumerate((q_tok, k_tok)):
                        for b in range(2):
                            consumed(dve, (s, 2 * i + b), TT - 1)
                        for t in range(TT):
                            xv = x[:, t, :].rearrange("p (g c) -> p g c", c=64)
                            rv = rot[:, t, :].rearrange("p (g c) -> p g c", c=64)
                            cos = C("cos")[:, t * 64:(t + 1) * 64].unsqueeze(1).broadcast_to([P, 16, 64])
                            sin = C("sin")[:, t * 64:(t + 1) * 64].unsqueeze(1).broadcast_to([P, 16, 64])
                            O.step(dve.tensor_tensor(rv[:, :, 0:32], xv[:, :, 32:64], sin[:, :, 0:32], ALU.mult))
                            O.step(dve.tensor_tensor(rv[:, :, 32:64], xv[:, :, 0:32], sin[:, :, 32:64], ALU.mult))
                            O.settle()
                            O.step(dve.tensor_tensor(xv, xv, cos, ALU.mult))
                            O.settle()
                            signal(dve.tensor_tensor(x[:, t, :], x[:, t, :], rot[:, t, :], ALU.add),
                                   event(s, "roped"), 2 * i + t + 1)

                    for u in range(8 * TT):
                        hd, qt = u // TT, u % TT
                        n = (qt + 1) * P
                        if u >= 2:
                            dve.wait_ge(event(s, "exp"), 2 * (u - 1))
                        for c in range(2):
                            ready(dve, s, "s", hd, qt, c)
                            frees_bank(dve.tensor_tensor(scores[:, u % 2, c, 0:n], B(s, "s", hd, qt, c)[:, 0:n],
                                                         C("causal")[:, T - n:T], ALU.add), s, "s", hd, qt, c)
                        O.settle()
                        O.step(dve.tensor_reduce(sm[:, u, 0:2], scores[:, u % 2, :, 0:n], X, ALU.max))
                        O.settle()
                        signal(dve.tensor_scalar(sm[:, u, 2:4], sm[:, u, 0:2], -(64 ** -0.5), None, ALU.mult),
                               event(s, "max"), u + 1)
                        dve.wait_ge(event(s, "exp"), 2 * (u + 1))
                        O.step(dve.reciprocal(sm[:, u, 6:8], sm[:, u, 4:6]))
                        O.settle()
                        O.step(dve.tensor_scalar(sm[:, u, 7:8], sm[:, u, 7:8], lam[:, 5:6], None, ALU.mult))
                        O.settle()
                        O.step(dve.tensor_scalar(expo[:, u % 2, 1, 0:n], expo[:, u % 2, 1, 0:n], sm[:, u, 7:8],
                                                 None, ALU.mult))
                        O.settle()
                        if hd >= 2 and qt == 0:
                            ready(dve, s, "at", hd - 2)
                        signal(dve.scalar_tensor_tensor(out=att[:, hd % 2, qt, 0:n], in0=expo[:, u % 2, 0, 0:n],
                                                        scalar=sm[:, u, 6:7], in1=expo[:, u % 2, 1, 0:n],
                                                        op0=ALU.mult, op1=ALU.add), event(s, "att"), u + 1)

                    consumed(dve, s, "o", 7)
                    O.step(dve.tensor_tensor(rot[:, :, :], xn[:, :, :], xn[:, :, :], ALU.mult))
                    O.settle()
                    heads = rot[:, :, :].rearrange("p t (h c) -> p (t h) c", c=P)
                    O.step(dve.tensor_reduce(da_stat[:, 0, :], heads, X, ALU.add))
                    O.settle()
                    signal(dve.tensor_scalar(da_stat[:, 0, :], da_stat[:, 0, :], 1.0 / P, 1e-5, ALU.mult, ALU.add),
                           event(s, "head_mean"), 1)
                    consumed(dve, (s, 7), TT - 1)
                    gv = gate[:, :, :].rearrange("p t (h c) -> p (t h) c", c=P)
                    xv = xn[:, :, :].rearrange("p t (h c) -> p (t h) c", c=P)
                    O.step(dve.tensor_tensor(gv, gv, subln[:, :].unsqueeze(1).broadcast_to([P, 16, P]), ALU.mult))
                    O.settle()
                    O.step(dve.tensor_tensor(xn[:, :, :], xn[:, :, :], gate[:, :, :], ALU.mult))
                    dve.wait_ge(event(s, "head_rstd"), 1)
                    O.settle()
                    signal(dve.tensor_tensor(xv, xv, da_stat[:, 1, :].unsqueeze(2).broadcast_to([P, 16, P]),
                                             ALU.mult), event(s, "heads"), 1)
                    lo_parts((s, "out", 0))
                    activations(s, "dao")
                    lo_parts((s, "out", 1))
                    for b in range(2):
                        add_to_h((s, "out", b), b * COLS)
                elif s == "ssm":
                    norm(s)
                    lo_parts((s, "dt"))
                    activations(s)
                    signal(dve.memset(conv_in[:, :, :, 0:3], 0.0), event(s, "padded"), 1)
                    raw_, nabs, ex, lg, one_, dt, dta, nacum = (dts[:, i] for i in range(8))
                    dve.wait_ge(ld_ssm, 16 * 5)
                    for t in range(TT):
                        ready(dve, (s, "dt"), t)
                        frees_bank(dve.tensor_tensor(raw_[:, t, :], B((s, "dt"), t)[:, 0:SSM_H],
                                                     per_head_in[:, 0, :], ALU.add), (s, "dt"), t)
                    O.settle()
                    O.step(dve.tensor_scalar(lg, raw_, -1.0, None, ALU.mult))
                    O.settle()
                    signal(dve.tensor_tensor(nabs, raw_, lg, ALU.min), event(s, "dt_minus_abs"), 1)
                    dve.wait_ge(event(s, "dt_log"), 1)
                    O.step(dve.tensor_scalar(one_, ex, 1.0, None, ALU.add))
                    O.settle()
                    O.step(dve.scalar_tensor_tensor(out=ex, in0=one_, scalar=-1.0, in1=ex, op0=ALU.add,
                                                    op1=ALU.subtract))
                    O.step(dve.reciprocal(one_, one_))
                    O.settle()
                    O.step(dve.tensor_tensor(ex, ex, one_, ALU.mult))
                    O.settle()
                    O.step(dve.tensor_tensor(lg, lg, ex, ALU.subtract))
                    O.settle()
                    O.step(dve.scalar_tensor_tensor(out=dt, in0=raw_, scalar=0.0, in1=lg, op0=ALU.max,
                                                    op1=ALU.add))
                    O.settle()
                    dve.wait_ge(event(s, "a"), 1)
                    for t in range(TT):
                        signal(dve.scalar_tensor_tensor(out=dta[:, t, :], in0=dt[:, t, :], scalar=-1.0,
                                                        in1=per_head_in[:, 1, :], op0=ALU.mult, op1=ALU.mult),
                               event(s, "dta"), t + 1)
                    lo_parts((s, "z", 0))
                    ready(dve, s, "acum")
                    frees_bank(dve.tensor_scalar(nacum, B(s, "acum")[:, 0:TT * SSM_H].rearrange(
                        "p (t h) -> p t h", t=TT), -1.0, None, ALU.mult), s, "acum")
                    for i in range(1, 4):
                        lo_parts((s, "z", i))
                    lo_parts((s, "xb", CONV_ORDER[0]))
                    for n, i in enumerate(CONV_ORDER):
                        if n < 5:
                            lo_parts((s, "xb", CONV_ORDER[n + 1]), 1)
                        for j in range(2):
                            consumed(dve, (s, "xb", i), j)
                            m = 2 * n + j
                            if m >= 2:
                                dve.wait_ge(event(s, "conv_out"), 2 * (m - 1))
                                prev = CONV_ORDER[n - 1]
                                if prev < 4:
                                    ready(dve, s, "xt", prev, j)
                            for k in range(4):
                                if k:
                                    O.settle()
                                for c in range(2):
                                    tile_ = 4 * i + 2 * j + c
                                    src, dst = conv_in[:, j, c, k:k + T], conv_sum[:, j, c, :]
                                    w_ = conv_w[:, tile_, k:k + 1]
                                    if k == 0:
                                        ins = dve.tensor_scalar(dst, src, w_, None, ALU.mult)
                                    else:
                                        ins = dve.scalar_tensor_tensor(out=dst, in0=src, scalar=w_, in1=dst,
                                                                       op0=ALU.mult, op1=ALU.add)
                                    if k < 3 or c == 0:
                                        O.step(ins)
                            signal(ins, event(s, "convolved"), m + 1)
                        if n < 5:
                            lo_parts((s, "xb", CONV_ORDER[n + 1]))
                    for g in range(4):
                        ready(dve, s, "cb", g)
                        O.step(dve.tensor_tensor(cb[:, g, 0:T], B(s, "cb", g)[:, 0:T], C("tri"), ALU.mult))
                        frees_bank(dve.tensor_tensor(cb[:, g, T:T + P], B(s, "cb", g)[:, T:T + P],
                                                     C("tri")[:, 0:P], ALU.mult), s, "cb", g)
                    for j in range(2):
                        consumed(dve, s, "xt", 3, j)

                    def ssm_heads(x):
                        return x[:, :, :].rearrange("p t (h c) -> p (t h) c", c=64)

                    def ssm_per_head(x):
                        return x.rearrange("p t h -> p (t h)").unsqueeze(2).broadcast_to([P, TT * SSM_H, 64])

                    signal(dve.tensor_tensor(ssm_heads(y_tok), ssm_heads(xs_tok), ssm_per_head(dt), ALU.mult),
                           event(s, "x_dt"), 1)
                    for u in range(SSM_H // 2 + 1):
                        if u < SSM_H // 2:
                            ready(dve, s, "seg", u)
                            if u >= 2:
                                ready(dve, s, "y", u - 2)
                            o = B(s, "seg", u)
                            for c in range(2):
                                hd = 2 * u + c
                                for lo2, n2, t in ((0, T, 0), (T, P, 1)):
                                    ins = dve.tensor_scalar(seg[:, u % 2, c, lo2:lo2 + n2],
                                                            o[:, c * T + t * P:c * T + t * P + n2],
                                                            nacum[:, t, hd:hd + 1], 0.0, ALU.add, ALU.min)
                                    if (c, t) != (1, 1):
                                        O.step(ins)
                            frees_bank(ins, s, "seg", u)
                            O.settle()
                            dve.sem_inc(event(s, "seg"), 1)
                        if u:
                            v = u - 1
                            dve.wait_ge(event(s, "seg_exp"), v + 1)
                            signal(dve.tensor_tensor(seg[:, v % 2, :, :], seg[:, v % 2, :, :],
                                                     over(cb[:, v // 4, :], 2), ALU.mult),
                                   event(s, "weights"), v + 1)
                    lo_parts((s, "out", 0), 2)
                    O.step(dve.tensor_tensor(xs_tok[:, 0, :].rearrange("p (h c) -> p h c", c=64),
                                             xs_tok[:, 0, :].rearrange("p (h c) -> p h c", c=64),
                                             per_head_in[:, 2, :].unsqueeze(2).broadcast_to([P, SSM_H, 64]), ALU.mult))
                    O.step(dve.tensor_tensor(xs_tok[:, 1, :].rearrange("p (h c) -> p h c", c=64),
                                             xs_tok[:, 1, :].rearrange("p (h c) -> p h c", c=64),
                                             per_head_in[:, 2, :].unsqueeze(2).broadcast_to([P, SSM_H, 64]), ALU.mult))
                    O.settle()
                    consumed(dve, s, "y", SSM_H // 2 - 1)
                    O.step(dve.tensor_tensor(y_tok[:, :, :], y_tok[:, :, :], xs_tok[:, :, :], ALU.add))
                    O.settle()
                    O.step(dve.tensor_tensor(y_tok[:, :, :], y_tok[:, :, :], z_tok[:, :, :], ALU.mult))
                    O.settle()
                    O.step(dve.tensor_tensor(xs_tok[:, :, :], y_tok[:, :, :], y_tok[:, :, :], ALU.mult))
                    O.settle()
                    O.step(dve.tensor_reduce(ss_stat[:, 0, :], xs_tok[:, :, :].rearrange("p t (g c) -> p (t g) c", c=COLS),
                                             X, ALU.add))
                    O.settle()
                    signal(dve.tensor_scalar(ss_stat[:, 0, :], ss_stat[:, 0, :], 1.0 / COLS, 1e-6, ALU.mult, ALU.add),
                           event(s, "group_mean"), 1)
                    dve.wait_ge(event(s, "group_rstd"), 1)
                    for b in range(2):
                        gain = use_row(s, "gate_norm%d" % b)
                        for t in range(TT):
                            for g in range(2):
                                c = slice((2 * b + g) * COLS, (2 * b + g + 1) * COLS)
                                n = t * 4 + 2 * b + g
                                signal(dve.scalar_tensor_tensor(out=y_tok[:, t, c], in0=y_tok[:, t, c],
                                                                scalar=ss_stat[:, 1, n:n + 1],
                                                                in1=gain[:, g * COLS:(g + 1) * COLS],
                                                                op0=ALU.mult, op1=ALU.mult),
                                       event(s, "y_scaled"), 4 * b + 2 * t + g + 1)
                        release_row()
                    activations(s, "ssmo", 8)
                    for b in range(2):
                        lo_parts((s, "out", b))
                    for b in range(2):
                        add_to_h((s, "out", b), b * COLS)
                elif s == "kv":
                    h_done(dve, stage_before.get(s))
                    signal(dve.memset(rel[32:33, :], 1.0), event(s, "rel_one"), 1)
                    norm(s)
                    ready(dve, s, "bias")
                    frees_bank(dve.tensor_copy(bias_rows[:, :], B(s, "bias")[0:16, 0:BIAS_N]), s, "bias")
                    lo_parts((s, "kv"))
                    activations(s)
                    dve.wait_ge(ld_kv, 16 * 3)
                    for t in range(TT):
                        ready(dve, (s, "kv"), t)
                        O.step(dve.tensor_copy(k_tmp[:, t, :, 0, :],
                                               B((s, "kv"), t)[:, 0:P].rearrange("p (h c) -> p h c", c=64)))
                        frees_bank(dve.tensor_copy(v_tmp[:, t, :], B((s, "kv"), t)[:, P:2 * P]), (s, "kv"), t)
                    O.settle()
                    for t in range(TT):
                        O.step(dve.tensor_tensor(k_sq[:, t, :, :], k_tmp[:, t, :, 0, :], k_tmp[:, t, :, 0, :],
                                                 ALU.mult))
                    O.settle()
                    O.step(dve.tensor_reduce(sw_stat[:, 0, 0:4], k_sq[:, :, :, :].rearrange("p t h c -> p (t h) c"),
                                             X, ALU.add))
                    O.settle()
                    signal(dve.tensor_scalar(sw_stat[:, 0, 0:4], sw_stat[:, 0, 0:4], 1.0 / 64, 1e-6, ALU.mult,
                                             ALU.add), event(s, "head_mean"), 1)
                    dve.wait_ge(event(s, "head_rstd"), 1)
                    for t in range(TT):
                        for g in range(2):
                            O.step(dve.scalar_tensor_tensor(out=k_tmp[:, t, g, 0, :], in0=k_tmp[:, t, g, 0, :],
                                                            scalar=sw_stat[:, 1, 2 * t + g:2 * t + g + 1],
                                                            in1=k_norm[:, :], op0=ALU.mult, op1=ALU.mult))
                    O.settle()
                    signal(dve.tensor_copy(k_tmp[:, :, :, 1, :].rearrange("p t h c -> p (t h) c"),
                                           k_tmp[:, :, :, 0, :].rearrange("p t h c -> p (t h) c")),
                           event(s, "keys"), 1)
                elif s == "swa":
                    norm(s)
                    lo_parts((s, "q", 0))
                    activations(s)
                    lo_parts((s, "q", 1))
                    for b in range(2):
                        consumed(dve, (s, "q", b), TT - 1)
                    dve.wait_ge(ld_swa, 32)

                    def sw_heads(x):
                        return x[:, :, :].rearrange("p t (h c) -> p (t h) c", c=64)

                    O.step(dve.tensor_tensor(xn[:, :, :], sq_tok[:, :, :], sq_tok[:, :, :], ALU.mult))
                    O.settle()
                    O.step(dve.tensor_reduce(sw_stat[:, 0, :], sw_heads(xn), X, ALU.add))
                    O.settle()
                    signal(dve.tensor_scalar(sw_stat[:, 0, :], sw_stat[:, 0, :], 1.0 / 64, 1e-6, ALU.mult, ALU.add),
                           event(s, "head_mean"), 1)
                    O.step(dve.tensor_tensor(sw_heads(sq_tok), sw_heads(sq_tok), over(q_norm[:, :], 32), ALU.mult))
                    dve.wait_ge(event(s, "head_rstd"), 1)
                    O.settle()
                    signal(dve.tensor_tensor(sw_heads(sq_tok), sw_heads(sq_tok),
                                             sw_stat[:, 1, :].unsqueeze(2).broadcast_to([P, 32, 64]), ALU.mult),
                           event(s, "queries"), 1)
                    dve.wait_ge(ld_bias, 32)
                    for u in range(8 * TT):
                        pr, qt = u // TT, u % TT
                        n = (qt + 1) * P
                        if u >= 2:
                            dve.wait_ge(event(s, "exp"), 3 * (u - 1))
                        for c in range(2):
                            ready(dve, s, "s", pr, qt, c)
                            frees_bank(dve.scalar_tensor_tensor(
                                out=s_sc[:, u % 2, c, 0:n], in0=B(s, "s", pr, qt, c)[:, 0:n], scalar=64 ** -0.5,
                                in1=bias[:, 2 * pr + c, 0:n], op0=ALU.mult, op1=ALU.add), s, "s", pr, qt, c)
                        O.settle()
                        m_, sink = s_sm[:, u, 6:8], sinks[:, 2 * pr:2 * pr + 2]
                        O.step(dve.tensor_reduce(m_, s_sc[:, u % 2, :, 0:n], X, ALU.max))
                        O.settle()
                        O.step(dve.tensor_tensor(m_, m_, sink, ALU.max))
                        O.settle()
                        O.step(dve.tensor_scalar(s_sm[:, u, 2:4], m_, -1.0, None, ALU.mult))
                        signal(dve.tensor_tensor(s_sm[:, u, 0:2], sink, m_, ALU.subtract), event(s, "max"), u + 1)
                        dve.wait_ge(event(s, "exp"), 3 * (u + 1))
                        O.step(dve.tensor_tensor(s_sm[:, u, 4:6], s_sm[:, u, 4:6], s_sm[:, u, 0:2], ALU.add))
                        O.settle()
                        O.step(dve.reciprocal(s_sm[:, u, 6:8], s_sm[:, u, 4:6]))
                        O.settle()
                        for c in range(2):
                            v = s_pr[:, pr % 2, qt, c, 0:n]
                            signal(dve.tensor_scalar(v, v, s_sm[:, u, 6 + c:7 + c], None, ALU.mult),
                                   event(s, "att"), 2 * u + c + 1)
                    lo_parts((s, "out", 0))
                    activations(s, "swao")
                    lo_parts((s, "out", 1))
                    for b in range(2):
                        add_to_h((s, "out", b), b * COLS)
                elif s.startswith("ffn"):
                    norm(s)
                    activations(s)
                    blocks = ffn_blocks()

                    def gated(b):
                        if b >= 2:
                            ready(dve, s, "gt", b - 2, blocks[b - 2][1] // 256 - 1)
                        for t in range(TT):
                            consumed(dve, (s, "u", b), t)
                            ready(dve, (s, "v", b), t)
                            cols = blocks[b][1]
                            frees_bank(dve.tensor_tensor(g_tok[:, b % 2, t, 0:cols], silu[:, t, 0:cols],
                                                         B((s, "v", b), t)[:, 0:cols], ALU.mult), (s, "v", b), t)

                    def gated_lo(b):
                        for i in range(blocks[b][1] // 256):
                            take_lo(s, "gt", b, i)

                    for b in range(len(blocks)):
                        lo_parts((s, "u", b))
                        if b:
                            gated(b - 1)
                        lo_parts((s, "v", b))
                        if b:
                            gated_lo(b - 1)
                    lo_parts((s, "d", 0), 2)
                    gated(len(blocks) - 1)
                    gated_lo(len(blocks) - 1)
                    for b in range(2):
                        lo_parts((s, "d", b))
                    for b in range(2):
                        add_to_h((s, "d", b), b * COLS, 0.5)

        @block.tensor
        def _(pe):
            nth = [0]

            def begin(*name):
                assert jobs[name] == nth[0], (name, jobs[name], nth[0])
                nth[0] += 1
                if jobs[name] >= BANKS:
                    pe.wait_ge(bank_free[jobs[name] % BANKS], jobs[name] // BANKS)
                return B(*name)

            def end(ins):
                ins.then_inc(psum_ready, 1)

            def gemm(name, hi, lo_, need=None):
                first, last, cols = gemms[name]
                outs = [begin(name, t) for t in range(TT)]
                k_end = slabs[last - 1][1] + slabs[last - 1][2]
                for n in range(first, last):
                    _, k0, kn, _, _, release = slabs[n]
                    pe.wait_ge(slab_hi, n + 1)
                    pe.wait_ge(slab_lo, n + 1)
                    if need:
                        need(k0, kn)
                    for t in range(TT):
                        for k in range(k0, k0 + kn):
                            a_hi, a_lo = hi[:, k, t * P:(t + 1) * P], lo_[:, k, t * P:(t + 1) * P]
                            b_hi = w_hi[:, n % PART_SLOTS, k - k0, 0:cols]
                            b_lo = w_lo[:, n % PART_SLOTS, k - k0, 0:cols]
                            pe.matmul(outs[t][:, 0:cols], a_hi, b_hi, start=(k == 0), stop=False)
                            pe.matmul(outs[t][:, 0:cols], a_lo, b_hi, start=False, stop=False)
                            mm = pe.matmul(outs[t][:, 0:cols], a_hi, b_lo, start=False, stop=(k == k_end - 1))
                        if n == last - 1:
                            end(mm)
                    if n < last - 1:
                        mm.then_inc(slab_used, 1)

            def gemm_by_channel(name, hi, lo_, need):
                first, last, _ = gemms[name]
                for n in range(first, last):
                    pe.wait_ge(slab_hi, n + 1)
                    pe.wait_ge(slab_lo, n + 1)
                need(0, KD)
                for j in range(2):
                    o = begin(name, j)
                    for c in range(2):
                        dst = o[:, c * T:(c + 1) * T]
                        cols = slice((2 * j + c) * P, (2 * j + c + 1) * P)
                        for k in range(KD):
                            n = (first + k // SLAB_K) % PART_SLOTS
                            a, b = w_hi[:, n, k % SLAB_K, cols], w_lo[:, n, k % SLAB_K, cols]
                            pe.matmul(dst, a, hi[:, k, :], start=(k == 0), stop=False)
                            pe.matmul(dst, a, lo_[:, k, :], start=False, stop=False)
                            mm = pe.matmul(dst, b, hi[:, k, :], start=False, stop=(k == KD - 1))
                    end(mm)

            def turn(name, src, k0, nk=2):
                o = begin(*name)
                for k in range(nk):
                    for t in range(TT):
                        c = (k0 + k) * P
                        mm = pe.transpose(o[:, (k * TT + t) * P:(k * TT + t + 1) * P], src[:, t, c:c + P], ident)
                end(mm)

            def turn_activations(s, tag=None, wait=None):
                if wait is None:
                    pe.wait_ge(event(s, "scaled"), TT)
                else:
                    wait()
                for i in range(4):
                    turn((tag or s, "turn", i), xn, 2 * i)

            def turned(tag):
                def need(k0, kn):
                    for i in range(k0 // 2, (k0 + kn + 1) // 2):
                        consumed(pe, tag, "turn", i)
                return need

            def rwkv(s):
                turn_activations(s)
                pe.wait_ge(ld_lora, 16 * 6)
                for i, x in enumerate("wa"):
                    pe.wait_ge(event(s, "lora_mixed"), i + 1)
                    o = begin(s, "lora_in", x)
                    for k in range(KD):
                        mm = pe.matmul(o[0:64, 0:T], lora_w1[:, i, k, :], (mix_v, mix_k)[i][:, k, :],
                                       start=(k == 0), stop=(k == KD - 1))
                    end(mm)
                    consumed(pe, s, "lora_in", x)
                    for b in range(2):
                        for t in range(TT):
                            o = begin(s, "lora_out", x, b, t)
                            end(pe.matmul(o[:, :], lora_t[0:65, i, t * P:(t + 1) * P],
                                          rw_kap[0:65, i, b * COLS:(b + 1) * COLS], start=True, stop=True))
                for i, x in enumerate("rkvg"):
                    pe.wait_ge(event(s, "mix_lo"), i + 1)
                    for b in range(2):
                        gemm((s, x, b), x_hi[i % 2], x_lo[i % 2])
                consumed(pe, s, "lora_out", "w", 1, 1)
                for b in range(2):
                    for w in range(TT):
                        for what in ("cum", "cumx"):
                            o = begin(s, what, b, w)
                            end(pe.matmul(o[:, :], C(what), rw_sig[:, w, b * COLS:(b + 1) * COLS],
                                          start=True, stop=True))
                o = begin(s, "carry")
                for pr in range(8):
                    for w in range(TT):
                        mm = pe.matmul(o[:, pr:pr + 1], rw_sig[:, w, pr * P:(pr + 1) * P], C("ends")[:, w:w + 1],
                                       start=(w == 0), stop=(w == 1))
                end(mm)

                for w in range(TT):
                    for gg in range(2):
                        pair = (2 * gg, 2 * gg + 1)
                        for g in pair:
                            pe.wait_ge(event(s, "decayed"), 4 if g >= 2 or w else 2)
                            for pp in range(2):
                                o = begin(s, "ct", w, g, pp)
                                c = (2 * g + pp) * P
                                for i, x in enumerate((rw_kap, rw_r, rw_a, rw_k)):
                                    mm = pe.transpose(o[:, i * P:(i + 1) * P], x[:, w, c:c + P], ident)
                                end(mm)
                            for par in range(2):
                                r_ = slice(64 * par, 64 * par + 64)
                                for what, l_, rr, n in (("ab", 2, slice(0, 2), 2 * P), ("ak", 3, slice(0, 2), 2 * P),
                                                        ("a0", 0, slice(2, 3), P)):
                                    o = begin(s, what, w, g, par)
                                    for pp in range(2):
                                        consumed(pe, s, "ct", w, g, pp)
                                        mm = pe.matmul(o[:, pp * n:(pp + 1) * n], ct[r_, g % 2, pp, l_, :],
                                                       ct[r_, g % 2, pp, rr, :].rearrange("p i c -> p (i c)"),
                                                       start=True, stop=True)
                                    end(mm)
                        for l in range(1, 7):
                            for g in pair:
                                if l == 1:
                                    pe.wait_ge(event(s, "inverse_begun"), 4 * w + g + 1)
                                else:
                                    consumed(pe, s, "tx", w, g, l - 1)
                                o = begin(s, "x", w, g, l)
                                for it in range(4):
                                    mm = pe.matmul(o[:, it * P:(it + 1) * P], ab[:, g % 2, it, 0, :],
                                                   inv[:, g % 2, 0, it, :], start=True, stop=True)
                                end(mm)
                            for g in pair:
                                x_, tt_ = x_mask[:, g % 2], inv[:, g % 2, 1]
                                consumed(pe, s, "x", w, g, l)
                                if l > 1:
                                    consumed(pe, s, "xt", w, g, l - 1)
                                if l < 6:
                                    o = begin(s, "tx", w, g, l)
                                    for it in range(4):
                                        mm = pe.matmul(o[:, it * P:(it + 1) * P], tt_[:, it, :], x_[:, it, :],
                                                       start=True, stop=True)
                                    end(mm)
                                o = begin(s, "xt", w, g, l)
                                for it in range(4):
                                    mm = pe.matmul(o[:, it * P:(it + 1) * P], x_[:, it, :], tt_[:, it, :],
                                                   start=True, stop=True)
                                end(mm)
                        for g in pair:
                            if w:
                                consumed(pe, s, "s", 0, g)
                            o = begin(s, "rhs", w, g)
                            for pp in range(2):
                                pr = 2 * g + pp
                                if w:
                                    pe.matmul(o[:, pp * P:(pp + 1) * P], ct[:, g % 2, pp, 0, :], state[:, pr, :],
                                              start=True, stop=False)
                                for par in range(2):
                                    c = 64 * par
                                    mm = pe.matmul(o[:, pp * P + c:pp * P + c + 64], ab[:, g % 2, 2 * par + pp, 2, :],
                                                   rw_v[:, w, pr * P + c:pr * P + c + 64], start=(w == 0),
                                                   stop=(w == 0 or par == 1))
                            end(mm)
                        for g in pair:
                            consumed(pe, s, "rhs", w, g)
                            consumed(pe, s, "xt", w, g, 6)
                            o = begin(s, "u", w, g)
                            for pp in range(2):
                                for par in range(2):
                                    c = 64 * par
                                    mm = pe.matmul(o[:, pp * P + c:pp * P + c + 64], inv[:, g % 2, 1, 2 * par + pp, :],
                                                   rhs_sb[:, g % 2, pp, c:c + 64], start=True, stop=True)
                            end(mm)
                        for g in pair:
                            consumed(pe, s, "u", w, g)
                            o = begin(s, "y", w, g)
                            for pp in range(2):
                                pr = 2 * g + pp
                                if w:
                                    pe.matmul(o[:, pp * P:(pp + 1) * P], ct[:, g % 2, pp, 1, :], state[:, pr, :],
                                              start=True, stop=False)
                                for par in range(2):
                                    c = 64 * par
                                    dst = o[:, pp * P + c:pp * P + c + 64]
                                    pe.matmul(dst, ab[:, g % 2, 2 * par + pp, 3, :],
                                              rw_v[:, w, pr * P + c:pr * P + c + 64], start=(w == 0), stop=False)
                                    mm = pe.matmul(dst, ab[:, g % 2, 2 * par + pp, 1, :],
                                                   un_sb[:, g % 2, pp, c:c + 64], start=False,
                                                   stop=(w == 0 or par == 1))
                            end(mm)
                            if w == 0:
                                o = begin(s, "s", w, g)
                                for pp in range(2):
                                    c = slice((2 * g + pp) * P, (2 * g + pp + 1) * P)
                                    pe.matmul(o[:, pp * P:(pp + 1) * P], rw_k[:, 0, c], rw_v[:, 0, c],
                                              start=True, stop=False)
                                    mm = pe.matmul(o[:, pp * P:(pp + 1) * P], rw_a[:, 0, c], un_sb[:, g % 2, pp, :],
                                                   start=False, stop=True)
                                end(mm)
                turn_activations(s, "rwo", lambda: pe.wait_ge(event(s, "gated"), 1))
                for b in range(2):
                    gemm((s, "o", b), x_hi[0], x_lo[0], turned("rwo"))

            pe.wait_ge(ld_const, 32)
            for s in STAGES:
                if s == "rw":
                    rwkv(s)
                elif s in ("ple0", "ple1"):
                    i = int(s[-1])
                    pe.wait_ge(ld_p, 16)
                    turn((s, "turn_p", 0), p_tok[:, i], 0)
                    consumed(pe, s, "turn_p", 0)
                    for b in range(2):
                        gemm((s, "p", b), p_hi, p_lo)
                    turn_activations(s)
                    for b in range(2):
                        gemm((s, "g", b), x_hi[0], x_lo[0], turned(s))
                elif s == "da":
                    turn_activations(s)
                    for i in range(8):
                        gemm((s, i), x_hi[0], x_lo[0], turned(s))
                    for i in range(8):
                        pe.wait_ge(event(s, "roped"), 2 * (i // 4) + TT)
                        turn((s, "qk", i), q_tok if i < 4 else k_tok, 2 * (i % 4))
                    consumed(pe, s, "qk", 7)

                    def weigh_values(hd):
                        pe.wait_ge(event(s, "att"), 2 * (hd + 1))
                        o = begin(s, "at", hd)
                        for i, (qt, kt) in enumerate(((0, 0), (1, 0), (1, 1))):
                            mm = pe.transpose(o[:, i * P:(i + 1) * P], att[:, hd % 2, qt, kt * P:(kt + 1) * P], ident)
                        end(mm)
                        consumed(pe, s, "at", hd)
                        o = begin(s, "o", hd)
                        v = [v_tok[:, kt, hd * P:(hd + 1) * P] for kt in range(2)]
                        a = att_ch[:, hd % 2]
                        pe.matmul(o[:, 0:P], a[:, 0, :], v[0], start=True, stop=True)
                        pe.matmul(o[:, P:2 * P], a[:, 1, :], v[0], start=True, stop=False)
                        end(pe.matmul(o[:, P:2 * P], a[:, 2, :], v[1], start=False, stop=True))

                    for hd in range(8):
                        for qt in range(TT):
                            for c in range(2):
                                o = begin(s, "s", hd, qt, c)
                                rows_ = slice(64 * c, 64 * c + 64)
                                end(pe.matmul(o[:, 0:(qt + 1) * P], q_ch[rows_, hd, qt * P:(qt + 1) * P],
                                              k_ch[rows_, hd, 0:(qt + 1) * P], start=True, stop=True))
                        if hd:
                            weigh_values(hd - 1)
                    weigh_values(7)
                    turn_activations(s, "dao", lambda: pe.wait_ge(event(s, "heads"), 1))
                    for b in range(2):
                        gemm((s, "out", b), x_hi[0], x_lo[0], turned("dao"))
                elif s == "ssm":
                    turn_activations(s)
                    gemm((s, "dt"), x_hi[0], x_lo[0], turned(s))
                    dta = dts[:, 6]
                    pe.wait_ge(event(s, "dta"), TT)
                    o = begin(s, "acum")
                    tri, ones = C("tri")[:, 0:P], C("tri")[:, P:2 * P]
                    pe.matmul(o[:, 0:SSM_H], tri, dta[:, 0, :], start=True, stop=True)
                    pe.matmul(o[:, SSM_H:2 * SSM_H], ones, dta[:, 0, :], start=True, stop=False)
                    end(pe.matmul(o[:, SSM_H:2 * SSM_H], tri, dta[:, 1, :], start=False, stop=True))
                    for i in range(4):
                        gemm((s, "z", i), x_hi[0], x_lo[0])

                    def turn_conv(i):
                        n = CONV_ORDER.index(i)
                        for j in range(2):
                            pe.wait_ge(event(s, "conv_out"), 2 * (2 * n + j + 1))
                            o = begin(s, "xt", i, j)
                            for t in range(TT):
                                for c in range(2):
                                    m = (2 * t + c) * P
                                    mm = pe.transpose(o[:, m:m + P], conv_sum[:, j, c, t * P:(t + 1) * P], ident)
                            end(mm)

                    before = None
                    for i in CONV_ORDER:
                        gemm_by_channel((s, "xb", i), x_hi[0], x_lo[0], turned(s))
                        if before is not None and before < 4:
                            turn_conv(before)
                        before = i
                    turn_conv(before)
                    for g in range(4):
                        o = begin(s, "cb", g)
                        pe.matmul(o[:, 0:T], bc[:, g, 0:P], bc[:, 4 + g, :], start=True, stop=True)
                        end(pe.matmul(o[:, T:T + P], bc[:, g, P:T], bc[:, 4 + g, P:T], start=True, stop=True))
                    for u in range(SSM_H // 2 + 2):
                        if u < SSM_H // 2:
                            o = begin(s, "seg", u)
                            for c in range(2):
                                hd = 2 * u + c
                                col = [dta[:, t, hd:hd + 1].broadcast_to([P, P]) for t in range(TT)]
                                pe.matmul(o[:, c * T:(c + 1) * T], col[0], C("tri"), start=True, stop=False)
                                mm = pe.matmul(o[:, c * T + P:(c + 1) * T], col[1], tri, start=False, stop=True)
                            end(mm)
                        if u >= 2:
                            v = u - 2
                            pe.wait_ge(event(s, "x_dt"), 1)
                            pe.wait_ge(event(s, "weights"), v + 1)
                            o = begin(s, "y", v)
                            for c in range(2):
                                x_ = slice((2 * v + c) * 64, (2 * v + c + 1) * 64)
                                w_ = seg[:, v % 2, c, :]
                                pe.matmul(o[:, c * 64:c * 64 + 64], w_[:, 0:P], y_tok[:, 0, x_], start=True, stop=True)
                                dst = o[:, P + c * 64:P + c * 64 + 64]
                                pe.matmul(dst, w_[:, P:T], y_tok[:, 0, x_], start=True, stop=False)
                                mm = pe.matmul(dst, w_[:, T:T + P], y_tok[:, 1, x_], start=False, stop=True)
                            end(mm)
                    for i in range(8):
                        pe.wait_ge(event(s, "y_scaled"), 4 * (i // 4 + 1))
                        turn(("ssmo", "turn", i), y_tok, 2 * i)
                    for b in range(2):
                        gemm((s, "out", b), y_hi, y_lo, turned("ssmo"))
                elif s == "kv":
                    pe.wait_ge(ld_kv, 16 * 3)
                    pe.wait_ge(event(s, "rel_one"), 1)
                    o = begin(s, "bias")
                    end(pe.matmul(o[0:16, 0:BIAS_N], rel[:, :], picks[:, :], start=True, stop=True))
                    turn_activations(s)
                    gemm((s, "kv"), x_hi[0], x_lo[0], turned(s))
                    for t in range(TT):
                        consumed(pe, (s, "kv"), t)
                    o = begin(s, "vt")
                    for t in range(TT):
                        m = (1 - t) * P
                        mm = pe.matmul(o[:, m:m + P], C("flip"), v_tmp[:, t, :], start=True, stop=True)
                    end(mm)
                    pe.wait_ge(event(s, "keys"), 1)
                    o = begin(s, "kt")
                    for g in range(2):
                        for t in range(TT):
                            m = (g * TT + 1 - t) * P
                            mm = pe.matmul(o[:, m:m + P], k_tmp[:, t, g, :, :].rearrange("p a c -> p (a c)"),
                                           C("flip"), start=True, stop=True)
                    end(mm)
                elif s == "swa":
                    turn_activations(s)
                    for b in range(2):
                        gemm((s, "q", b), x_hi[0], x_lo[0], turned(s))
                    pe.wait_ge(event(s, "queries"), 1)
                    for i in range(4):
                        turn((s, "qt", i), sq_tok, 2 * i)
                    consumed(pe, s, "qt", 3)
                    consumed(pe, "kv", "kt")

                    def window_values(pr):
                        pe.wait_ge(event(s, "att"), 4 * (pr + 1))
                        for par in range(2):
                            o = begin(s, "at", pr, par)
                            for i, (qt, kt) in enumerate(((0, 0), (1, 0), (1, 1))):
                                mm = pe.transpose(o[:, i * P:(i + 1) * P],
                                                  s_pr[:, pr % 2, qt, par, kt * P:(kt + 1) * P], ident)
                            end(mm)
                        o = begin(s, "o", pr)
                        for par in range(2):
                            consumed(pe, s, "at", pr, par)
                            g = pr // 4
                            v = [kv_v[:, kt, 64 * g:64 * g + 64] for kt in range(2)]
                            c = 64 * par
                            pe.matmul(o[:, c:c + 64], s_at[:, par, 0, :], v[1], start=True, stop=True)
                            pe.matmul(o[:, P + c:P + c + 64], s_at[:, par, 1, :], v[0], start=True, stop=False)
                            mm = pe.matmul(o[:, P + c:P + c + 64], s_at[:, par, 2, :], v[1], start=False, stop=True)
                        end(mm)

                    for pr in range(8):
                        for qt in range(TT):
                            for par in range(2):
                                o = begin(s, "s", pr, qt, par)
                                r_ = slice(64 * par, 64 * par + 64)
                                end(pe.matmul(o[:, 0:(qt + 1) * P], sq_ch[r_, pr, qt * P:(qt + 1) * P],
                                              kv_k[r_, pr // 4, (1 - qt) * P:T], start=True, stop=True))
                        if pr:
                            window_values(pr - 1)
                    window_values(7)
                    turn_activations(s, "swao", lambda: consumed(pe, s, "o", 7))
                    for b in range(2):
                        gemm((s, "out", b), x_hi[0], x_lo[0], turned("swao"))
                elif s.startswith("ffn"):
                    turn_activations(s)
                    blocks = ffn_blocks()

                    def turn_gated(b):
                        for t in range(TT):
                            consumed(pe, (s, "v", b), t)
                        for i in range(blocks[b][1] // 256):
                            turn((s, "gt", b, i), g_tok[:, b % 2], 2 * i)

                    for b in range(len(blocks)):
                        gemm((s, "u", b), x_hi[0], x_lo[0], turned(s))
                        if b:
                            turn_gated(b - 1)
                        gemm((s, "v", b), x_hi[0], x_lo[0])
                    turn_gated(len(blocks) - 1)

                    def down(k0, kn):
                        b = min(k0 // 4, len(blocks) - 1)
                        consumed(pe, s, "gt", b, blocks[b][1] // 256 - 1)

                    for b in range(2):
                        gemm((s, "d", b), g_hi, g_lo, down)


_INS = ['x', 'p', 'rw_norm', 'rw_mu', 'rw_w_in', 'rw_w0', 'rw_w1', 'rw_w2', 'rw_a0', 'rw_a1', 'rw_a2', 'rw_k_k',
        'rw_k_a', 'rw_r_k', 'rw_ln_w', 'rw_ln_b', 'rw_w_out', 'da_norm', 'da_w_in', 'da_lq1', 'da_lk1', 'da_lq2',
        'da_lk2', 'da_subln', 'da_w_out', 'pe_norm', 'pe_w_gate', 'pe_w_proj', 'final_norm', 'ffn_norm_2',
        'ffn_w1_2', 'ffn_w3_2', 'ffn_w2_2', 'ssm_norm_2', 'ssm_w_in_2', 'ssm_conv_w_2', 'ssm_conv_b_2',
        'ssm_dt_bias_2', 'ssm_a_log_2', 'ssm_d_2', 'ssm_gate_norm_2', 'ssm_w_out_2', 'kv_norm_2', 'w_kv_2',
        'k_norm_2', 'attn_norm_2', 'w_q_2', 'q_norm_2', 'sinks_2', 'w_o_2', 'rel_bias_2']
_OUTS = [((1, T, D), 'float32')]


def kernel(**inputs):
    import numpy as _np
    import concourse.bacc as _bacc
    from concourse import mybir as _mybir
    from concourse.bass_utils import run_bass_kernel_spmd as _run

    nc = _bacc.Bacc("TRN2", target_bir_lowering=False, num_devices=1)
    arrays, args = {}, {}
    made = {"constants": constants, "bias_picks": bias_picks}
    for name in _INS + list(made):
        a = made[name]() if name in made else _np.asarray(inputs[name])
        if name == "ssm_conv_w_2":
            a = a.reshape(4, 24, P).transpose(2, 1, 0)
        if name == "ssm_conv_b_2":
            a = a.reshape(24, P).T
        if name == "rw_mu":
            a = a.reshape(6, KD, P).transpose(2, 0, 1)
        a = _np.ascontiguousarray(a)
        arrays[f"in_{name}_dram"] = a
        args[name] = nc.dram_tensor(f"in_{name}_dram", a.shape, _mybir.dt.from_np(a.dtype), kind="ExternalInput").ap()
    shape, dtype = _OUTS[0]
    out = nc.dram_tensor("out_0_dram", shape, _mybir.dt.from_np(_np.dtype(dtype)), kind="ExternalOutput").ap()
    program(nc, args, out)
    r = _run(nc, [arrays], core_ids=[0])
    return r.results[0]["out_0_dram"]
```

```python
from contextlib import ExitStack
import math

import numpy as np
import concourse.bass as bass
from concourse import mybir

F32 = mybir.dt.float32
F32R = mybir.dt.float32r
ALU = mybir.AluOpType
ACT = mybir.ActivationFunctionType
X = mybir.AxisListType.X

P = 128
T = 256
TT = T // P
D = 1024
KD = D // P
FF = 2816
KF = FF // P
COLS = 512
SLAB_K = 4
BANKS = 8
RAW_SLOTS, PART_SLOTS = 3, 3
ROW_SLOTS = 2
DECAY = math.exp(-0.5)
NEG = -1.0e30
LAMBDA_INIT = 0.8 - 0.6 * math.exp(-0.3)

SSM_H = 32
CONV_ORDER = (4, 5, 0, 1, 2, 3)
BIAS_N = 3 * P

DEFERRED = ("ple0", "ple1", "da", "ffn0", "ffn1", "ffn2", "ffn3", "kv", "swa")

STAGES = ["rw", "ple0", "da", "ple1", "final", "ffn0", "ssm", "ffn1", "kv", "ffn2", "swa", "ffn3"]


def column_blocks(n):
    return [(c, min(COLS, n - c)) for c in range(0, n, COLS)]


CONST_COLS = [
    ("ident", P),
    ("flip", P),
    ("strict_incl", 2 * P),
    ("levels", 7 * P),
    ("cum", P),
    ("cumx", P),
    ("ends", 2),
    ("causal", P),
    ("cos", TT * 64), ("sin", TT * 64),
    ("tri", 2 * P),
]
CONST_AT, N_CONST = {}, 0
for _name, _n in CONST_COLS:
    CONST_AT[_name] = (N_CONST, N_CONST + _n)
    N_CONST += _n


def constants():
    f = np.float32
    a, b = np.arange(P)[:, None], np.arange(P)[None, :]
    levels = []
    for l in range(7):
        m = 1 << l
        levels.append(((a // (2 * m) == b // (2 * m)) & ((a // m) % 2 == 1) & ((b // m) % 2 == 0)).T)
    half = 64 // 2
    inv_freq = 1.0 / (10000.0 ** (np.arange(0, 64, 2, dtype=f) / f(64)))
    ang = np.arange(T, dtype=f)[:, None] * inv_freq[None, :].astype(f)
    ang = np.concatenate([ang, ang], 1)
    sign = np.concatenate([-np.ones(half), np.ones(half)])[None, :]

    def tiles(x):
        return x.reshape(TT, P, 64).transpose(1, 0, 2).reshape(P, TT * 64)

    parts = {
        "ident": a == b, "flip": a + b == P - 1, "strict_incl": np.concatenate([a < b, a <= b], 1),
        "levels": np.concatenate(levels, 1),
        "cum": -DECAY * ((a <= b) * 1.0 - (a < 64)), "cumx": -DECAY * ((a < b) * 1.0 - (a < 64)),
        "ends": np.concatenate([-DECAY * (a >= 64), -DECAY * (a < 64)], 1),
        "causal": np.where(b > a, NEG, 0.0),
        "cos": tiles(np.cos(ang)), "sin": tiles(np.sin(ang) * sign),
        "tri": np.concatenate([a <= b, np.ones((P, P))], 1),
    }
    return np.ascontiguousarray(np.concatenate([parts[n].astype(f) for n, _ in CONST_COLS], 1))


def bias_picks():
    f = np.float32
    dist = np.arange(BIAS_N) - 127
    n = np.maximum(dist, 0)
    large = 16 + (np.log(np.maximum(n, 1).astype(f) / f(16)) / f(math.log(128 / 16)) * f(16)).astype(np.int32)
    bucket = np.where(n < 16, n, np.minimum(large, 31))
    inside = (dist >= 0) & (dist < 128)
    picks = np.zeros((33, BIAS_N), f)
    picks[bucket, np.arange(BIAS_N)] = inside
    picks[32] = np.where(inside, 0.0, NEG)
    return picks


class Order:

    def __init__(self, eng, sem):
        self.eng, self.sem, self.n = eng, sem, 0
        self.last = None

    def step(self, ins):
        ins.then_inc(self.sem, 1)
        self.n += 1
        self.last = (self.sem, self.n)

    def settle(self):
        if self.last:
            self.eng.wait_ge(*self.last)


class Plan:

    def __init__(self):
        self.jobs = {}
        self.slabs = []
        self.gemms = {}
        self.used = 0

    def job(self, *name):
        assert name not in self.jobs, name
        self.jobs[name] = len(self.jobs)

    def gemm_by_channel(self, name, w, c0):
        first = len(self.slabs)
        for k0 in range(0, KD, SLAB_K):
            self.slabs.append((w, k0, SLAB_K, c0, COLS, ("job", (name, 1))))
        self.gemms[name] = (first, len(self.slabs), COLS)
        for j in range(2):
            self.job(name, j)

    def gemm(self, name, w, k_tiles, c0, cols):
        first = len(self.slabs)
        for k0 in range(0, k_tiles, SLAB_K):
            kn = min(SLAB_K, k_tiles - k0)
            last = k0 + kn == k_tiles
            if not last:
                self.used += 1
            release = ("job", (name, TT - 1)) if last else ("used", self.used)
            self.slabs.append((w, k0, kn, c0, cols, release))
        self.gemms[name] = (first, len(self.slabs), cols)
        for t in range(TT):
            self.job(name, t)


def ffn_blocks():
    return column_blocks(FF)


def build_plan(W):
    p = Plan()

    def turned(tag, n=4):
        for i in range(n):
            p.job(tag, "turn", i)

    for s in STAGES:
        if s == "rw":
            turned(s)
            for i, x in enumerate("rkvg"):
                for b in range(2):
                    p.gemm((s, x, b), W["rw_w_in"], KD, i * D + b * COLS, COLS)
                if x == "k":
                    for y in "wa":
                        p.job(s, "lora_in", y)
                    for y in "wa":
                        for b in range(2):
                            for t in range(TT):
                                p.job(s, "lora_out", y, b, t)
            for b in range(2):
                for w in range(2):
                    p.job(s, "cum", b, w)
                    p.job(s, "cumx", b, w)
            p.job(s, "carry")
            for w in range(2):
                for gg in range(2):
                    for g in (2 * gg, 2 * gg + 1):
                        for pp in range(2):
                            p.job(s, "ct", w, g, pp)
                        for par in range(2):
                            p.job(s, "ab", w, g, par)
                            p.job(s, "ak", w, g, par)
                        p.job(s, "t0", w, g)
                    for l in range(1, 7):
                        for g in (2 * gg, 2 * gg + 1):
                            p.job(s, "x", w, g, l)
                        for g in (2 * gg, 2 * gg + 1):
                            p.job(s, "tx", w, g, l)
                        for g in (2 * gg, 2 * gg + 1):
                            if l < 6:
                                p.job(s, "tt", w, g, l)
                    for g in (2 * gg, 2 * gg + 1):
                        p.job(s, "rhs", w, g)
                    for g in (2 * gg, 2 * gg + 1):
                        p.job(s, "u", w, g)
                    for g in (2 * gg, 2 * gg + 1):
                        p.job(s, "y", w, g)
                        if w == 0:
                            p.job(s, "s", w, g)
            turned("rwo")
            for b in range(2):
                p.gemm((s, "o", b), W["rw_w_out"], KD, b * COLS, COLS)
        elif s in ("ple0", "ple1"):
            i = int(s[-1])
            for j in range(1):
                p.job(s, "turn_p", j)
            for b in range(2):
                p.gemm((s, "p", b), W["pe_w_proj%d" % i], 2, b * COLS, COLS)
            turned(s)
            for b in range(2):
                p.gemm((s, "g", b), W["pe_w_gate%d" % i], KD, b * COLS, COLS)
        elif s == "da":
            turned(s)
            for i in range(8):
                p.gemm((s, i), W["da_w_in"], KD, i * COLS, COLS)
            for i in range(8):
                p.job(s, "qk", i)
            for hd in range(8):
                for qt in range(2):
                    for c in range(2):
                        p.job(s, "s", hd, qt, c)
                if hd:
                    p.job(s, "at", hd - 1)
                    p.job(s, "o", hd - 1)
            p.job(s, "at", 7)
            p.job(s, "o", 7)
            turned("dao")
            for b in range(2):
                p.gemm((s, "out", b), W["da_w_out"], KD, b * COLS, COLS)
        elif s == "ssm":
            turned(s)
            p.gemm((s, "dt"), W["ssm_w_in"], KD, 5 * D, SSM_H)
            p.job(s, "acum")
            for i in range(4):
                p.gemm((s, "z", i), W["ssm_w_in"], KD, i * COLS, COLS)
            before = None
            for i in CONV_ORDER:
                p.gemm_by_channel((s, "xb", i), W["ssm_w_in"], 2 * D + i * COLS)
                if before is not None and before < 4:
                    for j in range(2):
                        p.job(s, "xt", before, j)
                before = i
            for j in range(2):
                p.job(s, "xt", before, j)
            for g in range(4):
                p.job(s, "cb", g)
            for u in range(SSM_H // 2 + 2):
                if u < SSM_H // 2:
                    p.job(s, "seg", u)
                if u >= 2:
                    p.job(s, "y", u - 2)
            turned("ssmo", 8)
            for b in range(2):
                p.gemm((s, "out", b), W["ssm_w_out"], 2 * KD, b * COLS, COLS)
        elif s == "kv":
            p.job(s, "bias")
            turned(s)
            p.gemm((s, "kv"), W["w_kv"], KD, 0, 256)
            p.job(s, "vt")
            p.job(s, "kt")
        elif s == "swa":
            turned(s)
            for b in range(2):
                p.gemm((s, "q", b), W["w_q"], KD, b * COLS, COLS)
            for i in range(4):
                p.job(s, "qt", i)
            for pr in range(8):
                for qt in range(2):
                    for par in range(2):
                        p.job(s, "s", pr, qt, par)
                if pr:
                    for par in range(2):
                        p.job(s, "at", pr - 1, par)
                    p.job(s, "o", pr - 1)
            for par in range(2):
                p.job(s, "at", 7, par)
            p.job(s, "o", 7)
            turned("swao")
            for b in range(2):
                p.gemm((s, "out", b), W["w_o"], KD, b * COLS, COLS)
        elif s == "final":
            pass
        elif s.startswith("ffn"):
            turned(s)
            n = len(ffn_blocks())
            for b, (c0, cols) in enumerate(ffn_blocks()):
                p.gemm((s, "u", b), W["w1_" + s[-1]], KD, c0, cols)
                if b:
                    for i in range(2):
                        p.job(s, "gt", b - 1, i)
                p.gemm((s, "v", b), W["w3_" + s[-1]], KD, c0, cols)
            p.job(s, "gt", n - 1, 0)
            for b in range(2):
                p.gemm((s, "d", b), W["w2_" + s[-1]], KF, b * COLS, COLS)
    return p


ROW_SOURCES = {
    "rw": ["rw_norm", "rw_k_k", "rw_k_a", "rw_r_k", "rw_ln_w", "rw_ln_b"],
    "ple0": ["pe_norm0"], "ple1": ["pe_norm1"], "da": ["da_norm"], "final": ["final_norm"],
    "ffn0": ["ffn_norm0"], "ffn1": ["ffn_norm1"], "ffn2": ["ffn_norm2"], "ffn3": ["ffn_norm3"],
    "ssm": ["ssm_norm", "gate_norm0", "gate_norm1"], "kv": ["kv_norm"], "swa": ["attn_norm"],
}


def program(nc, A, out):
    W = {"rw_w_in": A["rw_w_in"][0], "rw_w_out": A["rw_w_out"][0], "da_w_in": A["da_w_in"][0],
         "da_w_out": A["da_w_out"][0], "ssm_w_in": A["ssm_w_in_2"][0], "ssm_w_out": A["ssm_w_out_2"][0],
         "w_kv": A["w_kv_2"], "w_q": A["w_q_2"][0], "w_o": A["w_o_2"][0]}
    for i in range(2):
        W["pe_w_gate%d" % i] = A["pe_w_gate"][i]
        W["pe_w_proj%d" % i] = A["pe_w_proj"][i]
    for i in range(4):
        for m in (1, 2, 3):
            W["w%d_%d" % (m, i)] = A["ffn_w%d_2" % m][i // 2, i % 2]
    R = {"rw_norm": A["rw_norm"][0], "rw_k_k": A["rw_k_k"][0], "rw_k_a": A["rw_k_a"][0],
         "rw_r_k": A["rw_r_k"][0].rearrange("h n -> (h n)"), "rw_ln_w": A["rw_ln_w"][0],
         "rw_ln_b": A["rw_ln_b"][0], "pe_norm0": A["pe_norm"][0], "pe_norm1": A["pe_norm"][1],
         "da_norm": A["da_norm"][0], "final_norm": A["final_norm"], "ssm_norm": A["ssm_norm_2"][0],
         "gate_norm0": A["ssm_gate_norm_2"][0, 0:D], "gate_norm1": A["ssm_gate_norm_2"][0, D:2 * D],
         "kv_norm": A["kv_norm_2"], "attn_norm": A["attn_norm_2"][0]}
    for i in range(4):
        R["ffn_norm%d" % i] = A["ffn_norm_2"][i // 2, i % 2]

    plan = build_plan(W)
    jobs, slabs, gemms = plan.jobs, plan.slabs, plan.gemms
    rows = [(s, r) for s in STAGES for r in ROW_SOURCES[s]]
    row_at = {key: n for n, key in enumerate(rows)}

    with ExitStack() as ctx:
        def sb(name, shape, dt=F32, scope=ctx):
            return scope.enter_context(nc.sbuf_tensor(name, shape, dt))

        def sem(name):
            return ctx.enter_context(nc.semaphore(name))

        bank = [ctx.enter_context(nc.psum_tensor("bank%d" % i, [P, COLS], F32)) for i in range(BANKS)]

        h = sb("h", [P, TT, D])
        xn = sb("xn", [P, TT, D])
        raw = sb("raw", [P, RAW_SLOTS, SLAB_K, COLS])
        w_hi = sb("w_hi", [P, PART_SLOTS, SLAB_K, COLS], F32R)
        w_lo = sb("w_lo", [P, PART_SLOTS, SLAB_K, COLS], F32R)
        row = sb("row", [P, ROW_SLOTS, D])
        const = sb("const", [P, N_CONST])
        stat = sb("stat", [P, 8])
        junk = sb("junk", [P, COLS], mybir.dt.bfloat16)
        first_half = ExitStack()
        p_tok = sb("p_tok", [P, TT, TT, 256], scope=first_half)
        first_half.close()
        kv_k = sb("kv_k", [P, 2, T])
        kv_v = sb("kv_v", [P, TT, P])
        rest_of_p_tok = sb("rest_of_p_tok", [P, 256])
        minus_half = sb("minus_half", [P, 32])

        core = ExitStack()
        ct = sb("ct", [P, 2, 2, 4, P], scope=core)
        ab = sb("ab", [P, 2, 4, 4, P], scope=core)
        inv = sb("inv", [P, 2, 2, 4, P], scope=core)
        core.close()
        x_hi = [sb("x_hi0", [P, KD, T], F32R)]
        x_lo = [sb("x_lo0", [P, KD, T], F32R)]

        rw = ExitStack()
        x_hi.append(sb("x_hi1", [P, KD, T], F32R, rw))
        x_lo.append(sb("x_lo1", [P, KD, T], F32R, rw))
        rw_r = sb("rw_r", [P, TT, D], scope=rw)
        rw_k = sb("rw_k", [P, TT, D], scope=rw)
        rw_v = sb("rw_v", [P, TT, D], scope=rw)
        rw_gate = sb("rw_gate", [P, TT, D], scope=rw)
        rw_sig = sb("rw_sig", [P, TT, D], scope=rw)
        rw_a = sb("rw_a", [P, TT, D], scope=rw)
        rw_kap = sb("rw_kap", [P, TT, D], scope=rw)
        level_a = sb("level_a", [P, 2, 4, P], scope=rw)
        state = sb("state", [P, 8, P], scope=rw)
        carry = sb("carry", [P, 8], scope=rw)
        bonus = sb("bonus", [P, TT, 16], scope=rw)
        hstat = sb("hstat", [P, 3, TT, 16], scope=rw)
        mu = sb("mu", [P, 6, KD], scope=rw)
        xn_ch = rw_gate[:, :, :].rearrange("p t (k c) -> p (t k) c", c=T)
        dx_ch = xn[:, :, :].rearrange("p t (k c) -> p (t k) c", c=T)
        mix_v = rw_v[:, :, :].rearrange("p t (k c) -> p (t k) c", c=T)
        mix_k = rw_k[:, :, :].rearrange("p t (k c) -> p (t k) c", c=T)
        rhs_sb = rw_sig[:, 1, 0:COLS].rearrange("p (g i c) -> p g i c", g=2, i=2)
        un_sb = rw_sig[:, 1, COLS:D].rearrange("p (g i c) -> p g i c", g=2, i=2)
        x_sb = rw_sig[:, 0, :].rearrange("p (g i c) -> p g i c", g=2, i=4)
        mix_s = rw_sig[:, :, :].rearrange("p t (k c) -> p (t k) c", c=T)
        lora_w1 = rw_a[:, 0, :].rearrange("p (x k c) -> p x k c", x=2, k=KD)
        lora_t = rw_a[:, 1, COLS:D].rearrange("p (x t) -> p x t", x=2)
        rw.close()
        decays = [[ab[:, i, :, :, :].rearrange("p a b c -> p (a b c)")[:, j * COLS:(j + 1) * COLS]
                   for j in range(3)] for i in range(2)]
        ff = ExitStack()
        g_hi = sb("g_hi", [P, KF, T], F32R, ff)
        g_lo = sb("g_lo", [P, KF, T], F32R, ff)
        g_tok = sb("g_tok", [P, 2, TT, COLS], scope=ff)
        silu = sb("silu", [P, TT, COLS], scope=ff)
        bias = sb("bias", [P, 16, T], scope=ff)
        bias_rows = sb("bias_rows", [16, BIAS_N], scope=ff)
        rel = sb("rel", [33, 16], scope=ff)
        picks = sb("picks", [33, BIAS_N], scope=ff)
        ff.close()
        bias_dram = nc.dram_tensor("bias_dram", [16, BIAS_N], F32, kind="Internal").ap()
        sw = ExitStack()
        sq_tok = sb("sq_tok", [P, TT, D], scope=sw)
        sq_ch = sb("sq_ch", [P, KD, T], scope=sw)
        s_sc = sb("s_sc", [P, 2, 2, T], scope=sw)
        s_pr = sb("s_pr", [P, 2, TT, 2, T], scope=sw)
        s_at = sb("s_at", [P, 2, 3, P], scope=sw)
        s_sm = sb("s_sm", [P, 16, 8], scope=sw)
        sinks = sb("sinks", [P, 16], scope=sw)
        q_norm = sb("q_norm", [P, 64], scope=sw)
        k_norm = sb("k_norm", [P, 64], scope=sw)
        k_tmp = sb("k_tmp", [P, TT, 2, 2, 64], scope=sw)
        v_tmp = sb("v_tmp", [P, TT, P], scope=sw)
        k_sq = sb("k_sq", [P, TT, 2, 64], scope=sw)
        sw_stat = sb("sw_stat", [P, 2, 32], scope=sw)
        sw.close()
        late = ExitStack()
        y_hi = sb("y_hi", [P, 2 * KD, T], F32R, late)
        y_lo = sb("y_lo", [P, 2 * KD, T], F32R, late)
        late.close()
        ss = ExitStack()
        z_tok = sb("z_tok", [P, TT, 2 * D], scope=ss)
        xs_tok = sb("xs_tok", [P, TT, 2 * D], scope=ss)
        y_tok = sb("y_tok", [P, TT, 2 * D], scope=ss)
        bc = sb("bc", [P, 8, T], scope=ss)
        conv_in = sb("conv_in", [P, 2, 2, T + 4], scope=ss)
        conv_sum = sb("conv_sum", [P, 2, 2, T], scope=ss)
        cb = sb("cb", [P, 4, 3 * P], scope=ss)
        seg = sb("seg", [P, 2, 2, 3 * P], scope=ss)
        conv_w = sb("conv_w", [P, 24, 4], scope=ss)
        conv_b = sb("conv_b", [P, 24], scope=ss)
        per_head_in = sb("per_head_in", [P, 3, SSM_H], scope=ss)
        dts = sb("dts", [P, 8, TT, SSM_H], scope=ss)
        ss_stat = sb("ss_stat", [P, 2, 8], scope=ss)
        ss.close()
        da = ExitStack()
        q_tok = sb("q_tok", [P, TT, D], scope=da)
        k_tok = sb("k_tok", [P, TT, D], scope=da)
        v_tok = sb("v_tok", [P, TT, D], scope=da)
        gate = sb("gate", [P, TT, D], scope=da)
        rot = sb("rot", [P, TT, D], scope=da)
        q_ch = sb("q_ch", [P, KD, T], scope=da)
        k_ch = sb("k_ch", [P, KD, T], scope=da)
        expo = sb("expo", [P, 2, 2, T], scope=da)
        att = sb("att", [P, 2, TT, T], scope=da)
        att_ch = sb("att_ch", [P, 2, 3, P], scope=da)
        sm = sb("sm", [P, 8 * TT, 8], scope=da)
        lq = sb("lq", [P, 4, 64], scope=da)
        lam = sb("lam", [P, 6], scope=da)
        subln = sb("subln", [P, P], scope=da)
        da_stat = sb("da_stat", [P, 2, 16], scope=da)
        da.close()
        pl = ExitStack()
        p_hi = sb("p_hi", [P, 2, T], F32R, pl)
        p_lo = sb("p_lo", [P, 2, T], F32R, pl)
        p_out = sb("p_out", [P, TT, D], scope=pl)
        sig = sb("sig", [P, TT, D], scope=pl)
        pl.close()

        ld_const, ld_mu, ld_lora, ld_p = sem("ld_const"), sem("ld_mu"), sem("ld_lora"), sem("ld_p")
        ld_bias = sem("ld_bias")
        ld_da, ld_ssm, ld_kv, ld_swa = sem("ld_da"), sem("ld_ssm"), sem("ld_kv"), sem("ld_swa")
        lora_ready_for_load = sem("lora_ready_for_load")
        slab_loaded = [sem("slab_loaded%d" % i) for i in range(RAW_SLOTS)]
        row_loaded = [sem("row_loaded%d" % i) for i in range(ROW_SLOTS)]
        row_used = sem("row_used")
        slab_hi, slab_lo, slab_used = sem("slab_hi"), sem("slab_lo"), sem("slab_used")
        psum_ready = sem("psum_ready")
        bank_free = [sem("bank_free%d" % i) for i in range(BANKS)]
        turned_hi = sem("turned_hi")
        vec_step, act_step, pool_step = sem("vec_step"), sem("act_step"), sem("pool_step")
        stored = sem("stored")
        named = {}

        def event(*name):
            key = "_".join(map(str, name))
            if key not in named:
                named[key] = sem(key)
            return named[key]

        def ready(eng, *name):
            eng.wait_ge(psum_ready, jobs[name] + 1)

        def consumed(eng, *name):
            j = jobs[name]
            eng.wait_ge(bank_free[j % BANKS], j // BANKS + 1)

        def B(*name):
            return bank[jobs[name] % BANKS]

        def frees(ins, *name):
            ins.then_inc(bank_free[jobs[name] % BANKS], 1)

        def slab_released(eng, n):
            kind, what = slabs[n][5]
            if kind == "job":
                eng.wait_ge(psum_ready, jobs[what] + 1)
            else:
                eng.wait_ge(slab_used, what)

        def C(name, part=slice(0, P)):
            lo_, hi_ = CONST_AT[name]
            return const[part, lo_:hi_]

        def over(x, n):
            return x.unsqueeze(1).broadcast_to([P, n, x.shape[1]])

        def level_no(w, g, l):
            return ((2 * w + g // 2) * 7 + l) * 2 + g % 2 + 1

        mixes = (mix_v, mix_k, mix_v, xn_ch)
        ident = C("ident")
        stage_before = dict(zip(STAGES[1:], STAGES))

        def h_done(eng, s):
            if s is None:
                eng.wait_ge(ld_const, 32)
            elif s == "rw":
                consumed(eng, (s, "o", 1), TT - 1)
            elif s in ("ple0", "ple1"):
                eng.wait_ge(event(s, "added"), 2 * TT)
            elif s in ("da", "swa", "ssm"):
                consumed(eng, (s, "out", 1), TT - 1)
            elif s == "final":
                eng.wait_ge(event(s, "normed"), TT)
            elif s.startswith("ffn"):
                consumed(eng, (s, "d", 1), TT - 1)
            elif s == "kv":
                consumed(eng, s, "turn", 3)

        turned_no = {}
        for name in jobs:
            if name[1] in ("turn", "turn_p", "gt") and name[0] != "rw":
                turned_no[name] = len(turned_no) + 1

        block = ctx.enter_context(nc.Block())

        @block.sync
        def _(sp):
            sp.dma_start(h[:, :, :], A["x"][0].rearrange("(t p) d -> p t d", p=P)).then_inc(ld_const, 16)
            sp.dma_start(const[:, :], A["constants"]).then_inc(ld_const, 16)
            nrow = [0]

            def load_rows(upto):
                while nrow[0] < upto:
                    n = nrow[0]
                    if n >= ROW_SLOTS:
                        sp.wait_ge(row_used, n - ROW_SLOTS + 1)
                    sp.dma_start(row[:, n % ROW_SLOTS, :], R[rows[n][1]].partition_broadcast(P)) \
                        .then_inc(row_loaded[n % ROW_SLOTS], 16)
                    nrow[0] += 1

            def load_slabs(lo_, hi_):
                for n in range(lo_, hi_):
                    w, k0, kn, c0, cols, _ = slabs[n]
                    if n >= RAW_SLOTS:
                        sp.wait_ge(slab_lo, n - RAW_SLOTS + 1)
                    sp.dma_start(raw[:, n % RAW_SLOTS, 0:kn, 0:cols],
                                 w[k0 * P:(k0 + kn) * P, c0:c0 + cols].rearrange("(k p) c -> p k c", p=P)) \
                        .then_inc(slab_loaded[n % RAW_SLOTS], 16)

            def load_extras(s):
                if s == "ssm":
                    h_done(sp, stage_before.get(s))
                    sp.dma_start(conv_w[:, :, :], A["ssm_conv_w_2"]).then_inc(ld_ssm, 16)
                    sp.dma_start(conv_b[:, :], A["ssm_conv_b_2"]).then_inc(ld_ssm, 16)
                    for i, n in enumerate(("ssm_dt_bias_2", "ssm_a_log_2", "ssm_d_2")):
                        sp.dma_start(per_head_in[:, i, :], A[n][0].partition_broadcast(P)).then_inc(ld_ssm, 16)
                if s == "kv":
                    h_done(sp, stage_before.get(s))
                    sp.dma_start(rel[0:32, :], A["rel_bias_2"]).then_inc(ld_kv, 16)
                    sp.dma_start(picks[:, :], A["bias_picks"]).then_inc(ld_kv, 16)
                    sp.dma_start(k_norm[:, :], A["k_norm_2"].partition_broadcast(P)).then_inc(ld_kv, 16)
                if s == "swa":
                    h_done(sp, stage_before.get(s))
                    sp.dma_start(sinks[:, :], A["sinks_2"][0].partition_broadcast(P)).then_inc(ld_swa, 16)
                    sp.dma_start(q_norm[:, :], A["q_norm_2"][0].partition_broadcast(P)).then_inc(ld_swa, 16)
                if s == "da":
                    h_done(sp, stage_before.get(s))
                    for i, n in enumerate(("da_lq1", "da_lk1", "da_lq2", "da_lk2")):
                        sp.dma_start(lq[:, i, :], A[n][0].partition_broadcast(P)).then_inc(ld_da, 16)
                    sp.dma_start(subln[:, :], A["da_subln"][0].partition_broadcast(P)).then_inc(ld_da, 16)
                if s == "rw":
                    sp.dma_start(mu[:, :, :], A["rw_mu"]).then_inc(ld_mu, 16)
                    for i, (w1, w2, w0) in enumerate((("rw_w1", "rw_w2", "rw_w0"), ("rw_a1", "rw_a2", "rw_a0"))):
                        sp.dma_start(lora_w1[:, i], A[w1][0].rearrange("(k p) c -> p k c", p=P)).then_inc(ld_lora, 16)
                        sp.dma_start(rw_kap[0:64, i, :], A[w2][0]).then_inc(ld_lora, 16)
                        sp.dma_start(rw_kap[64:65, i, :], A[w0]).then_inc(ld_lora, 16)

            sp.dma_start(p_tok[:, :, :, :], A["p"][:, 0].rearrange("i (t p) c -> p i t c", p=P)).then_inc(ld_p, 16)
            for s in STAGES:
                here = [n for n, (st, _) in enumerate(rows) if st == s]
                mine = [g for g in gemms if g[0] == s]
                load_rows(here[0] + min(len(here), ROW_SLOTS))
                if s == "rw":
                    load_extras(s)
                for g in mine:
                    if g == mine[max(0, len(mine) - 2)]:
                        load_rows(here[-1] + 1)
                    load_slabs(gemms[g][0], gemms[g][1])
                    if g == mine[0] and s != "rw":
                        load_extras(s)
                if not mine:
                    load_rows(here[-1] + 1)
            h_done(sp, STAGES[-1])
            sp.dma_start(out[0].rearrange("(t p) d -> p t d", p=P), h[:, :, :]).then_inc(stored, 16)
            sp.wait_ge(stored, 16)

        @block.gpsimd
        def _(pool):
            O = Order(pool, pool_step)

            def power(s, what, dst, src, n):
                pool.wait_ge(event(s, what + "_mean"), 1)
                pool.tensor_tensor(dst, src, minus_half[:, 0:n], ALU.pow).then_inc(event(s, what + "_rstd"), 1)

            def group_power(s, t, b):
                h8 = slice(8 * b, 8 * b + 8)
                power(s, "group%d%d" % (t, b), hstat[:, 1, t, h8], hstat[:, 2, t, h8], 8)

            O.step(pool.memset(minus_half[:, :], -0.5))
            O.settle()
            for s in STAGES:
                power(s, "norm", stat[:, 6:8], stat[:, 4:6], 2)
                if s == "rw":
                    power(s, "kap", hstat[:, 1, :, :].rearrange("p t h -> p (t h)"),
                          hstat[:, 0, :, :].rearrange("p t h -> p (t h)"), 32)
                    for w in range(TT):
                        for gg in range(2):
                            for l in range(7):
                                for g in (2 * gg, 2 * gg + 1):
                                    if l == 0:
                                        for par in range(2):
                                            consumed(pool, s, "ab", w, g, par)
                                        if (w, gg) != (0, 0):
                                            ready(pool, s, "x", w if gg else w - 1, g - 2 if gg else g + 2, 6)
                                    elif l == 1:
                                        pool.wait_ge(event(s, "inverse_begun"), 4 * w + g + 1)
                                    else:
                                        ready(pool, s, "x", w, g, l - 1)
                                    pool.tensor_tensor(level_a[:, g % 2, :, :], ab[:, g % 2, :, 0, :],
                                                       over(C("levels")[:, l * P:(l + 1) * P], 4), ALU.mult) \
                                        .then_inc(event(s, "level_a"), 1)
                                if w == 1 and l == 3:
                                    for t, b in (((0, 0), (0, 1)), ((1, 0),))[gg]:
                                        group_power(s, t, b)
                    group_power(s, 1, 1)
                if s == "da":
                    power(s, "head", da_stat[:, 1, :], da_stat[:, 0, :], 16)
                if s == "ssm":
                    power(s, "group", ss_stat[:, 1, :], ss_stat[:, 0, :], 8)
                if s == "kv":
                    power(s, "head", sw_stat[:, 1, 0:4], sw_stat[:, 0, 0:4], 4)
                    consumed(pool, s, "bias")
                    pool.dma_start(bias_dram, bias_rows[:, :]).then_inc(ld_bias, 16)
                    pool.wait_ge(ld_bias, 16)
                    pool.dma_start(bias[:, :, :], bass.AP(bias_dram.tensor, 0, [[1, P], [BIAS_N, 16], [1, T]])) \
                        .then_inc(ld_bias, 16)
                if s == "swa":
                    power(s, "head", sw_stat[:, 1, :], sw_stat[:, 0, :], 32)

        @block.scalar
        def _(act):
            O = Order(act, act_step)
            split = [0]

            def hi_parts(name, count=99):
                while split[0] < min(gemms[name][1], gemms[name][0] + count):
                    n = split[0]
                    _, _, kn, _, cols, _ = slabs[n]
                    act.wait_ge(slab_loaded[n % RAW_SLOTS], 16 * (n // RAW_SLOTS + 1))
                    if n >= PART_SLOTS:
                        slab_released(act, n - PART_SLOTS)
                    act.activation(w_hi[:, n % PART_SLOTS, 0:kn, 0:cols], raw[:, n % RAW_SLOTS, 0:kn, 0:cols],
                                   ACT.Copy).then_inc(slab_hi, 1)
                    split[0] += 1

            def squares(s):
                h_done(act, stage_before.get(s))
                for b in range(2):
                    for t in range(TT):
                        O.step(act.activation(junk[:, :], h[:, t, b * COLS:(b + 1) * COLS], ACT.Square,
                                              accum_out=stat[:, 2 * b + t:2 * b + t + 1]))
                        if (b, t) == (1, 1):
                            O.settle()
                            act.sem_inc(event(s, "squares"), 1)
                        O.settle()

            def rstd(s, t):
                if s not in DEFERRED:
                    return 1.0
                if s not in waited_for:
                    act.wait_ge(event(s, "norm_rstd"), 1)
                    waited_for.add(s)
                return stat[:, 6 + t:7 + t]

            waited_for = set()

            def take_hi(*name):
                ready(act, *name)
                i = name[-1]
                hi = {"turn": x_hi[0], "turn_p": p_hi, "gt": g_hi}[name[1]]
                if name[0] == "ssmo":
                    hi = y_hi
                b_ = i if name[1] != "gt" else 2 * name[2] + i
                act.activation(hi[:, 2 * b_:2 * b_ + 2, :], B(*name)[:, :].rearrange("p (k t) -> p k t", k=2),
                               ACT.Copy).then_inc(turned_hi, 1)

            def activations(s, tag=None, n=4):
                for i in range(n):
                    take_hi(tag or s, "turn", i)

            def evacuate(name, dst, func=ACT.Copy):
                for t in range(TT):
                    ready(act, name, t)
                    scale = 1.0 if name[1] == "p" else rstd(name[0], t)
                    frees(act.activation(dst(t), B(name, t)[:, 0:gemms[name][2]], func, scale=scale), name, t)

            def rwkv(s):
                hi_parts((s, "r", 0))
                for i in range(4):
                    ready(act, s, "turn", i)
                    frees(act.activation(xn_ch[:, 2 * i:2 * i + 2, :],
                                         B(s, "turn", i)[:, :].rearrange("p (k t) -> p k t", k=2), ACT.Copy),
                          s, "turn", i)
                def mix_hi(i):
                    act.wait_ge(event(s, "mixed"), i + 1)
                    if i >= 2:
                        ready(act, (s, "rkvg"[i - 2], 1), TT - 1)
                    act.activation(x_hi[i % 2][:, :, :], mixes[i], ACT.Copy) \
                        .then_inc(event(s, "mix_hi"), 1)

                def take(x, b):
                    dst = {"r": rw_r, "k": rw_k, "v": rw_v, "g": rw_gate}[x]
                    evacuate((s, x, b), lambda t: dst[:, t, b * COLS:(b + 1) * COLS],
                             ACT.Silu if x == "g" else ACT.Copy)

                mix_hi(0)
                hi_parts((s, "r", 1))
                mix_hi(1)
                hi_parts((s, "k", 0))
                take("r", 0)
                take("r", 1)
                hi_parts((s, "k", 1))
                take("k", 0)
                hi_parts((s, "v", 0))
                take("k", 1)
                for i, (x, func) in enumerate((("w", ACT.Tanh), ("a", ACT.Copy))):
                    ready(act, s, "lora_in", x)
                    frees(act.activation(lora_t[0:64, i, :], B(s, "lora_in", x)[0:64, 0:T], func), s, "lora_in", x)
                mix_hi(2)
                for i, x in enumerate("wa"):
                    for b in range(2):
                        for t in range(TT):
                            ready(act, s, "lora_out", x, b, t)
                            frees(act.activation((rw_sig, rw_a)[i][:, t, b * COLS:(b + 1) * COLS],
                                                 B(s, "lora_out", x, b, t)[:, :], ACT.Sigmoid),
                                  s, "lora_out", x, b, t)
                hi_parts((s, "v", 1))
                mix_hi(3)
                hi_parts((s, "g", 0))
                take("v", 0)
                take("v", 1)
                hi_parts((s, "g", 1))
                take("g", 0)
                take("g", 1)
                for b in range(2):
                    for w in range(TT):
                        i = 2 * b + w
                        ready(act, s, "cum", b, w)
                        if i >= 2:
                            act.wait_ge(event(s, "decayed"), i - 1)
                        e = decays[i % 2]
                        act.activation(e[0], B(s, "cum", b, w)[:, :], ACT.Exp).then_inc(event(s, "exp_p"), 1)
                        frees(act.activation(e[1], B(s, "cum", b, w)[:, :], ACT.Exp, scale=-1.0), s, "cum", b, w)
                        ready(act, s, "cumx", b, w)
                        frees(act.activation(e[2], B(s, "cumx", b, w)[:, :], ACT.Exp), s, "cumx", b, w)
                ready(act, s, "carry")
                frees(act.activation(carry[:, :], B(s, "carry")[:, 0:8], ACT.Exp), s, "carry")
                for w in range(TT):
                    for gg in range(2):
                        pair = (2 * gg, 2 * gg + 1)
                        for g in pair:
                            for pp in range(2):
                                ready(act, s, "ct", w, g, pp)
                                frees(act.activation(ct[:, g % 2, pp, :, :],
                                                     B(s, "ct", w, g, pp)[:, :].rearrange("p (i c) -> p i c", i=4),
                                                     ACT.Copy), s, "ct", w, g, pp)
                        def four(*name):
                            return B(*name)[:, :].rearrange("p (i c) -> p i c", i=4)

                        for g in pair:
                            ready(act, s, "t0", w, g)
                            frees(act.activation(inv[:, g % 2, 0], four(s, "t0", w, g), ACT.Copy), s, "t0", w, g)
                        for l in range(1, 7):
                            for g in pair:
                                ready(act, s, "x", w, g, l)
                                frees(act.activation(x_sb[:, g % 2], four(s, "x", w, g, l), ACT.Copy),
                                      s, "x", w, g, l)
                            if l < 6:
                                for g in pair:
                                    ready(act, s, "tt", w, g, l)
                                    frees(act.activation(inv[:, g % 2, 1], four(s, "tt", w, g, l), ACT.Copy),
                                          s, "tt", w, g, l)
                        for what, dst, sign in (("rhs", rhs_sb, 1.0), ("u", un_sb, -1.0)):
                            for g in pair:
                                ready(act, s, what, w, g)
                                frees(act.activation(dst[:, g % 2, :, :],
                                                     B(s, what, w, g)[:, 0:2 * P].rearrange("p (i c) -> p i c", i=2),
                                                     ACT.Copy, scale=sign), s, what, w, g)
                        for g in pair:
                            ready(act, s, "y", w, g)
                            frees(act.activation(xn[:, w, g * 2 * P:(g + 1) * 2 * P], B(s, "y", w, g)[:, 0:2 * P],
                                                 ACT.Copy), s, "y", w, g)
                            if w == 0:
                                ready(act, s, "s", w, g)
                                act.wait_ge(event(s, "state_zeroed"), 1)
                                consumed(act, s, "carry")
                                o = B(s, "s", w, g)
                                for pp in range(2):
                                    for par in range(2):
                                        r_, c_ = slice(64 * par, 64 * par + 64), pp * P + 64 * par
                                        ins = act.activation(state[r_, 2 * g + pp, 64 * par:64 * par + 64],
                                                             o[r_, c_:c_ + 64], ACT.Copy,
                                                             scale=carry[r_, 2 * g + pp:2 * g + pp + 1])
                                frees(ins, s, "s", w, g)
                hi_parts((s, "o", 0))
                activations(s, "rwo")
                hi_parts((s, "o", 1))

            for s in STAGES:
                if s not in DEFERRED:
                    squares(s)
                if s == "rw":
                    rwkv(s)
                elif s in ("ple0", "ple1"):
                    hi_parts((s, "p", 0))
                    take_hi(s, "turn_p", 0)
                    hi_parts((s, "p", 1))
                    hi_parts((s, "g", 0), 1)
                    for b in range(2):
                        evacuate((s, "p", b), lambda t: p_out[:, t, b * COLS:(b + 1) * COLS])
                    activations(s)
                    squares(s)
                    for b in range(2):
                        hi_parts((s, "g", b))
                        if b:
                            evacuate((s, "g", 0), lambda t: sig[:, t, 0:COLS], ACT.Sigmoid)
                    evacuate((s, "g", 1), lambda t: sig[:, t, COLS:D], ACT.Sigmoid)
                elif s == "da":
                    hi_parts((s, 0))
                    activations(s)
                    squares(s)
                    dst = [q_tok, q_tok, k_tok, k_tok, v_tok, v_tok, gate, gate]
                    for i in range(8):
                        if i < 7:
                            hi_parts((s, i + 1))
                        if i == 4:
                            act.wait_ge(event(s, "lq_dots"), 1)
                            act.activation(lam[:, 2:4], lam[:, 0:2], ACT.Exp).then_inc(event(s, "lq_exp"), 1)
                        evacuate((s, i), lambda t: dst[i][:, t, (i % 2) * COLS:(i % 2 + 1) * COLS],
                                 ACT.Silu if i >= 6 else ACT.Copy)
                    for i in range(8):
                        ready(act, s, "qk", i)
                        dst_ch = (q_ch if i < 4 else k_ch)[:, 2 * (i % 4):2 * (i % 4) + 2, :]
                        frees(act.activation(dst_ch, B(s, "qk", i)[:, :].rearrange("p (k t) -> p k t", k=2),
                                             ACT.Copy), s, "qk", i)

                    def weigh_values(hd):
                        ready(act, s, "at", hd)
                        frees(act.activation(att_ch[:, hd % 2, :, :],
                                             B(s, "at", hd)[:, 0:3 * P].rearrange("p (i q) -> p i q", i=3),
                                             ACT.Copy), s, "at", hd)
                        ready(act, s, "o", hd)
                        frees(act.activation(xn[:, :, hd * P:(hd + 1) * P],
                                             B(s, "o", hd)[:, 0:T].rearrange("p (t c) -> p t c", t=TT),
                                             ACT.Copy), s, "o", hd)

                    for hd in range(8):
                        for qt in range(TT):
                            u, n = hd * TT + qt, (qt + 1) * P
                            act.wait_ge(event(s, "max"), u + 1)
                            if u >= 2:
                                act.wait_ge(event(s, "att"), u - 1)
                            for c in range(2):
                                frees(act.activation(expo[:, u % 2, c, 0:n], B(s, "s", hd, qt, c)[:, 0:n], ACT.Exp,
                                                     bias=sm[:, u, 2 + c:3 + c], scale=64 ** -0.5,
                                                     accum_out=sm[:, u, 4 + c:5 + c]), s, "s", hd, qt, c)
                        if hd:
                            weigh_values(hd - 1)
                    weigh_values(7)
                    for b in range(2):
                        hi_parts((s, "out", b))
                        if b == 0:
                            activations(s, "dao")
                elif s == "ssm":
                    hi_parts((s, "dt"))
                    activations(s)
                    act.wait_ge(ld_ssm, 16 * 5)
                    act.activation(per_head_in[:, 1, :], per_head_in[:, 1, :], ACT.Exp) \
                        .then_inc(event(s, "a"), 1)
                    act.wait_ge(event(s, "dt_minus_abs"), 1)
                    O.step(act.activation(dts[:, 2], dts[:, 1], ACT.Exp))
                    O.settle()
                    act.activation(dts[:, 3], dts[:, 2], ACT.Ln, bias=1.0).then_inc(event(s, "dt_log"), 1)
                    hi_parts((s, "z", 0))
                    for i in range(4):
                        hi_parts((s, "z", i + 1) if i < 3 else (s, "xb", CONV_ORDER[0]))
                        evacuate((s, "z", i), lambda t: z_tok[:, t, i * COLS:(i + 1) * COLS], ACT.Silu)

                    def conv_out(i, j):
                        m = 2 * i + j
                        n = CONV_ORDER.index(i) * 2 + j
                        act.wait_ge(event(s, "convolved"), n + 1)
                        for c in range(2):
                            tile_ = 4 * i + 2 * j + c
                            dst = bc[:, tile_ - 16, :] if i >= 4 else conv_sum[:, n % 2, c, :]
                            act.activation(dst, conv_sum[:, n % 2, c, :], ACT.Silu,
                                           bias=conv_b[:, tile_:tile_ + 1]).then_inc(event(s, "conv_out"), 1)

                    def take_tokens(i):
                        for j in range(2):
                            ready(act, s, "xt", i, j)
                            c = i * COLS + j * 256
                            frees(act.activation(xs_tok[:, :, c:c + 256],
                                                 B(s, "xt", i, j)[:, :].rearrange("p (t c) -> p t c", t=TT),
                                                 ACT.Copy), s, "xt", i, j)

                    for n, i in enumerate(CONV_ORDER):
                        if n < 5:
                            hi_parts((s, "xb", CONV_ORDER[n + 1]), 1)
                        for j in range(2):
                            ready(act, (s, "xb", i), j)
                            if 2 * n + j >= 2:
                                act.wait_ge(event(s, "convolved"), 2 * n + j - 1)
                            frees(act.activation(conv_in[:, j, :, 3:3 + T],
                                                 B((s, "xb", i), j)[:, :].rearrange("p (c t) -> p c t", c=2),
                                                 ACT.Copy), (s, "xb", i), j)
                            conv_out(i, j)
                        if n < 5:
                            hi_parts((s, "xb", CONV_ORDER[n + 1]))
                        if i < 4:
                            if i:
                                take_tokens(i - 1)
                    take_tokens(3)
                    for u in range(SSM_H // 2 + 2):
                        if u < SSM_H // 2:
                            act.wait_ge(event(s, "seg"), u + 1)
                            act.activation(seg[:, u % 2, :, :], seg[:, u % 2, :, :], ACT.Exp) \
                                .then_inc(event(s, "seg_exp"), 1)
                        if u >= 2:
                            ready(act, s, "y", u - 2)
                            frees(act.activation(y_tok[:, :, (u - 2) * P:(u - 1) * P],
                                                 B(s, "y", u - 2)[:, 0:T].rearrange("p (t c) -> p t c", t=TT),
                                                 ACT.Copy), s, "y", u - 2)
                    hi_parts((s, "out", 0), 2)
                    activations(s, "ssmo", 8)
                    for b in range(2):
                        hi_parts((s, "out", b))
                elif s == "kv":
                    hi_parts((s, "kv"))
                    activations(s)
                    squares(s)
                    ready(act, (s, "kv"), TT - 1)
                    ready(act, s, "vt")
                    frees(act.activation(kv_v[:, :, :], B(s, "vt")[:, 0:2 * P].rearrange("p (t c) -> p t c", t=TT),
                                         ACT.Copy), s, "vt")
                    ready(act, s, "kt")
                    frees(act.activation(kv_k[:, :, :], B(s, "kt")[:, :].rearrange("p (h t) -> p h t", h=2),
                                         ACT.Copy), s, "kt")
                elif s == "swa":
                    hi_parts((s, "q", 0))
                    activations(s)
                    squares(s)
                    for b in range(2):
                        if b == 0:
                            hi_parts((s, "q", 1))
                        evacuate((s, "q", b), lambda t: sq_tok[:, t, b * COLS:(b + 1) * COLS])
                    for i in range(4):
                        ready(act, s, "qt", i)
                        frees(act.activation(sq_ch[:, 2 * i:2 * i + 2, :],
                                             B(s, "qt", i)[:, :].rearrange("p (k t) -> p k t", k=2), ACT.Copy),
                              s, "qt", i)

                    def window_values(pr):
                        for par in range(2):
                            ready(act, s, "at", pr, par)
                            frees(act.activation(s_at[:, par, :, :],
                                                 B(s, "at", pr, par)[:, 0:3 * P].rearrange("p (i q) -> p i q", i=3),
                                                 ACT.Copy), s, "at", pr, par)
                        ready(act, s, "o", pr)
                        frees(act.activation(xn[:, :, pr * P:(pr + 1) * P],
                                             B(s, "o", pr)[:, 0:T].rearrange("p (t c) -> p t c", t=TT),
                                             ACT.Copy), s, "o", pr)

                    for pr in range(8):
                        for qt in range(TT):
                            u, n = pr * TT + qt, (qt + 1) * P
                            act.wait_ge(event(s, "max"), u + 1)
                            if pr >= 2:
                                ready(act, s, "at", pr - 2, 1)
                            for c in range(2):
                                act.activation(s_pr[:, pr % 2, qt, c, 0:n], s_sc[:, u % 2, c, 0:n], ACT.Exp,
                                               bias=s_sm[:, u, 2 + c:3 + c],
                                               accum_out=s_sm[:, u, 4 + c:5 + c]).then_inc(event(s, "exp"), 1)
                            act.activation(s_sm[:, u, 0:2], s_sm[:, u, 0:2], ACT.Exp).then_inc(event(s, "exp"), 1)
                        if pr:
                            window_values(pr - 1)
                    window_values(7)
                    hi_parts((s, "out", 0))
                    activations(s, "swao")
                    hi_parts((s, "out", 1))
                elif s.startswith("ffn"):
                    hi_parts((s, "u", 0))
                    activations(s)
                    squares(s)
                    blocks = ffn_blocks()

                    def gated_hi(b):
                        for i in range(blocks[b][1] // 256):
                            take_hi(s, "gt", b, i)

                    for b, (_, cols) in enumerate(blocks):
                        hi_parts((s, "u", b))
                        hi_parts((s, "v", b))
                        if b:
                            gated_hi(b - 1)
                            act.wait_ge(bank_free[jobs[(s, "v", b - 1), 1] % BANKS],
                                        jobs[(s, "v", b - 1), 1] // BANKS + 1)
                        evacuate((s, "u", b), lambda t: silu[:, t, 0:cols], ACT.Silu)
                    hi_parts((s, "d", 0), 2)
                    gated_hi(len(blocks) - 1)
                    for b in range(2):
                        hi_parts((s, "d", b))

        @block.vector
        def _(dve):
            O = Order(dve, vec_step)
            split = [0]

            def lo_parts(name, count=99):
                while split[0] < min(gemms[name][1], gemms[name][0] + count):
                    n = split[0]
                    _, _, kn, _, cols, _ = slabs[n]
                    dve.wait_ge(slab_hi, n + 1)
                    hi = w_hi[:, n % PART_SLOTS, 0:kn, 0:cols]
                    dve.tensor_tensor(w_lo[:, n % PART_SLOTS, 0:kn, 0:cols], raw[:, n % RAW_SLOTS, 0:kn, 0:cols],
                                      hi.bitcast(F32), ALU.subtract).then_inc(slab_lo, 1)
                    split[0] += 1

            def use_row(s, r):
                n = row_at[(s, r)]
                dve.wait_ge(row_loaded[n % ROW_SLOTS], 16 * (n // ROW_SLOTS + 1))
                return row[:, n % ROW_SLOTS, :]

            def release_row():
                O.settle()
                dve.sem_inc(row_used, 1)

            def signal(ins, sem_, value):
                ins.then_inc(sem_, 1)
                O.last = (sem_, value)

            def frees_bank(ins, *name):
                frees(ins, *name)
                O.last = (bank_free[jobs[name] % BANKS], jobs[name] // BANKS + 1)

            def mean_square(s):
                dve.wait_ge(event(s, "squares"), 1)
                O.step(dve.tensor_tensor(stat[:, 4:6], stat[:, 0:2], stat[:, 2:4], ALU.add))
                O.settle()
                signal(dve.tensor_scalar(stat[:, 4:6], stat[:, 4:6], 1.0 / D, 1e-6, ALU.mult, ALU.add),
                       event(s, "norm_mean"), 1)

            def norm(s, dst, done):
                mean_square(s)
                gain = use_row(s, ROW_SOURCES[s][0])
                dve.wait_ge(event(s, "norm_rstd"), 1)
                for t in range(TT):
                    signal(dve.scalar_tensor_tensor(out=dst[:, t, :], in0=h[:, t, :],
                                                    scalar=stat[:, 6 + t:7 + t], in1=gain, op0=ALU.mult,
                                                    op1=ALU.mult), event(s, done), t + 1)
                release_row()

            def rstd(s, t):
                if s not in waited_for:
                    dve.wait_ge(event(s, "norm_rstd"), 1)
                    waited_for.add(s)
                return stat[:, 6 + t:7 + t]

            waited_for = set()

            def gain_next(s, b):
                after = STAGES[STAGES.index(s) + 1] if s in STAGES[:-1] else STAGES[0] if s is None else None
                if after not in DEFERRED:
                    return
                gain = use_row(after, ROW_SOURCES[after][0])
                O.settle()
                c = slice(b * COLS, (b + 1) * COLS)
                for t in range(TT):
                    signal(dve.tensor_tensor(xn[:, t, c], h[:, t, c], gain[:, c], ALU.mult),
                           event(after, "scaled"), 2 * b + t + 1)
                if b:
                    release_row()
                elif s not in (None, "final", "kv") and not s.startswith("ple"):
                    lo_parts(next(g for g in gemms if g[0] == after), 1)

            def take_lo(*name):
                dve.wait_ge(turned_hi, turned_no[name])
                i = name[-1]
                hi, lo_ = {"turn": (x_hi[0], x_lo[0]), "turn_p": (p_hi, p_lo), "gt": (g_hi, g_lo)}[name[1]]
                if name[0] == "ssmo":
                    hi, lo_ = y_hi, y_lo
                b_ = i if name[1] != "gt" else 2 * name[2] + i
                frees_bank(dve.tensor_tensor(lo_[:, 2 * b_:2 * b_ + 2, :],
                                             B(*name)[:, :].rearrange("p (k t) -> p k t", k=2),
                                             hi[:, 2 * b_:2 * b_ + 2, :].bitcast(F32), ALU.subtract), *name)

            def activations(s, tag=None, n=4):
                for i in range(n):
                    take_lo(tag or s, "turn", i)

            def add_to_h(name, c0, scale=1.0):
                cols = gemms[name][2]
                for t in range(TT):
                    ready(dve, name, t)
                    dst = h[:, t, c0:c0 + cols]
                    frees_bank(dve.scalar_tensor_tensor(out=dst, in0=B(name, t)[:, 0:cols], scalar=scale, in1=dst,
                                                        op0=ALU.mult, op1=ALU.add), name, t)

            def rwkv(s):
                norm(s, xn, "scaled")
                O.step(dve.memset(lora_t[64:65, :, :], 1.0))
                signal(dve.memset(state[:, :, :], 0.0), event(s, "state_zeroed"), 1)
                for i in range(4):
                    consumed(dve, s, "turn", i)
                dve.wait_ge(ld_mu, 16)
                O.step(dve.tensor_scalar(dx_ch[:, :, 0:1], xn_ch[:, :, 0:1], -1.0, None, ALU.mult))
                O.step(dve.tensor_tensor(dx_ch[:, :, 1:T], xn_ch[:, :, 0:T - 1], xn_ch[:, :, 1:T], ALU.subtract))
                O.settle()

                def mix(dst, m, sem_, value):
                    for k in range(KD):
                        ins = dve.scalar_tensor_tensor(out=dst[:, k, :], in0=dx_ch[:, k, :], scalar=mu[:, m, k:k + 1],
                                                       in1=xn_ch[:, k, :], op0=ALU.mult, op1=ALU.add)
                        if k < KD - 1:
                            O.step(ins)
                    signal(ins, sem_, value)

                def mix_projection(i):
                    mix(mixes[i], i, event(s, "mixed"), i + 1)

                def mix_lo(i):
                    dve.wait_ge(event(s, "mix_hi"), i + 1)
                    signal(dve.tensor_tensor(x_lo[i % 2][:, :, :], mixes[i],
                                             x_hi[i % 2][:, :, :].bitcast(F32), ALU.subtract),
                           event(s, "mix_lo"), i + 1)

                mix_projection(0)
                lo_parts((s, "r", 0))
                mix_lo(0)
                mix_projection(1)
                lo_parts((s, "r", 1))
                mix_lo(1)
                mix(mix_s, 4, event(s, "lora_mixed"), 1)
                lo_parts((s, "k", 0))
                mix(mix_v, 5, event(s, "lora_mixed"), 2)
                lo_parts((s, "k", 1))
                lo_parts((s, "v", 0), 1)
                ready(dve, s, "lora_in", "a")
                mix_projection(2)
                mix_lo(2)
                lo_parts((s, "v", 0))
                mix_projection(3)
                lo_parts((s, "v", 1))
                mix_lo(3)

                heads32 = [P, 2 * 16, 64]

                def by_head(x):
                    return x[:, :, :].rearrange("p t (h c) -> p (t h) c", c=64)

                def per_head(x):
                    return x.rearrange("p t h -> p (t h)").unsqueeze(2).broadcast_to(heads32)

                def row_op(dst, a_, r_, op):
                    for t in range(TT):
                        O.step(dve.tensor_tensor(dst[:, t, :], a_[:, t, :], r_, op))

                for b in range(2):
                    consumed(dve, (s, "k", b), TT - 1)
                ready(dve, s, "lora_out", "a", 1, 1)
                row_op(rw_kap, rw_k, use_row(s, "rw_k_k"), ALU.mult)
                release_row()
                O.step(dve.tensor_tensor(xn[:, :, :], rw_kap[:, :, :], rw_kap[:, :, :], ALU.mult))
                O.settle()
                O.step(dve.tensor_reduce(hstat[:, 0, :, :].rearrange("p t h -> p (t h)"), by_head(xn), X, ALU.add))
                O.settle()
                signal(dve.tensor_scalar(hstat[:, 0, :, :], hstat[:, 0, :, :], 1e-24, None, ALU.max),
                       event(s, "kap_mean"), 1)
                lo_parts((s, "g", 0))
                consumed(dve, s, "lora_out", "a", 1, 1)
                ka = use_row(s, "rw_k_a")
                for t in range(TT):
                    O.step(dve.scalar_tensor_tensor(out=xn[:, t, :], in0=rw_a[:, t, :], scalar=-1.0, in1=ka,
                                                    op0=ALU.add, op1=ALU.mult))
                release_row()
                for t in range(TT):
                    O.step(dve.scalar_tensor_tensor(out=rw_k[:, t, :], in0=xn[:, t, :], scalar=1.0, in1=rw_k[:, t, :],
                                                    op0=ALU.add, op1=ALU.mult))
                O.settle()
                dve.wait_ge(event(s, "kap_rstd"), 1)
                O.step(dve.tensor_tensor(by_head(rw_kap), by_head(rw_kap), per_head(hstat[:, 1, :, :]), ALU.mult))
                lo_parts((s, "g", 1))
                O.step(dve.tensor_tensor(xn[:, :, :], rw_r[:, :, :], rw_k[:, :, :], ALU.mult))
                O.settle()
                row_op(xn, xn, use_row(s, "rw_r_k"), ALU.mult)
                release_row()
                O.step(dve.tensor_reduce(bonus[:, :, :].rearrange("p t h -> p (t h)"), by_head(xn), X, ALU.add))
                O.step(dve.tensor_tensor(rw_a[:, :, :], rw_kap[:, :, :], rw_a[:, :, :], ALU.mult))
                O.settle()
                for b in range(2):
                    for w in range(TT):
                        consumed(dve, s, "cumx", b, w)
                        e, c = decays[(2 * b + w) % 2], slice(b * COLS, (b + 1) * COLS)
                        for x, i in ((rw_r, 0), (rw_k, 1), (rw_a, 1)):
                            O.step(dve.tensor_tensor(x[:, w, c], x[:, w, c], e[i], ALU.mult))
                        signal(dve.tensor_tensor(rw_kap[:, w, c], rw_kap[:, w, c], e[2], ALU.mult),
                               event(s, "decayed"), 2 * b + w + 1)

                O.settle()
                def finish_heads(t, b, part):
                    c, h8 = slice(b * COLS, (b + 1) * COLS), slice(8 * b, 8 * b + 8)
                    mean, rstd_, var, bon = hstat[:, 0, t, h8], hstat[:, 1, t, h8], hstat[:, 2, t, h8], bonus[:, t, h8]
                    y, tmp = xn[:, t, c], rw_r[:, t, c]

                    def by_h(x):
                        return x.rearrange("p (h c) -> p h c", c=64)

                    def each(x):
                        return x.unsqueeze(2).broadcast_to([P, 8, 64])

                    def then(ins):
                        O.step(ins)
                        O.settle()

                    if part == 0:
                        for g in (2 * b, 2 * b + 1):
                            consumed(dve, s, "y", t, g)
                        then(dve.tensor_reduce(mean, by_h(y), X, ALU.add))
                        then(dve.tensor_scalar(mean, mean, 1.0 / 64, None, ALU.mult))
                        then(dve.tensor_tensor(by_h(y), by_h(y), each(mean), ALU.subtract))
                    elif part == 1:
                        then(dve.tensor_tensor(tmp, y, y, ALU.mult))
                        then(dve.tensor_reduce(var, by_h(tmp), X, ALU.add))
                        signal(dve.tensor_scalar(var, var, 1.0 / 64, 64e-5, ALU.mult, ALU.add),
                               event(s, "group%d%d_mean" % (t, b)), 1)
                    elif part == 2:
                        then(dve.tensor_tensor(by_h(tmp), by_h(rw_v[:, t, c]), each(bon), ALU.mult))
                    elif part == 3:
                        then(dve.tensor_tensor(tmp, tmp, use_row(s, "rw_ln_b")[:, c], ALU.add))
                    elif part == 4:
                        dve.wait_ge(event(s, "group%d%d_rstd" % (t, b)), 1)
                        then(dve.tensor_tensor(by_h(y), by_h(y), each(rstd_), ALU.mult))
                        then(dve.tensor_tensor(y, y, use_row(s, "rw_ln_w")[:, c], ALU.mult))
                    else:
                        then(dve.tensor_tensor(y, y, tmp, ALU.add))
                        signal(dve.tensor_tensor(y, y, rw_gate[:, t, c], ALU.mult),
                               event(s, "gated"), 2 * t + b + 1)

                for w in range(TT):
                    for gg in range(2):
                        pair = (2 * gg, 2 * gg + 1)
                        for g in pair:
                            a_, t_ = ab[:, g % 2], inv[:, g % 2]
                            for par in range(2):
                                it = slice(2 * par, 2 * par + 2)
                                for what, j in (("ab", 0), ("ak", 2)):
                                    ready(dve, s, what, w, g, par)
                                    frees_bank(dve.tensor_tensor(
                                        a_[:, it, j:j + 2, :].rearrange("p i j c -> p i (j c)"),
                                        B(s, what, w, g, par)[:, :].rearrange("p (i c) -> p i c", i=2),
                                        over(C("strict_incl"), 2), ALU.mult), s, what, w, g, par)
                            dve.wait_ge(event(s, "level_a"), level_no(w, g, 0))
                            signal(dve.tensor_tensor(t_[:, 1], over(ident, 4), level_a[:, g % 2, :, :], ALU.subtract),
                                   event(s, "inverse_begun"), 4 * w + g + 1)
                        for l in range(1, 7):
                            for g in pair:
                                ready(dve, s, "tx", w, g, l)
                                t_ = inv[:, g % 2, l // 6]
                                frees_bank(dve.tensor_tensor(
                                    t_, t_, B(s, "tx", w, g, l)[:, :].rearrange("p (i c) -> p i c", i=4),
                                    ALU.subtract), s, "tx", w, g, l)
                            if w:
                                for t, b in (((0, 0), (0, 1)), ((1, 0),))[gg]:
                                    finish_heads(t, b, l - 1)
                lo_parts((s, "o", 0))
                for part in range(6):
                    finish_heads(1, 1, part)
                release_row()
                release_row()
                activations(s, "rwo")
                lo_parts((s, "o", 1))
                for b in range(2):
                    add_to_h((s, "o", b), b * COLS)
                    gain_next(s, b)

            h_done(dve, None)
            for b in range(2):
                gain_next(None, b)
            for s in STAGES:
                if s == "rw":
                    rwkv(s)
                elif s in ("ple0", "ple1"):
                    lo_parts((s, "p", 0))
                    take_lo(s, "turn_p", 0)
                    lo_parts((s, "p", 1))
                    activations(s)
                    mean_square(s)
                    lo_parts((s, "g", 0))
                    for b in range(2):
                        lo_parts((s, "g", b))
                        for t in range(TT):
                            c = slice(b * COLS, (b + 1) * COLS)
                            consumed(dve, (s, "g", b), t)
                            O.step(dve.tensor_tensor(sig[:, t, c], sig[:, t, c], p_out[:, t, c], ALU.mult))
                            O.settle()
                            signal(dve.tensor_tensor(h[:, t, c], h[:, t, c], sig[:, t, c], ALU.add),
                                   event(s, "added"), b * TT + t + 1)
                        gain_next(s, b)
                elif s == "final":
                    norm(s, h, "normed")
                    for b in range(2):
                        gain_next(s, b)
                elif s == "da":
                    lo_parts((s, 0))
                    activations(s)
                    mean_square(s)
                    for i in range(5):
                        lo_parts((s, i))
                    dve.wait_ge(ld_da, 16 * 5)
                    O.step(dve.tensor_tensor(lq[:, 0:4:2, :], lq[:, 0:4:2, :], lq[:, 1:4:2, :], ALU.mult))
                    O.settle()
                    signal(dve.tensor_reduce(lam[:, 0:2], lq[:, 0:4:2, :], X, ALU.add), event(s, "lq_dots"), 1)
                    O.step(dve.tensor_scalar(subln[:, :], subln[:, :], 1.0 - LAMBDA_INIT, None, ALU.mult))
                    dve.wait_ge(event(s, "lq_exp"), 1)
                    O.step(dve.tensor_tensor(lam[:, 4:5], lam[:, 2:3], lam[:, 3:4], ALU.subtract))
                    O.settle()
                    O.step(dve.tensor_scalar(lam[:, 5:6], lam[:, 4:5], -1.0, -LAMBDA_INIT, ALU.mult, ALU.add))

                    for i, x in enumerate((q_tok, k_tok)):
                        for b in range(2):
                            consumed(dve, (s, 2 * i + b), TT - 1)
                        for t in range(TT):
                            xv = x[:, t, :].rearrange("p (g c) -> p g c", c=64)
                            rv = rot[:, t, :].rearrange("p (g c) -> p g c", c=64)
                            cos = C("cos")[:, t * 64:(t + 1) * 64].unsqueeze(1).broadcast_to([P, 16, 64])
                            sin = C("sin")[:, t * 64:(t + 1) * 64].unsqueeze(1).broadcast_to([P, 16, 64])
                            O.step(dve.tensor_tensor(rv[:, :, 0:32], xv[:, :, 32:64], sin[:, :, 0:32], ALU.mult))
                            O.step(dve.tensor_tensor(rv[:, :, 32:64], xv[:, :, 0:32], sin[:, :, 32:64], ALU.mult))
                            O.settle()
                            O.step(dve.tensor_tensor(xv, xv, cos, ALU.mult))
                            O.settle()
                            signal(dve.tensor_tensor(x[:, t, :], x[:, t, :], rot[:, t, :], ALU.add),
                                   event(s, "roped"), 2 * i + t + 1)
                        lo_parts((s, 5 + i))
                    lo_parts((s, 7))

                    for u in range(8 * TT):
                        hd, qt = u // TT, u % TT
                        n = (qt + 1) * P
                        for c in range(2):
                            ready(dve, s, "s", hd, qt, c)
                            O.step(dve.tensor_reduce(sm[:, u, c:c + 1], B(s, "s", hd, qt, c)[:, 0:n], X, ALU.max))
                        O.settle()
                        signal(dve.tensor_scalar(sm[:, u, 2:4], sm[:, u, 0:2], -(64 ** -0.5), None, ALU.mult),
                               event(s, "max"), u + 1)
                        for c in range(2):
                            consumed(dve, s, "s", hd, qt, c)
                        O.step(dve.reciprocal(sm[:, u, 6:8], sm[:, u, 4:6]))
                        O.settle()
                        O.step(dve.tensor_scalar(sm[:, u, 7:8], sm[:, u, 7:8], lam[:, 5:6], None, ALU.mult))
                        O.settle()
                        O.step(dve.tensor_scalar(expo[:, u % 2, 1, 0:n], expo[:, u % 2, 1, 0:n], sm[:, u, 7:8],
                                                 None, ALU.mult))
                        O.settle()
                        if hd >= 2 and qt == 0:
                            ready(dve, s, "at", hd - 2)
                        signal(dve.scalar_tensor_tensor(out=att[:, hd % 2, qt, 0:n], in0=expo[:, u % 2, 0, 0:n],
                                                        scalar=sm[:, u, 6:7], in1=expo[:, u % 2, 1, 0:n],
                                                        op0=ALU.mult, op1=ALU.add), event(s, "att"), u + 1)

                    consumed(dve, s, "o", 7)
                    O.step(dve.tensor_tensor(rot[:, :, :], xn[:, :, :], xn[:, :, :], ALU.mult))
                    O.settle()
                    heads = rot[:, :, :].rearrange("p t (h c) -> p (t h) c", c=P)
                    O.step(dve.tensor_reduce(da_stat[:, 0, :], heads, X, ALU.add))
                    O.settle()
                    signal(dve.tensor_scalar(da_stat[:, 0, :], da_stat[:, 0, :], 1.0 / P, 1e-5, ALU.mult, ALU.add),
                           event(s, "head_mean"), 1)
                    consumed(dve, (s, 7), TT - 1)
                    gv = gate[:, :, :].rearrange("p t (h c) -> p (t h) c", c=P)
                    xv = xn[:, :, :].rearrange("p t (h c) -> p (t h) c", c=P)
                    O.step(dve.tensor_tensor(gv, gv, subln[:, :].unsqueeze(1).broadcast_to([P, 16, P]), ALU.mult))
                    O.settle()
                    O.step(dve.tensor_tensor(xn[:, :, :], xn[:, :, :], gate[:, :, :], ALU.mult))
                    dve.wait_ge(event(s, "head_rstd"), 1)
                    O.settle()
                    signal(dve.tensor_tensor(xv, xv, da_stat[:, 1, :].unsqueeze(2).broadcast_to([P, 16, P]),
                                             ALU.mult), event(s, "heads"), 1)
                    lo_parts((s, "out", 0))
                    activations(s, "dao")
                    lo_parts((s, "out", 1))
                    for b in range(2):
                        add_to_h((s, "out", b), b * COLS)
                        gain_next(s, b)
                elif s == "ssm":
                    norm(s, xn, "scaled")
                    lo_parts((s, "dt"))
                    activations(s)
                    signal(dve.memset(conv_in[:, :, :, 0:3], 0.0), event(s, "padded"), 1)
                    raw_, nabs, ex, lg, one_, dt, dta, nacum = (dts[:, i] for i in range(8))
                    dve.wait_ge(ld_ssm, 16 * 5)
                    for t in range(TT):
                        ready(dve, (s, "dt"), t)
                        frees_bank(dve.tensor_tensor(raw_[:, t, :], B((s, "dt"), t)[:, 0:SSM_H],
                                                     per_head_in[:, 0, :], ALU.add), (s, "dt"), t)
                    O.settle()
                    O.step(dve.tensor_scalar(lg, raw_, -1.0, None, ALU.mult))
                    O.settle()
                    signal(dve.tensor_tensor(nabs, raw_, lg, ALU.min), event(s, "dt_minus_abs"), 1)
                    dve.wait_ge(event(s, "dt_log"), 1)
                    O.step(dve.tensor_scalar(one_, ex, 1.0, None, ALU.add))
                    O.settle()
                    O.step(dve.scalar_tensor_tensor(out=ex, in0=one_, scalar=-1.0, in1=ex, op0=ALU.add,
                                                    op1=ALU.subtract))
                    O.step(dve.reciprocal(one_, one_))
                    O.settle()
                    O.step(dve.tensor_tensor(ex, ex, one_, ALU.mult))
                    O.settle()
                    O.step(dve.tensor_tensor(lg, lg, ex, ALU.subtract))
                    O.settle()
                    O.step(dve.scalar_tensor_tensor(out=dt, in0=raw_, scalar=0.0, in1=lg, op0=ALU.max,
                                                    op1=ALU.add))
                    O.settle()
                    dve.wait_ge(event(s, "a"), 1)
                    for t in range(TT):
                        signal(dve.scalar_tensor_tensor(out=dta[:, t, :], in0=dt[:, t, :], scalar=-1.0,
                                                        in1=per_head_in[:, 1, :], op0=ALU.mult, op1=ALU.mult),
                               event(s, "dta"), t + 1)
                    lo_parts((s, "z", 0))
                    ready(dve, s, "acum")
                    frees_bank(dve.tensor_scalar(nacum, B(s, "acum")[:, 0:TT * SSM_H].rearrange(
                        "p (t h) -> p t h", t=TT), -1.0, None, ALU.mult), s, "acum")
                    for i in range(1, 4):
                        lo_parts((s, "z", i))
                    lo_parts((s, "xb", CONV_ORDER[0]))
                    for n, i in enumerate(CONV_ORDER):
                        if n < 5:
                            lo_parts((s, "xb", CONV_ORDER[n + 1]), 1)
                        for j in range(2):
                            consumed(dve, (s, "xb", i), j)
                            m = 2 * n + j
                            if m >= 2:
                                dve.wait_ge(event(s, "conv_out"), 2 * (m - 1))
                                prev = CONV_ORDER[n - 1]
                                if prev < 4:
                                    ready(dve, s, "xt", prev, j)
                            for k in range(4):
                                if k:
                                    O.settle()
                                for c in range(2):
                                    tile_ = 4 * i + 2 * j + c
                                    src, dst = conv_in[:, j, c, k:k + T], conv_sum[:, j, c, :]
                                    w_ = conv_w[:, tile_, k:k + 1]
                                    if k == 0:
                                        ins = dve.tensor_scalar(dst, src, w_, None, ALU.mult)
                                    else:
                                        ins = dve.scalar_tensor_tensor(out=dst, in0=src, scalar=w_, in1=dst,
                                                                       op0=ALU.mult, op1=ALU.add)
                                    if k < 3 or c == 0:
                                        O.step(ins)
                            signal(ins, event(s, "convolved"), m + 1)
                        if n < 5:
                            lo_parts((s, "xb", CONV_ORDER[n + 1]))
                    for g in range(4):
                        ready(dve, s, "cb", g)
                        O.step(dve.tensor_tensor(cb[:, g, 0:T], B(s, "cb", g)[:, 0:T], C("tri"), ALU.mult))
                        frees_bank(dve.tensor_tensor(cb[:, g, T:T + P], B(s, "cb", g)[:, T:T + P],
                                                     C("tri")[:, 0:P], ALU.mult), s, "cb", g)
                    for j in range(2):
                        consumed(dve, s, "xt", 3, j)

                    def ssm_heads(x):
                        return x[:, :, :].rearrange("p t (h c) -> p (t h) c", c=64)

                    def ssm_per_head(x):
                        return x.rearrange("p t h -> p (t h)").unsqueeze(2).broadcast_to([P, TT * SSM_H, 64])

                    signal(dve.tensor_tensor(ssm_heads(y_tok), ssm_heads(xs_tok), ssm_per_head(dt), ALU.mult),
                           event(s, "x_dt"), 1)
                    for u in range(SSM_H // 2 + 1):
                        if u < SSM_H // 2:
                            ready(dve, s, "seg", u)
                            if u >= 2:
                                ready(dve, s, "y", u - 2)
                            o = B(s, "seg", u)
                            for c in range(2):
                                hd = 2 * u + c
                                for lo2, n2, t in ((0, T, 0), (T, P, 1)):
                                    ins = dve.tensor_scalar(seg[:, u % 2, c, lo2:lo2 + n2],
                                                            o[:, c * T + t * P:c * T + t * P + n2],
                                                            nacum[:, t, hd:hd + 1], 0.0, ALU.add, ALU.min)
                                    if (c, t) != (1, 1):
                                        O.step(ins)
                            frees_bank(ins, s, "seg", u)
                            O.settle()
                            dve.sem_inc(event(s, "seg"), 1)
                        if u:
                            v = u - 1
                            dve.wait_ge(event(s, "seg_exp"), v + 1)
                            signal(dve.tensor_tensor(seg[:, v % 2, :, :], seg[:, v % 2, :, :],
                                                     over(cb[:, v // 4, :], 2), ALU.mult),
                                   event(s, "weights"), v + 1)
                    lo_parts((s, "out", 0), 2)
                    O.step(dve.tensor_tensor(xs_tok[:, 0, :].rearrange("p (h c) -> p h c", c=64),
                                             xs_tok[:, 0, :].rearrange("p (h c) -> p h c", c=64),
                                             per_head_in[:, 2, :].unsqueeze(2).broadcast_to([P, SSM_H, 64]), ALU.mult))
                    O.step(dve.tensor_tensor(xs_tok[:, 1, :].rearrange("p (h c) -> p h c", c=64),
                                             xs_tok[:, 1, :].rearrange("p (h c) -> p h c", c=64),
                                             per_head_in[:, 2, :].unsqueeze(2).broadcast_to([P, SSM_H, 64]), ALU.mult))
                    O.settle()
                    consumed(dve, s, "y", SSM_H // 2 - 1)
                    O.step(dve.tensor_tensor(y_tok[:, :, :], y_tok[:, :, :], xs_tok[:, :, :], ALU.add))
                    O.settle()
                    O.step(dve.tensor_tensor(y_tok[:, :, :], y_tok[:, :, :], z_tok[:, :, :], ALU.mult))
                    O.settle()
                    O.step(dve.tensor_tensor(xs_tok[:, :, :], y_tok[:, :, :], y_tok[:, :, :], ALU.mult))
                    O.settle()
                    O.step(dve.tensor_reduce(ss_stat[:, 0, :], xs_tok[:, :, :].rearrange("p t (g c) -> p (t g) c", c=COLS),
                                             X, ALU.add))
                    O.settle()
                    signal(dve.tensor_scalar(ss_stat[:, 0, :], ss_stat[:, 0, :], 1.0 / COLS, 1e-6, ALU.mult, ALU.add),
                           event(s, "group_mean"), 1)
                    dve.wait_ge(event(s, "group_rstd"), 1)
                    for b in range(2):
                        gain = use_row(s, "gate_norm%d" % b)
                        for t in range(TT):
                            for g in range(2):
                                c = slice((2 * b + g) * COLS, (2 * b + g + 1) * COLS)
                                n = t * 4 + 2 * b + g
                                signal(dve.scalar_tensor_tensor(out=y_tok[:, t, c], in0=y_tok[:, t, c],
                                                                scalar=ss_stat[:, 1, n:n + 1],
                                                                in1=gain[:, g * COLS:(g + 1) * COLS],
                                                                op0=ALU.mult, op1=ALU.mult),
                                       event(s, "y_scaled"), 4 * b + 2 * t + g + 1)
                        release_row()
                    activations(s, "ssmo", 8)
                    for b in range(2):
                        lo_parts((s, "out", b))
                    for b in range(2):
                        add_to_h((s, "out", b), b * COLS)
                        gain_next(s, b)
                elif s == "kv":
                    h_done(dve, stage_before.get(s))
                    signal(dve.memset(rel[32:33, :], 1.0), event(s, "rel_one"), 1)
                    ready(dve, s, "bias")
                    frees_bank(dve.tensor_copy(bias_rows[:, :], B(s, "bias")[0:16, 0:BIAS_N]), s, "bias")
                    lo_parts((s, "kv"))
                    activations(s)
                    mean_square(s)
                    for b in range(2):
                        gain_next(s, b)
                    dve.wait_ge(ld_kv, 16 * 3)
                    for t in range(TT):
                        ready(dve, (s, "kv"), t)
                        O.step(dve.tensor_scalar(k_tmp[:, t, :, 0, :],
                                                 B((s, "kv"), t)[:, 0:P].rearrange("p (h c) -> p h c", c=64),
                                                 rstd(s, t), None, ALU.mult))
                        frees_bank(dve.tensor_scalar(v_tmp[:, t, :], B((s, "kv"), t)[:, P:2 * P], rstd(s, t),
                                                     None, ALU.mult), (s, "kv"), t)
                    O.settle()
                    for t in range(TT):
                        O.step(dve.tensor_tensor(k_sq[:, t, :, :], k_tmp[:, t, :, 0, :], k_tmp[:, t, :, 0, :],
                                                 ALU.mult))
                    O.settle()
                    O.step(dve.tensor_reduce(sw_stat[:, 0, 0:4], k_sq[:, :, :, :].rearrange("p t h c -> p (t h) c"),
                                             X, ALU.add))
                    O.settle()
                    signal(dve.tensor_scalar(sw_stat[:, 0, 0:4], sw_stat[:, 0, 0:4], 1.0 / 64, 1e-6, ALU.mult,
                                             ALU.add), event(s, "head_mean"), 1)
                    dve.wait_ge(event(s, "head_rstd"), 1)
                    for t in range(TT):
                        for g in range(2):
                            O.step(dve.scalar_tensor_tensor(out=k_tmp[:, t, g, 0, :], in0=k_tmp[:, t, g, 0, :],
                                                            scalar=sw_stat[:, 1, 2 * t + g:2 * t + g + 1],
                                                            in1=k_norm[:, :], op0=ALU.mult, op1=ALU.mult))
                    O.settle()
                    signal(dve.tensor_copy(k_tmp[:, :, :, 1, :].rearrange("p t h c -> p (t h) c"),
                                           k_tmp[:, :, :, 0, :].rearrange("p t h c -> p (t h) c")),
                           event(s, "keys"), 1)
                elif s == "swa":
                    lo_parts((s, "q", 0))
                    activations(s)
                    mean_square(s)
                    lo_parts((s, "q", 1))
                    for b in range(2):
                        consumed(dve, (s, "q", b), TT - 1)
                    dve.wait_ge(ld_swa, 32)

                    def sw_heads(x):
                        return x[:, :, :].rearrange("p t (h c) -> p (t h) c", c=64)

                    O.step(dve.tensor_tensor(xn[:, :, :], sq_tok[:, :, :], sq_tok[:, :, :], ALU.mult))
                    O.settle()
                    O.step(dve.tensor_reduce(sw_stat[:, 0, :], sw_heads(xn), X, ALU.add))
                    O.settle()
                    signal(dve.tensor_scalar(sw_stat[:, 0, :], sw_stat[:, 0, :], 1.0 / 64, 1e-6, ALU.mult, ALU.add),
                           event(s, "head_mean"), 1)
                    O.step(dve.tensor_tensor(sw_heads(sq_tok), sw_heads(sq_tok), over(q_norm[:, :], 32), ALU.mult))
                    dve.wait_ge(event(s, "head_rstd"), 1)
                    O.settle()
                    signal(dve.tensor_tensor(sw_heads(sq_tok), sw_heads(sq_tok),
                                             sw_stat[:, 1, :].unsqueeze(2).broadcast_to([P, 32, 64]), ALU.mult),
                           event(s, "queries"), 1)
                    dve.wait_ge(ld_bias, 32)
                    for u in range(8 * TT):
                        pr, qt = u // TT, u % TT
                        n = (qt + 1) * P
                        if u >= 2:
                            dve.wait_ge(event(s, "exp"), 3 * (u - 1))
                        for c in range(2):
                            ready(dve, s, "s", pr, qt, c)
                            frees_bank(dve.scalar_tensor_tensor(
                                out=s_sc[:, u % 2, c, 0:n], in0=B(s, "s", pr, qt, c)[:, 0:n], scalar=64 ** -0.5,
                                in1=bias[:, 2 * pr + c, 0:n], op0=ALU.mult, op1=ALU.add), s, "s", pr, qt, c)
                        O.settle()
                        m_, sink = s_sm[:, u, 6:8], sinks[:, 2 * pr:2 * pr + 2]
                        O.step(dve.tensor_reduce(m_, s_sc[:, u % 2, :, 0:n], X, ALU.max))
                        O.settle()
                        O.step(dve.tensor_tensor(m_, m_, sink, ALU.max))
                        O.settle()
                        O.step(dve.tensor_scalar(s_sm[:, u, 2:4], m_, -1.0, None, ALU.mult))
                        signal(dve.tensor_tensor(s_sm[:, u, 0:2], sink, m_, ALU.subtract), event(s, "max"), u + 1)
                        dve.wait_ge(event(s, "exp"), 3 * (u + 1))
                        O.step(dve.tensor_tensor(s_sm[:, u, 4:6], s_sm[:, u, 4:6], s_sm[:, u, 0:2], ALU.add))
                        O.settle()
                        O.step(dve.reciprocal(s_sm[:, u, 6:8], s_sm[:, u, 4:6]))
                        O.settle()
                        for c in range(2):
                            v = s_pr[:, pr % 2, qt, c, 0:n]
                            signal(dve.tensor_scalar(v, v, s_sm[:, u, 6 + c:7 + c], None, ALU.mult),
                                   event(s, "att"), 2 * u + c + 1)
                    lo_parts((s, "out", 0))
                    activations(s, "swao")
                    lo_parts((s, "out", 1))
                    for b in range(2):
                        add_to_h((s, "out", b), b * COLS)
                        gain_next(s, b)
                elif s.startswith("ffn"):
                    lo_parts((s, "u", 0))
                    activations(s)
                    mean_square(s)
                    blocks = ffn_blocks()

                    def gated(b):
                        if b >= 2:
                            ready(dve, s, "gt", b - 2, blocks[b - 2][1] // 256 - 1)
                        for t in range(TT):
                            consumed(dve, (s, "u", b), t)
                            ready(dve, (s, "v", b), t)
                            cols = blocks[b][1]
                            frees_bank(dve.scalar_tensor_tensor(
                                out=g_tok[:, b % 2, t, 0:cols], in0=B((s, "v", b), t)[:, 0:cols],
                                scalar=rstd(s, t), in1=silu[:, t, 0:cols], op0=ALU.mult, op1=ALU.mult),
                                (s, "v", b), t)

                    def gated_lo(b):
                        for i in range(blocks[b][1] // 256):
                            take_lo(s, "gt", b, i)

                    for b in range(len(blocks)):
                        lo_parts((s, "u", b))
                        if b:
                            gated(b - 1)
                        lo_parts((s, "v", b))
                        if b:
                            gated_lo(b - 1)
                    lo_parts((s, "d", 0), 2)
                    gated(len(blocks) - 1)
                    gated_lo(len(blocks) - 1)
                    for b in range(2):
                        lo_parts((s, "d", b))
                    for b in range(2):
                        add_to_h((s, "d", b), b * COLS, 0.5)
                        gain_next(s, b)

        @block.tensor
        def _(pe):
            nth = [0]

            def begin(*name):
                assert jobs[name] == nth[0], (name, jobs[name], nth[0])
                nth[0] += 1
                if jobs[name] >= BANKS:
                    pe.wait_ge(bank_free[jobs[name] % BANKS], jobs[name] // BANKS)
                return B(*name)

            def end(ins):
                ins.then_inc(psum_ready, 1)

            def gemm(name, hi, lo_, need=None):
                first, last, cols = gemms[name]
                outs = [begin(name, t) for t in range(TT)]
                k_end = slabs[last - 1][1] + slabs[last - 1][2]
                for n in range(first, last):
                    _, k0, kn, _, _, release = slabs[n]
                    pe.wait_ge(slab_hi, n + 1)
                    pe.wait_ge(slab_lo, n + 1)
                    if need:
                        need(k0, kn)
                    for t in range(TT):
                        for k in range(k0, k0 + kn):
                            a_hi, a_lo = hi[:, k, t * P:(t + 1) * P], lo_[:, k, t * P:(t + 1) * P]
                            b_hi = w_hi[:, n % PART_SLOTS, k - k0, 0:cols]
                            b_lo = w_lo[:, n % PART_SLOTS, k - k0, 0:cols]
                            pe.matmul(outs[t][:, 0:cols], a_hi, b_hi, start=(k == 0), stop=False)
                            pe.matmul(outs[t][:, 0:cols], a_lo, b_hi, start=False, stop=False)
                            mm = pe.matmul(outs[t][:, 0:cols], a_hi, b_lo, start=False, stop=(k == k_end - 1))
                        if n == last - 1:
                            end(mm)
                    if n < last - 1:
                        mm.then_inc(slab_used, 1)

            def gemm_by_channel(name, hi, lo_, need):
                first, last, _ = gemms[name]
                for n in range(first, last):
                    pe.wait_ge(slab_hi, n + 1)
                    pe.wait_ge(slab_lo, n + 1)
                need(0, KD)
                for j in range(2):
                    o = begin(name, j)
                    for c in range(2):
                        dst = o[:, c * T:(c + 1) * T]
                        cols = slice((2 * j + c) * P, (2 * j + c + 1) * P)
                        for k in range(KD):
                            n = (first + k // SLAB_K) % PART_SLOTS
                            a, b = w_hi[:, n, k % SLAB_K, cols], w_lo[:, n, k % SLAB_K, cols]
                            pe.matmul(dst, a, hi[:, k, :], start=(k == 0), stop=False)
                            pe.matmul(dst, a, lo_[:, k, :], start=False, stop=False)
                            mm = pe.matmul(dst, b, hi[:, k, :], start=False, stop=(k == KD - 1))
                    end(mm)

            def turn(name, src, k0, nk=2):
                o = begin(*name)
                for k in range(nk):
                    for t in range(TT):
                        c = (k0 + k) * P
                        mm = pe.transpose(o[:, (k * TT + t) * P:(k * TT + t + 1) * P], src[:, t, c:c + P], ident)
                end(mm)

            def turn_activations(s, tag=None, wait=None):
                if wait:
                    wait()
                for i in range(4):
                    if wait is None and i % 2 == 0:
                        pe.wait_ge(event(s, "scaled"), 2 * (i // 2 + 1) if s in DEFERRED else TT)
                    turn((tag or s, "turn", i), xn, 2 * i)

            def turned(tag):
                def need(k0, kn):
                    for i in range(k0 // 2, (k0 + kn + 1) // 2):
                        consumed(pe, tag, "turn", i)
                return need

            def low_rank(s):
                pe.wait_ge(ld_lora, 16 * 6)
                for i, x in enumerate("wa"):
                    pe.wait_ge(event(s, "lora_mixed"), i + 1)
                    o = begin(s, "lora_in", x)
                    for k in range(KD):
                        mm = pe.matmul(o[0:64, 0:T], lora_w1[:, i, k, :], (mix_s, mix_v)[i][:, k, :],
                                       start=(k == 0), stop=(k == KD - 1))
                    end(mm)
                for i, x in enumerate("wa"):
                    consumed(pe, s, "lora_in", x)
                    for b in range(2):
                        for t in range(TT):
                            o = begin(s, "lora_out", x, b, t)
                            end(pe.matmul(o[:, :], lora_t[0:65, i, t * P:(t + 1) * P],
                                          rw_kap[0:65, i, b * COLS:(b + 1) * COLS], start=True, stop=True))

            def rwkv(s):
                turn_activations(s)
                for i, x in enumerate("rkvg"):
                    pe.wait_ge(event(s, "mix_lo"), i + 1)
                    for b in range(2):
                        gemm((s, x, b), x_hi[i % 2], x_lo[i % 2])
                    if x == "k":
                        low_rank(s)
                consumed(pe, s, "lora_out", "w", 1, 1)
                for b in range(2):
                    for w in range(TT):
                        for what in ("cum", "cumx"):
                            o = begin(s, what, b, w)
                            end(pe.matmul(o[:, :], C(what), rw_sig[:, w, b * COLS:(b + 1) * COLS],
                                          start=True, stop=True))
                o = begin(s, "carry")
                for pr in range(8):
                    for w in range(TT):
                        mm = pe.matmul(o[:, pr:pr + 1], rw_sig[:, w, pr * P:(pr + 1) * P], C("ends")[:, w:w + 1],
                                       start=(w == 0), stop=(w == 1))
                end(mm)

                def turn_four(name, src):
                    o = begin(s, *name)
                    for it in range(4):
                        mm = pe.transpose(o[:, it * P:(it + 1) * P], src[:, it, :], ident)
                    end(mm)

                for w in range(TT):
                    for gg in range(2):
                        pair = (2 * gg, 2 * gg + 1)
                        for g in pair:
                            pe.wait_ge(event(s, "decayed"), 4 if g >= 2 or w else 2)
                            for pp in range(2):
                                o = begin(s, "ct", w, g, pp)
                                c = (2 * g + pp) * P
                                for i, x in enumerate((rw_kap, rw_r, rw_a, rw_k)):
                                    mm = pe.transpose(o[:, i * P:(i + 1) * P], x[:, w, c:c + P], ident)
                                end(mm)
                            for par in range(2):
                                r_ = slice(64 * par, 64 * par + 64)
                                for what, l_ in (("ab", 2), ("ak", 3)):
                                    o = begin(s, what, w, g, par)
                                    for pp in range(2):
                                        consumed(pe, s, "ct", w, g, pp)
                                        mm = pe.matmul(o[:, pp * T:(pp + 1) * T], ct[r_, g % 2, pp, l_, :],
                                                       ct[r_, g % 2, pp, 0:2, :].rearrange("p i c -> p (i c)"),
                                                       start=True, stop=True)
                                    end(mm)
                            pe.wait_ge(event(s, "inverse_begun"), 4 * w + g + 1)
                            turn_four(("t0", w, g), inv[:, g % 2, 1])
                        for l in range(1, 7):
                            for g in pair:
                                if l == 1:
                                    consumed(pe, s, "t0", w, g)
                                else:
                                    consumed(pe, s, "tx", w, g, l - 1)
                                pe.wait_ge(event(s, "level_a"), level_no(w, g, l))
                                o = begin(s, "x", w, g, l)
                                for it in range(4):
                                    mm = pe.matmul(o[:, it * P:(it + 1) * P], level_a[:, g % 2, it, :],
                                                   inv[:, g % 2, 0, it, :], start=True, stop=True)
                                end(mm)
                            for g in pair:
                                x_, tt_ = x_sb[:, g % 2], inv[:, g % 2, 1]
                                consumed(pe, s, "x", w, g, l)
                                if l > 1:
                                    consumed(pe, s, "tt", w, g, l - 1)
                                o = begin(s, "tx", w, g, l)
                                for it in range(4):
                                    a_, b_ = (tt_[:, it, :], x_[:, it, :]) if l < 6 else (x_[:, it, :], tt_[:, it, :])
                                    mm = pe.matmul(o[:, it * P:(it + 1) * P], a_, b_, start=True, stop=True)
                                end(mm)
                            if l < 6:
                                for g in pair:
                                    consumed(pe, s, "tx", w, g, l)
                                    turn_four(("tt", w, g, l), inv[:, g % 2, 0])
                        for g in pair:
                            if w:
                                consumed(pe, s, "s", 0, g)
                            o = begin(s, "rhs", w, g)
                            for pp in range(2):
                                pr = 2 * g + pp
                                if w:
                                    pe.matmul(o[:, pp * P:(pp + 1) * P], ct[:, g % 2, pp, 0, :], state[:, pr, :],
                                              start=True, stop=False)
                                for par in range(2):
                                    c = 64 * par
                                    mm = pe.matmul(o[:, pp * P + c:pp * P + c + 64], ab[:, g % 2, 2 * par + pp, 2, :],
                                                   rw_v[:, w, pr * P + c:pr * P + c + 64], start=(w == 0),
                                                   stop=(w == 0 or par == 1))
                            end(mm)
                        for g in pair:
                            consumed(pe, s, "rhs", w, g)
                            consumed(pe, s, "tx", w, g, 6)
                            o = begin(s, "u", w, g)
                            for pp in range(2):
                                for par in range(2):
                                    c = 64 * par
                                    mm = pe.matmul(o[:, pp * P + c:pp * P + c + 64], inv[:, g % 2, 1, 2 * par + pp, :],
                                                   rhs_sb[:, g % 2, pp, c:c + 64], start=True, stop=True)
                            end(mm)
                        for g in pair:
                            consumed(pe, s, "u", w, g)
                            o = begin(s, "y", w, g)
                            for pp in range(2):
                                pr = 2 * g + pp
                                if w:
                                    pe.matmul(o[:, pp * P:(pp + 1) * P], ct[:, g % 2, pp, 1, :], state[:, pr, :],
                                              start=True, stop=False)
                                for par in range(2):
                                    c = 64 * par
                                    dst = o[:, pp * P + c:pp * P + c + 64]
                                    pe.matmul(dst, ab[:, g % 2, 2 * par + pp, 3, :],
                                              rw_v[:, w, pr * P + c:pr * P + c + 64], start=(w == 0), stop=False)
                                    mm = pe.matmul(dst, ab[:, g % 2, 2 * par + pp, 1, :],
                                                   un_sb[:, g % 2, pp, c:c + 64], start=False,
                                                   stop=(w == 0 or par == 1))
                            end(mm)
                            if w == 0:
                                o = begin(s, "s", w, g)
                                for pp in range(2):
                                    c = slice((2 * g + pp) * P, (2 * g + pp + 1) * P)
                                    pe.matmul(o[:, pp * P:(pp + 1) * P], rw_k[:, 0, c], rw_v[:, 0, c],
                                              start=True, stop=False)
                                    mm = pe.matmul(o[:, pp * P:(pp + 1) * P], rw_a[:, 0, c], un_sb[:, g % 2, pp, :],
                                                   start=False, stop=True)
                                end(mm)
                for i in range(4):
                    pe.wait_ge(event(s, "gated"), 3 + i // 2)
                    turn(("rwo", "turn", i), xn, 2 * i)
                for b in range(2):
                    gemm((s, "o", b), x_hi[0], x_lo[0], turned("rwo"))

            pe.wait_ge(ld_const, 32)
            for s in STAGES:
                if s == "rw":
                    rwkv(s)
                elif s in ("ple0", "ple1"):
                    i = int(s[-1])
                    pe.wait_ge(ld_p, 16)
                    turn((s, "turn_p", 0), p_tok[:, i], 0)
                    consumed(pe, s, "turn_p", 0)
                    for b in range(2):
                        gemm((s, "p", b), p_hi, p_lo)
                    turn_activations(s)
                    for b in range(2):
                        gemm((s, "g", b), x_hi[0], x_lo[0], turned(s))
                elif s == "da":
                    turn_activations(s)
                    for i in range(8):
                        gemm((s, i), x_hi[0], x_lo[0], turned(s))
                    for i in range(8):
                        pe.wait_ge(event(s, "roped"), 2 * (i // 4) + TT)
                        turn((s, "qk", i), q_tok if i < 4 else k_tok, 2 * (i % 4))
                    consumed(pe, s, "qk", 7)

                    def weigh_values(hd):
                        pe.wait_ge(event(s, "att"), 2 * (hd + 1))
                        o = begin(s, "at", hd)
                        for i, (qt, kt) in enumerate(((0, 0), (1, 0), (1, 1))):
                            mm = pe.transpose(o[:, i * P:(i + 1) * P], att[:, hd % 2, qt, kt * P:(kt + 1) * P], ident)
                        end(mm)
                        consumed(pe, s, "at", hd)
                        o = begin(s, "o", hd)
                        v = [v_tok[:, kt, hd * P:(hd + 1) * P] for kt in range(2)]
                        a = att_ch[:, hd % 2]
                        pe.matmul(o[:, 0:P], a[:, 0, :], v[0], start=True, stop=True)
                        pe.matmul(o[:, P:2 * P], a[:, 1, :], v[0], start=True, stop=False)
                        end(pe.matmul(o[:, P:2 * P], a[:, 2, :], v[1], start=False, stop=True))

                    for hd in range(8):
                        for qt in range(TT):
                            for c in range(2):
                                o = begin(s, "s", hd, qt, c)
                                rows_ = slice(64 * c, 64 * c + 64)
                                pe.matmul(o[:, 0:(qt + 1) * P], q_ch[rows_, hd, qt * P:(qt + 1) * P],
                                          k_ch[rows_, hd, 0:(qt + 1) * P], start=True, stop=False)
                                end(pe.matmul(o[:, qt * P:(qt + 1) * P], ident, C("causal"), start=False, stop=True))
                        if hd:
                            weigh_values(hd - 1)
                    weigh_values(7)
                    turn_activations(s, "dao", lambda: pe.wait_ge(event(s, "heads"), 1))
                    for b in range(2):
                        gemm((s, "out", b), x_hi[0], x_lo[0], turned("dao"))
                elif s == "ssm":
                    turn_activations(s)
                    gemm((s, "dt"), x_hi[0], x_lo[0], turned(s))
                    dta = dts[:, 6]
                    pe.wait_ge(event(s, "dta"), TT)
                    o = begin(s, "acum")
                    tri, ones = C("tri")[:, 0:P], C("tri")[:, P:2 * P]
                    pe.matmul(o[:, 0:SSM_H], tri, dta[:, 0, :], start=True, stop=True)
                    pe.matmul(o[:, SSM_H:2 * SSM_H], ones, dta[:, 0, :], start=True, stop=False)
                    end(pe.matmul(o[:, SSM_H:2 * SSM_H], tri, dta[:, 1, :], start=False, stop=True))
                    for i in range(4):
                        gemm((s, "z", i), x_hi[0], x_lo[0])

                    def turn_conv(i):
                        n = CONV_ORDER.index(i)
                        for j in range(2):
                            pe.wait_ge(event(s, "conv_out"), 2 * (2 * n + j + 1))
                            o = begin(s, "xt", i, j)
                            for t in range(TT):
                                for c in range(2):
                                    m = (2 * t + c) * P
                                    mm = pe.transpose(o[:, m:m + P], conv_sum[:, j, c, t * P:(t + 1) * P], ident)
                            end(mm)

                    before = None
                    for i in CONV_ORDER:
                        gemm_by_channel((s, "xb", i), x_hi[0], x_lo[0], turned(s))
                        if before is not None and before < 4:
                            turn_conv(before)
                        before = i
                    turn_conv(before)
                    for g in range(4):
                        o = begin(s, "cb", g)
                        pe.matmul(o[:, 0:T], bc[:, g, 0:P], bc[:, 4 + g, :], start=True, stop=True)
                        end(pe.matmul(o[:, T:T + P], bc[:, g, P:T], bc[:, 4 + g, P:T], start=True, stop=True))
                    for u in range(SSM_H // 2 + 2):
                        if u < SSM_H // 2:
                            o = begin(s, "seg", u)
                            for c in range(2):
                                hd = 2 * u + c
                                col = [dta[:, t, hd:hd + 1].broadcast_to([P, P]) for t in range(TT)]
                                pe.matmul(o[:, c * T:(c + 1) * T], col[0], C("tri"), start=True, stop=False)
                                mm = pe.matmul(o[:, c * T + P:(c + 1) * T], col[1], tri, start=False, stop=True)
                            end(mm)
                        if u >= 2:
                            v = u - 2
                            pe.wait_ge(event(s, "x_dt"), 1)
                            pe.wait_ge(event(s, "weights"), v + 1)
                            o = begin(s, "y", v)
                            for c in range(2):
                                x_ = slice((2 * v + c) * 64, (2 * v + c + 1) * 64)
                                w_ = seg[:, v % 2, c, :]
                                pe.matmul(o[:, c * 64:c * 64 + 64], w_[:, 0:P], y_tok[:, 0, x_], start=True, stop=True)
                                dst = o[:, P + c * 64:P + c * 64 + 64]
                                pe.matmul(dst, w_[:, P:T], y_tok[:, 0, x_], start=True, stop=False)
                                mm = pe.matmul(dst, w_[:, T:T + P], y_tok[:, 1, x_], start=False, stop=True)
                            end(mm)
                    for i in range(8):
                        pe.wait_ge(event(s, "y_scaled"), 4 * (i // 4 + 1))
                        turn(("ssmo", "turn", i), y_tok, 2 * i)
                    for b in range(2):
                        gemm((s, "out", b), y_hi, y_lo, turned("ssmo"))
                elif s == "kv":
                    pe.wait_ge(ld_kv, 16 * 3)
                    pe.wait_ge(event(s, "rel_one"), 1)
                    o = begin(s, "bias")
                    end(pe.matmul(o[0:16, 0:BIAS_N], rel[:, :], picks[:, :], start=True, stop=True))
                    turn_activations(s)
                    gemm((s, "kv"), x_hi[0], x_lo[0], turned(s))
                    for t in range(TT):
                        consumed(pe, (s, "kv"), t)
                    o = begin(s, "vt")
                    for t in range(TT):
                        m = (1 - t) * P
                        mm = pe.matmul(o[:, m:m + P], C("flip"), v_tmp[:, t, :], start=True, stop=True)
                    end(mm)
                    pe.wait_ge(event(s, "keys"), 1)
                    o = begin(s, "kt")
                    for g in range(2):
                        for t in range(TT):
                            m = (g * TT + 1 - t) * P
                            mm = pe.matmul(o[:, m:m + P], k_tmp[:, t, g, :, :].rearrange("p a c -> p (a c)"),
                                           C("flip"), start=True, stop=True)
                    end(mm)
                elif s == "swa":
                    turn_activations(s)
                    for b in range(2):
                        gemm((s, "q", b), x_hi[0], x_lo[0], turned(s))
                    pe.wait_ge(event(s, "queries"), 1)
                    for i in range(4):
                        turn((s, "qt", i), sq_tok, 2 * i)
                    consumed(pe, s, "qt", 3)
                    consumed(pe, "kv", "kt")

                    def window_values(pr):
                        pe.wait_ge(event(s, "att"), 4 * (pr + 1))
                        for par in range(2):
                            o = begin(s, "at", pr, par)
                            for i, (qt, kt) in enumerate(((0, 0), (1, 0), (1, 1))):
                                mm = pe.transpose(o[:, i * P:(i + 1) * P],
                                                  s_pr[:, pr % 2, qt, par, kt * P:(kt + 1) * P], ident)
                            end(mm)
                        o = begin(s, "o", pr)
                        for par in range(2):
                            consumed(pe, s, "at", pr, par)
                            g = pr // 4
                            v = [kv_v[:, kt, 64 * g:64 * g + 64] for kt in range(2)]
                            c = 64 * par
                            pe.matmul(o[:, c:c + 64], s_at[:, par, 0, :], v[1], start=True, stop=True)
                            pe.matmul(o[:, P + c:P + c + 64], s_at[:, par, 1, :], v[0], start=True, stop=False)
                            mm = pe.matmul(o[:, P + c:P + c + 64], s_at[:, par, 2, :], v[1], start=False, stop=True)
                        end(mm)

                    for pr in range(8):
                        for qt in range(TT):
                            for par in range(2):
                                o = begin(s, "s", pr, qt, par)
                                r_ = slice(64 * par, 64 * par + 64)
                                end(pe.matmul(o[:, 0:(qt + 1) * P], sq_ch[r_, pr, qt * P:(qt + 1) * P],
                                              kv_k[r_, pr // 4, (1 - qt) * P:T], start=True, stop=True))
                        if pr:
                            window_values(pr - 1)
                    window_values(7)
                    turn_activations(s, "swao", lambda: consumed(pe, s, "o", 7))
                    for b in range(2):
                        gemm((s, "out", b), x_hi[0], x_lo[0], turned("swao"))
                elif s.startswith("ffn"):
                    turn_activations(s)
                    blocks = ffn_blocks()

                    def turn_gated(b):
                        for t in range(TT):
                            consumed(pe, (s, "v", b), t)
                        for i in range(blocks[b][1] // 256):
                            turn((s, "gt", b, i), g_tok[:, b % 2], 2 * i)

                    for b in range(len(blocks)):
                        gemm((s, "u", b), x_hi[0], x_lo[0], turned(s))
                        if b:
                            turn_gated(b - 1)
                        gemm((s, "v", b), x_hi[0], x_lo[0])
                    turn_gated(len(blocks) - 1)

                    def down(k0, kn):
                        b = min(k0 // 4, len(blocks) - 1)
                        consumed(pe, s, "gt", b, blocks[b][1] // 256 - 1)

                    for b in range(2):
                        gemm((s, "d", b), g_hi, g_lo, down)


_INS = ['x', 'p', 'rw_norm', 'rw_mu', 'rw_w_in', 'rw_w0', 'rw_w1', 'rw_w2', 'rw_a0', 'rw_a1', 'rw_a2', 'rw_k_k',
        'rw_k_a', 'rw_r_k', 'rw_ln_w', 'rw_ln_b', 'rw_w_out', 'da_norm', 'da_w_in', 'da_lq1', 'da_lk1', 'da_lq2',
        'da_lk2', 'da_subln', 'da_w_out', 'pe_norm', 'pe_w_gate', 'pe_w_proj', 'final_norm', 'ffn_norm_2',
        'ffn_w1_2', 'ffn_w3_2', 'ffn_w2_2', 'ssm_norm_2', 'ssm_w_in_2', 'ssm_conv_w_2', 'ssm_conv_b_2',
        'ssm_dt_bias_2', 'ssm_a_log_2', 'ssm_d_2', 'ssm_gate_norm_2', 'ssm_w_out_2', 'kv_norm_2', 'w_kv_2',
        'k_norm_2', 'attn_norm_2', 'w_q_2', 'q_norm_2', 'sinks_2', 'w_o_2', 'rel_bias_2']
_OUTS = [((1, T, D), 'float32')]


def kernel(**inputs):
    import numpy as _np
    import concourse.bacc as _bacc
    from concourse import mybir as _mybir
    from concourse.bass_utils import run_bass_kernel_spmd as _run

    nc = _bacc.Bacc("TRN2", target_bir_lowering=False, num_devices=1)
    arrays, args = {}, {}
    made = {"constants": constants, "bias_picks": bias_picks}
    for name in _INS + list(made):
        a = made[name]() if name in made else _np.asarray(inputs[name])
        if name == "ssm_conv_w_2":
            a = a.reshape(4, 24, P).transpose(2, 1, 0)
        if name == "ssm_conv_b_2":
            a = a.reshape(24, P).T
        if name == "rw_mu":
            a = a.reshape(6, KD, P).transpose(2, 0, 1)
        a = _np.ascontiguousarray(a)
        arrays[f"in_{name}_dram"] = a
        args[name] = nc.dram_tensor(f"in_{name}_dram", a.shape, _mybir.dt.from_np(a.dtype), kind="ExternalInput").ap()
    shape, dtype = _OUTS[0]
    out = nc.dram_tensor("out_0_dram", shape, _mybir.dt.from_np(_np.dtype(dtype)), kind="ExternalOutput").ap()
    program(nc, args, out)
    r = _run(nc, [arrays], core_ids=[0])
    return r.results[0]["out_0_dram"]
```

```python
from contextlib import ExitStack
import math

import numpy as np
import concourse.bass as bass
from concourse import mybir

F32 = mybir.dt.float32
F32R = mybir.dt.float32r
ALU = mybir.AluOpType
ACT = mybir.ActivationFunctionType
X = mybir.AxisListType.X

P = 128
T = 256
TT = T // P
D = 1024
KD = D // P
FF = 2816
KF = FF // P
COLS = 512
SLAB_K = 4
BANKS = 8
RAW_SLOTS, PART_SLOTS = 3, 3
ROW_SLOTS = 2
DECAY = math.exp(-0.5)
NEG = -1.0e30
LAMBDA_INIT = 0.8 - 0.6 * math.exp(-0.3)

SSM_H = 32
CONV_ORDER = (4, 5, 0, 1, 2, 3)
BIAS_N = 3 * P

DEFERRED = ("ple0", "ple1", "da", "ffn0", "ffn1", "ffn2", "ffn3", "kv", "swa")

STAGES = ["rw", "ple0", "da", "ple1", "final", "ffn0", "ssm", "ffn1", "kv", "ffn2", "swa", "ffn3"]


def column_blocks(n):
    return [(c, min(COLS, n - c)) for c in range(0, n, COLS)]


CONST_COLS = [
    ("ident", P),
    ("flip", P),
    ("strict_incl", 2 * P),
    ("levels", 7 * P),
    ("cum", P),
    ("cumx", P),
    ("ends", 2),
    ("causal", P),
    ("cos", TT * 64), ("sin", TT * 64),
    ("tri", 2 * P),
]
CONST_AT, N_CONST = {}, 0
for _name, _n in CONST_COLS:
    CONST_AT[_name] = (N_CONST, N_CONST + _n)
    N_CONST += _n


def constants():
    f = np.float32
    a, b = np.arange(P)[:, None], np.arange(P)[None, :]
    levels = []
    for l in range(7):
        m = 1 << l
        levels.append(((a // (2 * m) == b // (2 * m)) & ((a // m) % 2 == 1) & ((b // m) % 2 == 0)).T)
    half = 64 // 2
    inv_freq = 1.0 / (10000.0 ** (np.arange(0, 64, 2, dtype=f) / f(64)))
    ang = np.arange(T, dtype=f)[:, None] * inv_freq[None, :].astype(f)
    ang = np.concatenate([ang, ang], 1)
    sign = np.concatenate([-np.ones(half), np.ones(half)])[None, :]

    def tiles(x):
        return x.reshape(TT, P, 64).transpose(1, 0, 2).reshape(P, TT * 64)

    parts = {
        "ident": a == b, "flip": a + b == P - 1, "strict_incl": np.concatenate([a < b, a <= b], 1),
        "levels": np.concatenate(levels, 1),
        "cum": -DECAY * ((a <= b) * 1.0 - (a < 64)), "cumx": -DECAY * ((a < b) * 1.0 - (a < 64)),
        "ends": np.concatenate([-DECAY * (a >= 64), -DECAY * (a < 64)], 1),
        "causal": np.where(b > a, NEG, 0.0),
        "cos": tiles(np.cos(ang)), "sin": tiles(np.sin(ang) * sign),
        "tri": np.concatenate([a <= b, np.ones((P, P))], 1),
    }
    return np.ascontiguousarray(np.concatenate([parts[n].astype(f) for n, _ in CONST_COLS], 1))


def bias_picks():
    f = np.float32
    dist = np.arange(BIAS_N) - 127
    n = np.maximum(dist, 0)
    large = 16 + (np.log(np.maximum(n, 1).astype(f) / f(16)) / f(math.log(128 / 16)) * f(16)).astype(np.int32)
    bucket = np.where(n < 16, n, np.minimum(large, 31))
    inside = (dist >= 0) & (dist < 128)
    picks = np.zeros((33, BIAS_N), f)
    picks[bucket, np.arange(BIAS_N)] = inside
    picks[32] = np.where(inside, 0.0, NEG)
    return picks


class Order:

    def __init__(self, eng, sem):
        self.eng, self.sem, self.n = eng, sem, 0
        self.last = None

    def step(self, ins):
        ins.then_inc(self.sem, 1)
        self.n += 1
        self.last = (self.sem, self.n)

    def settle(self):
        if self.last:
            self.eng.wait_ge(*self.last)


class Plan:

    def __init__(self):
        self.jobs = {}
        self.slabs = []
        self.gemms = {}
        self.used = 0

    def job(self, *name):
        assert name not in self.jobs, name
        self.jobs[name] = len(self.jobs)

    def gemm_by_channel(self, name, w, c0, between):
        first = len(self.slabs)
        for j in range(2):
            self.slabs.append((w, 0, KD, c0 + j * COLS // 2, COLS // 2, ("job", (name, j))))
            self.job(name, j)
            between(j)
        self.gemms[name] = (first, len(self.slabs), COLS)

    def gemm(self, name, w, k_tiles, c0, cols):
        first = len(self.slabs)
        for k0 in range(0, k_tiles, SLAB_K):
            kn = min(SLAB_K, k_tiles - k0)
            last = k0 + kn == k_tiles
            if not last:
                self.used += 1
            release = ("job", (name, TT - 1)) if last else ("used", self.used)
            self.slabs.append((w, k0, kn, c0, cols, release))
        self.gemms[name] = (first, len(self.slabs), cols)
        for t in range(TT):
            self.job(name, t)


def ffn_blocks():
    return column_blocks(FF)


def build_plan(W):
    p = Plan()

    def turned(tag, n=4):
        for i in range(n):
            p.job(tag, "turn", i)

    for s in STAGES:
        if s == "rw":
            turned(s)
            for i, x in enumerate("rkvg"):
                for b in range(2):
                    p.gemm((s, x, b), W["rw_w_in"], KD, i * D + b * COLS, COLS)
                if x == "k":
                    for y in "wa":
                        p.job(s, "lora_in", y)
                    for y in "wa":
                        for b in range(2):
                            for t in range(TT):
                                p.job(s, "lora_out", y, b, t)
            for b in range(2):
                for w in range(2):
                    p.job(s, "cum", b, w)
                    p.job(s, "cumx", b, w)
            p.job(s, "carry")
            for w in range(2):
                for gg in range(2):
                    for g in (2 * gg, 2 * gg + 1):
                        for pp in range(2):
                            p.job(s, "ct", w, g, pp)
                        for par in range(2):
                            p.job(s, "ab", w, g, par)
                            p.job(s, "ak", w, g, par)
                        p.job(s, "t0", w, g)
                    for l in range(1, 7):
                        for g in (2 * gg, 2 * gg + 1):
                            p.job(s, "x", w, g, l)
                        for g in (2 * gg, 2 * gg + 1):
                            p.job(s, "tx", w, g, l)
                        for g in (2 * gg, 2 * gg + 1):
                            if l < 6:
                                p.job(s, "tt", w, g, l)
                    for g in (2 * gg, 2 * gg + 1):
                        p.job(s, "rhs", w, g)
                    for g in (2 * gg, 2 * gg + 1):
                        p.job(s, "u", w, g)
                    for g in (2 * gg, 2 * gg + 1):
                        p.job(s, "y", w, g)
                        if w == 0:
                            p.job(s, "s", w, g)
            turned("rwo")
            for b in range(2):
                p.gemm((s, "o", b), W["rw_w_out"], KD, b * COLS, COLS)
        elif s in ("ple0", "ple1"):
            i = int(s[-1])
            for j in range(1):
                p.job(s, "turn_p", j)
            turned(s)
            for b in range(2):
                p.gemm((s, "p", b), W["pe_w_proj%d" % i], 2, b * COLS, COLS)
            for b in range(2):
                p.gemm((s, "g", b), W["pe_w_gate%d" % i], KD, b * COLS, COLS)
        elif s == "da":
            turned(s)
            for i in range(8):
                p.gemm((s, i), W["da_w_in"], KD, i * COLS, COLS)
            for i in range(8):
                p.job(s, "qk", i)
            for hd in range(8):
                for qt in range(2):
                    for c in range(2):
                        p.job(s, "s", hd, qt, c)
                if hd:
                    p.job(s, "at", hd - 1)
                    p.job(s, "o", hd - 1)
            p.job(s, "at", 7)
            p.job(s, "o", 7)
            turned("dao")
            for b in range(2):
                p.gemm((s, "out", b), W["da_w_out"], KD, b * COLS, COLS)
        elif s == "ssm":
            turned(s)
            p.gemm((s, "dt"), W["ssm_w_in"], KD, 5 * D, SSM_H)
            for i in range(4):
                p.gemm((s, "z", i), W["ssm_w_in"], KD, i * COLS, COLS)
            p.job(s, "acum")
            before = None
            for i in CONV_ORDER:
                p.gemm_by_channel((s, "xb", i), W["ssm_w_in"], 2 * D + i * COLS,
                                  lambda j: before in (0, 1, 2) and p.job(s, "xt", before, j))
                before = i
            for j in range(2):
                p.job(s, "xt", before, j)
            for g in range(4):
                p.job(s, "cb", g)
            for u in range(SSM_H // 2 + 2):
                if u < SSM_H // 2:
                    p.job(s, "seg", u, 0)
                    p.job(s, "seg", u, 1)
                if u >= 2:
                    p.job(s, "y", u - 2)
            turned("ssmo", 8)
            for b in range(2):
                p.gemm((s, "out", b), W["ssm_w_out"], 2 * KD, b * COLS, COLS)
        elif s == "kv":
            p.job(s, "bias")
            turned(s)
            p.gemm((s, "kv"), W["w_kv"], KD, 0, 256)
            p.job(s, "vt")
            p.job(s, "kt")
        elif s == "swa":
            turned(s)
            for b in range(2):
                p.gemm((s, "q", b), W["w_q"], KD, b * COLS, COLS)
            for i in range(4):
                p.job(s, "qt", i)
            for pr in range(8):
                for qt in range(2):
                    for par in range(2):
                        p.job(s, "s", pr, qt, par)
                if pr:
                    for par in range(2):
                        p.job(s, "at", pr - 1, par)
                    p.job(s, "o", pr - 1)
            for par in range(2):
                p.job(s, "at", 7, par)
            p.job(s, "o", 7)
            turned("swao")
            for b in range(2):
                p.gemm((s, "out", b), W["w_o"], KD, b * COLS, COLS)
        elif s == "final":
            pass
        elif s.startswith("ffn"):
            turned(s)
            n = len(ffn_blocks())
            for b, (c0, cols) in enumerate(ffn_blocks()):
                p.gemm((s, "u", b), W["w1_" + s[-1]], KD, c0, cols)
                if b:
                    for i in range(2):
                        p.job(s, "gt", b - 1, i)
                p.gemm((s, "v", b), W["w3_" + s[-1]], KD, c0, cols)
            p.job(s, "gt", n - 1, 0)
            for b in range(2):
                p.gemm((s, "d", b), W["w2_" + s[-1]], KF, b * COLS, COLS)
    return p


ROW_SOURCES = {
    "rw": ["rw_norm", "rw_k_k", "rw_k_a", "rw_r_k", "rw_ln_w", "rw_ln_b"],
    "ple0": ["pe_norm0"], "ple1": ["pe_norm1"], "da": ["da_norm"], "final": ["final_norm"],
    "ffn0": ["ffn_norm0"], "ffn1": ["ffn_norm1"], "ffn2": ["ffn_norm2"], "ffn3": ["ffn_norm3"],
    "ssm": ["ssm_norm", "gate_norm0", "gate_norm1"], "kv": ["kv_norm"], "swa": ["attn_norm"],
}


def program(nc, A, out):
    W = {"rw_w_in": A["rw_w_in"][0], "rw_w_out": A["rw_w_out"][0], "da_w_in": A["da_w_in"][0],
         "da_w_out": A["da_w_out"][0], "ssm_w_in": A["ssm_w_in_2"][0], "ssm_w_out": A["ssm_w_out_2"][0],
         "w_kv": A["w_kv_2"], "w_q": A["w_q_2"][0], "w_o": A["w_o_2"][0]}
    for i in range(2):
        W["pe_w_gate%d" % i] = A["pe_w_gate"][i]
        W["pe_w_proj%d" % i] = A["pe_w_proj"][i]
    for i in range(4):
        for m in (1, 2, 3):
            W["w%d_%d" % (m, i)] = A["ffn_w%d_2" % m][i // 2, i % 2]
    R = {"rw_norm": A["rw_norm"][0], "rw_k_k": A["rw_k_k"][0], "rw_k_a": A["rw_k_a"][0],
         "rw_r_k": A["rw_r_k"][0].rearrange("h n -> (h n)"), "rw_ln_w": A["rw_ln_w"][0],
         "rw_ln_b": A["rw_ln_b"][0], "pe_norm0": A["pe_norm"][0], "pe_norm1": A["pe_norm"][1],
         "da_norm": A["da_norm"][0], "final_norm": A["final_norm"], "ssm_norm": A["ssm_norm_2"][0],
         "gate_norm0": A["ssm_gate_norm_2"][0, 0:D], "gate_norm1": A["ssm_gate_norm_2"][0, D:2 * D],
         "kv_norm": A["kv_norm_2"], "attn_norm": A["attn_norm_2"][0]}
    for i in range(4):
        R["ffn_norm%d" % i] = A["ffn_norm_2"][i // 2, i % 2]

    plan = build_plan(W)
    jobs, slabs, gemms = plan.jobs, plan.slabs, plan.gemms
    rows = [(s, r) for s in STAGES for r in ROW_SOURCES[s]]
    row_at = {key: n for n, key in enumerate(rows)}

    with ExitStack() as ctx:
        def sb(name, shape, dt=F32, scope=ctx):
            return scope.enter_context(nc.sbuf_tensor(name, shape, dt))

        def sem(name):
            return ctx.enter_context(nc.semaphore(name))

        bank = [ctx.enter_context(nc.psum_tensor("bank%d" % i, [P, COLS], F32)) for i in range(BANKS)]

        h = sb("h", [P, TT, D])
        xn = sb("xn", [P, TT, D])
        raw = sb("raw", [P, RAW_SLOTS, SLAB_K, COLS])
        w_hi = sb("w_hi", [P, PART_SLOTS, SLAB_K, COLS], F32R)
        w_lo = sb("w_lo", [P, PART_SLOTS, SLAB_K, COLS], F32R)
        row = sb("row", [P, ROW_SLOTS, D])
        const = sb("const", [P, N_CONST])
        stat = sb("stat", [P, 8])
        junk = sb("junk", [P, COLS], mybir.dt.bfloat16)
        first_half = ExitStack()
        p_tok = sb("p_tok", [P, TT, TT, 256], scope=first_half)
        first_half.close()
        kv_k = sb("kv_k", [P, 2, T])
        kv_v = sb("kv_v", [P, TT, P])
        rest_of_p_tok = sb("rest_of_p_tok", [P, 256])
        minus_half = sb("minus_half", [P, 32])

        core = ExitStack()
        ct = sb("ct", [P, 2, 2, 4, P], scope=core)
        ab = sb("ab", [P, 2, 4, 4, P], scope=core)
        inv = sb("inv", [P, 2, 2, 4, P], scope=core)
        core.close()
        x_hi = [sb("x_hi0", [P, KD, T], F32R)]
        x_lo = [sb("x_lo0", [P, KD, T], F32R)]

        rw = ExitStack()
        x_hi.append(sb("x_hi1", [P, KD, T], F32R, rw))
        x_lo.append(sb("x_lo1", [P, KD, T], F32R, rw))
        rw_r = sb("rw_r", [P, TT, D], scope=rw)
        rw_k = sb("rw_k", [P, TT, D], scope=rw)
        rw_v = sb("rw_v", [P, TT, D], scope=rw)
        rw_gate = sb("rw_gate", [P, TT, D], scope=rw)
        rw_sig = sb("rw_sig", [P, TT, D], scope=rw)
        rw_a = sb("rw_a", [P, TT, D], scope=rw)
        rw_kap = sb("rw_kap", [P, TT, D], scope=rw)
        level_a = sb("level_a", [P, 2, 4, P], scope=rw)
        state = sb("state", [P, 8, P], scope=rw)
        carry = sb("carry", [P, 8], scope=rw)
        bonus = sb("bonus", [P, TT, 16], scope=rw)
        hstat = sb("hstat", [P, 3, TT, 16], scope=rw)
        mu = sb("mu", [P, 6, KD], scope=rw)
        xn_ch = rw_gate[:, :, :].rearrange("p t (k c) -> p (t k) c", c=T)
        dx_ch = xn[:, :, :].rearrange("p t (k c) -> p (t k) c", c=T)
        mix_v = rw_v[:, :, :].rearrange("p t (k c) -> p (t k) c", c=T)
        mix_k = rw_k[:, :, :].rearrange("p t (k c) -> p (t k) c", c=T)
        rhs_sb = rw_sig[:, 1, 0:COLS].rearrange("p (g i c) -> p g i c", g=2, i=2)
        un_sb = rw_sig[:, 1, COLS:D].rearrange("p (g i c) -> p g i c", g=2, i=2)
        x_sb = rw_sig[:, 0, :].rearrange("p (g i c) -> p g i c", g=2, i=4)
        mix_s = rw_sig[:, :, :].rearrange("p t (k c) -> p (t k) c", c=T)
        lora_w1 = rw_a[:, 0, :].rearrange("p (x k c) -> p x k c", x=2, k=KD)
        lora_t = rw_a[:, 1, COLS:D].rearrange("p (x t) -> p x t", x=2)
        rw.close()
        decays = [[ab[:, i, :, :, :].rearrange("p a b c -> p (a b c)")[:, j * COLS:(j + 1) * COLS]
                   for j in range(3)] for i in range(2)]
        ff = ExitStack()
        g_hi = sb("g_hi", [P, KF, T], F32R, ff)
        g_lo = sb("g_lo", [P, KF, T], F32R, ff)
        g_tok = sb("g_tok", [P, 2, TT, COLS], scope=ff)
        silu = sb("silu", [P, TT, COLS], scope=ff)
        bias = sb("bias", [P, 16, T], scope=ff)
        bias_rows = sb("bias_rows", [16, BIAS_N], scope=ff)
        rel = sb("rel", [33, 16], scope=ff)
        picks = sb("picks", [33, BIAS_N], scope=ff)
        ff.close()
        bias_dram = nc.dram_tensor("bias_dram", [16, BIAS_N], F32, kind="Internal").ap()
        sw = ExitStack()
        sq_tok = sb("sq_tok", [P, TT, D], scope=sw)
        sq_ch = sb("sq_ch", [P, KD, T], scope=sw)
        s_sc = sb("s_sc", [P, 2, 2, T], scope=sw)
        s_pr = sb("s_pr", [P, 2, TT, 2, T], scope=sw)
        s_at = sb("s_at", [P, 2, 3, P], scope=sw)
        s_sm = sb("s_sm", [P, 16, 8], scope=sw)
        sinks = sb("sinks", [P, 16], scope=sw)
        q_norm = sb("q_norm", [P, 64], scope=sw)
        k_norm = sb("k_norm", [P, 64], scope=sw)
        k_tmp = sb("k_tmp", [P, TT, 2, 2, 64], scope=sw)
        v_tmp = sb("v_tmp", [P, TT, P], scope=sw)
        k_sq = sb("k_sq", [P, TT, 2, 64], scope=sw)
        sw_stat = sb("sw_stat", [P, 2, 32], scope=sw)
        sw.close()
        late = ExitStack()
        y_hi = sb("y_hi", [P, 2 * KD, T], F32R, late)
        y_lo = sb("y_lo", [P, 2 * KD, T], F32R, late)
        late.close()
        ss = ExitStack()
        z_tok = sb("z_tok", [P, TT, 2 * D], scope=ss)
        xs_tok = sb("xs_tok", [P, TT, 2 * D], scope=ss)
        y_tok = sb("y_tok", [P, TT, 2 * D], scope=ss)
        bc = sb("bc", [P, 8, T], scope=ss)
        conv_in = sb("conv_in", [P, 2, 2, T + 4], scope=ss)
        conv_sum = sb("conv_sum", [P, 2, 2, T], scope=ss)
        cb = sb("cb", [P, 4, 3 * P], scope=ss)
        seg = sb("seg", [P, 2, 2, 3 * P], scope=ss)
        conv_w = sb("conv_w", [P, 24, 4], scope=ss)
        conv_b = sb("conv_b", [P, 24], scope=ss)
        per_head_in = sb("per_head_in", [P, 3, SSM_H], scope=ss)
        dts = sb("dts", [P, 8, TT, SSM_H], scope=ss)
        ss_stat = sb("ss_stat", [P, 2, 8], scope=ss)
        seg_slot = [seg[:, 0, :, :], seg[:, 1, :, :],
                    conv_sum[:, :, :, :].rearrange("p a b c -> p (a b c)")[:, 0:6 * P].rearrange(
                        "p (c n) -> p c n", c=2)]
        ss.close()
        da = ExitStack()
        q_tok = sb("q_tok", [P, TT, D], scope=da)
        k_tok = sb("k_tok", [P, TT, D], scope=da)
        v_tok = sb("v_tok", [P, TT, D], scope=da)
        gate = sb("gate", [P, TT, D], scope=da)
        rot = sb("rot", [P, TT, D], scope=da)
        q_ch = sb("q_ch", [P, KD, T], scope=da)
        k_ch = sb("k_ch", [P, KD, T], scope=da)
        expo = sb("expo", [P, 2, 2, T], scope=da)
        att = sb("att", [P, 2, TT, T], scope=da)
        att_ch = sb("att_ch", [P, 2, 3, P], scope=da)
        sm = sb("sm", [P, 8 * TT, 8], scope=da)
        lq = sb("lq", [P, 4, 64], scope=da)
        lam = sb("lam", [P, 6], scope=da)
        subln = sb("subln", [P, P], scope=da)
        da_stat = sb("da_stat", [P, 2, 16], scope=da)
        da.close()
        pl = ExitStack()
        p_hi = sb("p_hi", [P, 2, T], F32R, pl)
        p_lo = sb("p_lo", [P, 2, T], F32R, pl)
        p_out = sb("p_out", [P, TT, D], scope=pl)
        sig = sb("sig", [P, TT, D], scope=pl)
        pl.close()

        ld_const, ld_mu, ld_lora, ld_p = sem("ld_const"), sem("ld_mu"), sem("ld_lora"), sem("ld_p")
        ld_bias, ld_tables = sem("ld_bias"), sem("ld_tables")
        ld_da, ld_ssm, ld_kv, ld_swa = sem("ld_da"), sem("ld_ssm"), sem("ld_kv"), sem("ld_swa")
        slab_loaded = [sem("slab_loaded%d" % i) for i in range(RAW_SLOTS)]
        row_loaded = [sem("row_loaded%d" % i) for i in range(ROW_SLOTS)]
        row_used = sem("row_used")
        slab_hi, slab_lo, slab_used = sem("slab_hi"), sem("slab_lo"), sem("slab_used")
        psum_ready = sem("psum_ready")
        bank_free = [sem("bank_free%d" % i) for i in range(BANKS)]
        turned_hi = sem("turned_hi")
        vec_step, act_step, pool_step = sem("vec_step"), sem("act_step"), sem("pool_step")
        stored = sem("stored")
        named = {}

        def event(*name):
            key = "_".join(map(str, name))
            if key not in named:
                named[key] = sem(key)
            return named[key]

        def ready(eng, *name):
            eng.wait_ge(psum_ready, jobs[name] + 1)

        def consumed(eng, *name):
            j = jobs[name]
            eng.wait_ge(bank_free[j % BANKS], j // BANKS + 1)

        def B(*name):
            return bank[jobs[name] % BANKS]

        def frees(ins, *name):
            ins.then_inc(bank_free[jobs[name] % BANKS], 1)

        def slab_released(eng, n):
            kind, what = slabs[n][5]
            if kind == "job":
                eng.wait_ge(psum_ready, jobs[what] + 1)
            else:
                eng.wait_ge(slab_used, what)

        def slab_in(buf, slot, n):
            kn, cols = slabs[n][2], slabs[n][4]
            if kn <= SLAB_K:
                return buf[:, slot, 0:kn, 0:cols]
            return buf[:, slot, :, :].rearrange("p k (x c) -> p (k x) c", c=cols)

        def C(name, part=slice(0, P)):
            lo_, hi_ = CONST_AT[name]
            return const[part, lo_:hi_]

        def over(x, n):
            return x.unsqueeze(1).broadcast_to([P, n, x.shape[1]])

        def level_no(w, g, l):
            return ((2 * w + g // 2) * 7 + l) * 2 + g % 2 + 1

        mixes = (mix_v, mix_k, mix_v, xn_ch)
        ident = C("ident")
        stage_before = dict(zip(STAGES[1:], STAGES))

        def h_done(eng, s):
            if s is None:
                eng.wait_ge(ld_const, 32)
            elif s == "rw":
                consumed(eng, (s, "o", 1), TT - 1)
            elif s in ("ple0", "ple1"):
                eng.wait_ge(event(s, "added"), 2 * TT)
            elif s in ("da", "swa", "ssm"):
                consumed(eng, (s, "out", 1), TT - 1)
            elif s == "final":
                eng.wait_ge(event(s, "normed"), TT)
            elif s.startswith("ffn"):
                consumed(eng, (s, "d", 1), TT - 1)
            elif s == "kv":
                consumed(eng, s, "turn", 3)

        turned_no = {}
        for name in jobs:
            if name[1] in ("turn", "turn_p", "gt") and name[0] != "rw":
                turned_no[name] = len(turned_no) + 1

        block = ctx.enter_context(nc.Block())

        @block.sync
        def _(sp):
            sp.dma_start(h[:, :, :], A["x"][0].rearrange("(t p) d -> p t d", p=P)).then_inc(ld_const, 16)
            sp.dma_start(const[:, 0:P], A["constants"][:, 0:P]).then_inc(ld_const, 16)
            nrow = [0]

            def load_rows(upto):
                while nrow[0] < upto:
                    n = nrow[0]
                    if n >= ROW_SLOTS:
                        sp.wait_ge(row_used, n - ROW_SLOTS + 1)
                    sp.dma_start(row[:, n % ROW_SLOTS, :], R[rows[n][1]].partition_broadcast(P)) \
                        .then_inc(row_loaded[n % ROW_SLOTS], 16)
                    nrow[0] += 1

            def load_slabs(lo_, hi_):
                for n in range(lo_, hi_):
                    w, k0, kn, c0, cols, _ = slabs[n]
                    if n >= RAW_SLOTS:
                        sp.wait_ge(slab_lo, n - RAW_SLOTS + 1)
                    sp.dma_start(slab_in(raw, n % RAW_SLOTS, n),
                                 w[k0 * P:(k0 + kn) * P, c0:c0 + cols].rearrange("(k p) c -> p k c", p=P)) \
                        .then_inc(slab_loaded[n % RAW_SLOTS], 16)

            def load_extras(s):
                if s == "ssm":
                    h_done(sp, stage_before.get(s))
                    sp.dma_start(conv_w[:, :, :], A["ssm_conv_w_2"]).then_inc(ld_ssm, 16)
                    sp.dma_start(conv_b[:, :], A["ssm_conv_b_2"]).then_inc(ld_ssm, 16)
                    for i, n in enumerate(("ssm_dt_bias_2", "ssm_a_log_2", "ssm_d_2")):
                        sp.dma_start(per_head_in[:, i, :], A[n][0].partition_broadcast(P)).then_inc(ld_ssm, 16)
                if s == "kv":
                    h_done(sp, stage_before.get(s))
                    sp.dma_start(rel[0:32, :], A["rel_bias_2"]).then_inc(ld_kv, 16)
                    sp.dma_start(picks[:, :], A["bias_picks"]).then_inc(ld_kv, 16)
                    sp.dma_start(k_norm[:, :], A["k_norm_2"].partition_broadcast(P)).then_inc(ld_kv, 16)
                if s == "swa":
                    h_done(sp, stage_before.get(s))
                    sp.dma_start(sinks[:, :], A["sinks_2"][0].partition_broadcast(P)).then_inc(ld_swa, 16)
                    sp.dma_start(q_norm[:, :], A["q_norm_2"][0].partition_broadcast(P)).then_inc(ld_swa, 16)
                if s == "da":
                    h_done(sp, stage_before.get(s))
                    for i, n in enumerate(("da_lq1", "da_lk1", "da_lq2", "da_lk2")):
                        sp.dma_start(lq[:, i, :], A[n][0].partition_broadcast(P)).then_inc(ld_da, 16)
                    sp.dma_start(subln[:, :], A["da_subln"][0].partition_broadcast(P)).then_inc(ld_da, 16)
                if s == "rw":
                    sp.dma_start(const[:, P:N_CONST], A["constants"][:, P:N_CONST]).then_inc(ld_tables, 16)
                    for i, (w1, w2, w0) in enumerate((("rw_w1", "rw_w2", "rw_w0"), ("rw_a1", "rw_a2", "rw_a0"))):
                        sp.dma_start(lora_w1[:, i], A[w1][0].rearrange("(k p) c -> p k c", p=P)).then_inc(ld_lora, 16)
                        sp.dma_start(rw_kap[0:64, i, :], A[w2][0]).then_inc(ld_lora, 16)
                        sp.dma_start(rw_kap[64:65, i, :], A[w0]).then_inc(ld_lora, 16)

            for s in STAGES:
                here = [n for n, (st, _) in enumerate(rows) if st == s]
                mine = [g for g in gemms if g[0] == s]
                if s == "rw":
                    load_rows(1)
                    sp.dma_start(mu[:, :, :], A["rw_mu"]).then_inc(ld_mu, 16)
                else:
                    load_rows(here[0] + min(len(here), ROW_SLOTS))
                for g in mine:
                    if g == mine[max(0, len(mine) - 2)]:
                        load_rows(here[-1] + 1)
                    load_slabs(gemms[g][0], gemms[g][1])
                    if g == mine[0]:
                        load_extras(s)
                    if s == "rw" and g == mine[2]:
                        load_rows(ROW_SLOTS)
                        sp.dma_start(p_tok[:, :, :, :], A["p"][:, 0].rearrange("i (t p) c -> p i t c", p=P)) \
                            .then_inc(ld_p, 16)
                if not mine:
                    load_rows(here[-1] + 1)
            h_done(sp, STAGES[-1])
            sp.dma_start(out[0].rearrange("(t p) d -> p t d", p=P), h[:, :, :]).then_inc(stored, 16)
            sp.wait_ge(stored, 16)

        @block.gpsimd
        def _(pool):
            O = Order(pool, pool_step)

            def power(s, what, dst, src, n):
                pool.wait_ge(event(s, what + "_mean"), 1)
                pool.tensor_tensor(dst, src, minus_half[:, 0:n], ALU.pow).then_inc(event(s, what + "_rstd"), 1)

            def group_power(s, t, b):
                h8 = slice(8 * b, 8 * b + 8)
                power(s, "group%d%d" % (t, b), hstat[:, 1, t, h8], hstat[:, 2, t, h8], 8)

            def half_power(s, dst, n, b):
                pool.wait_ge(event(s, "head_mean"), b + 1)
                pool.tensor_tensor(dst[:, 1, b * n:(b + 1) * n], dst[:, 0, b * n:(b + 1) * n],
                                   minus_half[:, 0:n], ALU.pow).then_inc(event(s, "head_rstd"), 1)

            def ssm_group_power(s, g):
                pool.wait_ge(event(s, "group_mean"), g + 1)
                pool.tensor_tensor(ss_stat[:, 1, 2 * g:2 * g + 2], ss_stat[:, 0, 2 * g:2 * g + 2],
                                   minus_half[:, 0:2], ALU.pow).then_inc(event(s, "group_rstd"), 1)

            O.step(pool.memset(minus_half[:, :], -0.5))
            O.settle()
            for s in STAGES:
                power(s, "norm", stat[:, 6:8], stat[:, 4:6], 2)
                if s == "rw":
                    ready(pool, s, "lora_out", "a", 1, 1)
                    for b in range(2):
                        consumed(pool, (s, "k", b), TT - 1)
                    n = row_at[(s, "rw_k_k")]
                    pool.wait_ge(row_loaded[n % ROW_SLOTS], 16 * (n // ROW_SLOTS + 1))
                    for t in range(TT):
                        pool.tensor_tensor(rw_kap[:, t, :], rw_k[:, t, :], row[:, n % ROW_SLOTS, :], ALU.mult) \
                            .then_inc(event(s, "kap"), 1)
                    pool.wait_ge(event(s, "mixed"), 4)
                    for t in range(TT):
                        pool.wait_ge(event(s, "kap"), t + 1)
                        pool.tensor_tensor(xn[:, t, :], rw_kap[:, t, :], rw_kap[:, t, :], ALU.mult) \
                            .then_inc(event(s, "kap_squared"), 1)
                    power(s, "kap", hstat[:, 1, :, :].rearrange("p t h -> p (t h)"),
                          hstat[:, 0, :, :].rearrange("p t h -> p (t h)"), 32)
                    pool.wait_ge(ld_tables, 16)
                    for w in range(TT):
                        for gg in range(2):
                            for l in range(7):
                                for g in (2 * gg, 2 * gg + 1):
                                    if l == 0:
                                        for par in range(2):
                                            consumed(pool, s, "ab", w, g, par)
                                        if (w, gg) != (0, 0):
                                            ready(pool, s, "x", w if gg else w - 1, g - 2 if gg else g + 2, 6)
                                    elif l == 1:
                                        pool.wait_ge(event(s, "inverse_begun"), 4 * w + g + 1)
                                    else:
                                        ready(pool, s, "x", w, g, l - 1)
                                    pool.tensor_tensor(level_a[:, g % 2, :, :], ab[:, g % 2, :, 0, :],
                                                       over(C("levels")[:, l * P:(l + 1) * P], 4), ALU.mult) \
                                        .then_inc(event(s, "level_a"), 1)
                                if w == 1 and l == 3:
                                    for t, b in (((0, 0), (0, 1)), ((1, 0),))[gg]:
                                        group_power(s, t, b)
                    group_power(s, 1, 1)
                if s == "da":
                    for hd in range(8):
                        consumed(pool, s, "o", hd)
                        if hd == 0:
                            pool.wait_ge(event(s, "gate_gained"), 1)
                        c = slice(hd * P, (hd + 1) * P)
                        pool.tensor_tensor(xn[:, :, c], xn[:, :, c], gate[:, :, c], ALU.mult) \
                            .then_inc(event(s, "head_gated"), 1)
                        if hd in (5, 7):
                            half_power(s, da_stat, 8, hd // 7)
                if s == "ssm":
                    for i in range(4):
                        for j in range(2):
                            consumed(pool, s, "xt", i, j)
                        c = slice(i * COLS, (i + 1) * COLS)
                        h8 = slice(8 * i, 8 * i + 8)
                        if i == 0:
                            pool.wait_ge(event(s, "dta"), TT)
                        pool.tensor_tensor(y_tok[:, :, c].rearrange("p t (h c) -> p t h c", c=64),
                                           xs_tok[:, :, c].rearrange("p t (h c) -> p t h c", c=64),
                                           dts[:, 5, :, h8].unsqueeze(3).broadcast_to([P, TT, 8, 64]),
                                           ALU.mult).then_inc(event(s, "x_dt"), 1)
                        pool.wait_ge(event(s, "x_dt"), i + 1)
                        for t in range(TT):
                            x8 = xs_tok[:, t, c].rearrange("p (h c) -> p h c", c=64)
                            pool.tensor_tensor(x8, x8, per_head_in[:, 2, h8].unsqueeze(2).broadcast_to([P, 8, 64]),
                                               ALU.mult).then_inc(event(s, "x_d"), 1)
                    for v in range(SSM_H // 2):
                        pool.wait_ge(event(s, "y_sum"), v + 1)
                        c = slice(v * P, (v + 1) * P)
                        pool.tensor_tensor(y_tok[:, :, c], y_tok[:, :, c], z_tok[:, :, c], ALU.mult) \
                            .then_inc(event(s, "y_gated"), 1)
                        if v % 4 == 1 and v > 4:
                            ssm_group_power(s, v // 4 - 1)
                    ssm_group_power(s, 3)
                if s == "kv":
                    power(s, "head", sw_stat[:, 1, 0:4], sw_stat[:, 0, 0:4], 4)
                    consumed(pool, s, "bias")
                    pool.dma_start(bias_dram, bias_rows[:, :]).then_inc(ld_bias, 16)
                    pool.wait_ge(ld_bias, 16)
                    pool.dma_start(bias[:, :, :], bass.AP(bias_dram.tensor, 0, [[1, P], [BIAS_N, 16], [1, T]])) \
                        .then_inc(ld_bias, 16)
                if s == "swa":
                    for b in range(2):
                        half_power(s, sw_stat, 16, b)

        @block.scalar
        def _(act):
            O = Order(act, act_step)
            split = [0]

            def hi_parts(name, count=99):
                while split[0] < min(gemms[name][1], gemms[name][0] + count):
                    n = split[0]
                    act.wait_ge(slab_loaded[n % RAW_SLOTS], 16 * (n // RAW_SLOTS + 1))
                    if n >= PART_SLOTS:
                        slab_released(act, n - PART_SLOTS)
                    act.activation(slab_in(w_hi, n % PART_SLOTS, n), slab_in(raw, n % RAW_SLOTS, n),
                                   ACT.Copy).then_inc(slab_hi, 1)
                    split[0] += 1

            def squares(s):
                h_done(act, stage_before.get(s))
                for b in range(2):
                    for t in range(TT):
                        O.step(act.activation(junk[:, :], h[:, t, b * COLS:(b + 1) * COLS], ACT.Square,
                                              accum_out=stat[:, 2 * b + t:2 * b + t + 1]))
                        if (b, t) == (1, 1):
                            O.settle()
                            act.sem_inc(event(s, "squares"), 1)
                        O.settle()

            def rstd(s, t):
                if s not in DEFERRED:
                    return 1.0
                if s not in waited_for:
                    act.wait_ge(event(s, "norm_rstd"), 1)
                    waited_for.add(s)
                return stat[:, 6 + t:7 + t]

            waited_for = set()

            def take_hi(*name):
                ready(act, *name)
                i = name[-1]
                hi = {"turn": x_hi[0], "turn_p": p_hi, "gt": g_hi}[name[1]]
                if name[0] == "ssmo":
                    hi = y_hi
                b_ = i if name[1] != "gt" else 2 * name[2] + i
                act.activation(hi[:, 2 * b_:2 * b_ + 2, :], B(*name)[:, :].rearrange("p (k t) -> p k t", k=2),
                               ACT.Copy).then_inc(turned_hi, 1)

            def activations(s, tag=None, n=4):
                for i in range(n):
                    take_hi(tag or s, "turn", i)

            def evacuate(name, dst, func=ACT.Copy):
                for t in range(TT):
                    ready(act, name, t)
                    scale = 1.0 if name[1] == "p" else rstd(name[0], t)
                    frees(act.activation(dst(t), B(name, t)[:, 0:gemms[name][2]], func, scale=scale), name, t)

            def rwkv(s):
                hi_parts((s, "r", 0), 1)
                for i in range(4):
                    ready(act, s, "turn", i)
                    frees(act.activation(xn_ch[:, 2 * i:2 * i + 2, :],
                                         B(s, "turn", i)[:, :].rearrange("p (k t) -> p k t", k=2), ACT.Copy),
                          s, "turn", i)
                def mix_hi(i):
                    act.wait_ge(event(s, "mixed"), i + 1)
                    if i >= 2:
                        ready(act, (s, "rkvg"[i - 2], 1), TT - 1)
                    act.activation(x_hi[i % 2][:, :, :], mixes[i], ACT.Copy) \
                        .then_inc(event(s, "mix_hi"), 1)

                def take(x, b):
                    dst = {"r": rw_r, "k": rw_k, "v": rw_v, "g": rw_gate}[x]
                    evacuate((s, x, b), lambda t: dst[:, t, b * COLS:(b + 1) * COLS],
                             ACT.Silu if x == "g" else ACT.Copy)

                hi_parts((s, "r", 0), 2)
                mix_hi(0)
                hi_parts((s, "r", 1))
                mix_hi(1)
                hi_parts((s, "k", 0))
                take("r", 0)
                take("r", 1)
                hi_parts((s, "k", 1))
                take("k", 0)
                hi_parts((s, "v", 0))
                take("k", 1)
                for i, (x, func) in enumerate((("w", ACT.Tanh), ("a", ACT.Copy))):
                    ready(act, s, "lora_in", x)
                    frees(act.activation(lora_t[0:64, i, :], B(s, "lora_in", x)[0:64, 0:T], func), s, "lora_in", x)
                mix_hi(2)
                for i, x in enumerate("wa"):
                    for b in range(2):
                        for t in range(TT):
                            ready(act, s, "lora_out", x, b, t)
                            frees(act.activation((rw_sig, rw_a)[i][:, t, b * COLS:(b + 1) * COLS],
                                                 B(s, "lora_out", x, b, t)[:, :], ACT.Sigmoid),
                                  s, "lora_out", x, b, t)
                hi_parts((s, "v", 1))
                mix_hi(3)
                hi_parts((s, "g", 0))
                take("v", 0)
                take("v", 1)
                hi_parts((s, "g", 1))
                take("g", 0)
                take("g", 1)
                for b in range(2):
                    for w in range(TT):
                        i = 2 * b + w
                        ready(act, s, "cum", b, w)
                        if i >= 2:
                            act.wait_ge(event(s, "decayed"), i - 1)
                        e = decays[i % 2]
                        act.activation(e[0], B(s, "cum", b, w)[:, :], ACT.Exp).then_inc(event(s, "exp_p"), 1)
                        frees(act.activation(e[1], B(s, "cum", b, w)[:, :], ACT.Exp, scale=-1.0), s, "cum", b, w)
                        ready(act, s, "cumx", b, w)
                        frees(act.activation(e[2], B(s, "cumx", b, w)[:, :], ACT.Exp), s, "cumx", b, w)
                ready(act, s, "carry")
                frees(act.activation(carry[:, :], B(s, "carry")[:, 0:8], ACT.Exp), s, "carry")
                for w in range(TT):
                    for gg in range(2):
                        pair = (2 * gg, 2 * gg + 1)
                        for g in pair:
                            for pp in range(2):
                                ready(act, s, "ct", w, g, pp)
                                frees(act.activation(ct[:, g % 2, pp, :, :],
                                                     B(s, "ct", w, g, pp)[:, :].rearrange("p (i c) -> p i c", i=4),
                                                     ACT.Copy), s, "ct", w, g, pp)
                        def four(*name):
                            return B(*name)[:, :].rearrange("p (i c) -> p i c", i=4)

                        for g in pair:
                            ready(act, s, "t0", w, g)
                            frees(act.activation(inv[:, g % 2, 0], four(s, "t0", w, g), ACT.Copy), s, "t0", w, g)
                        for l in range(1, 7):
                            for g in pair:
                                ready(act, s, "x", w, g, l)
                                frees(act.activation(x_sb[:, g % 2], four(s, "x", w, g, l), ACT.Copy),
                                      s, "x", w, g, l)
                            if (w, gg, l) == (1, 1, 3):
                                hi_parts((s, "o", 0))
                            if l < 6:
                                for g in pair:
                                    ready(act, s, "tt", w, g, l)
                                    frees(act.activation(inv[:, g % 2, 1], four(s, "tt", w, g, l), ACT.Copy),
                                          s, "tt", w, g, l)
                        for what, dst, sign in (("rhs", rhs_sb, 1.0), ("u", un_sb, -1.0)):
                            for g in pair:
                                ready(act, s, what, w, g)
                                frees(act.activation(dst[:, g % 2, :, :],
                                                     B(s, what, w, g)[:, 0:2 * P].rearrange("p (i c) -> p i c", i=2),
                                                     ACT.Copy, scale=sign), s, what, w, g)
                        for g in pair:
                            ready(act, s, "y", w, g)
                            frees(act.activation(xn[:, w, g * 2 * P:(g + 1) * 2 * P], B(s, "y", w, g)[:, 0:2 * P],
                                                 ACT.Copy), s, "y", w, g)
                            if w == 0:
                                ready(act, s, "s", w, g)
                                act.wait_ge(event(s, "state_zeroed"), 1)
                                consumed(act, s, "carry")
                                o = B(s, "s", w, g)
                                for pp in range(2):
                                    for par in range(2):
                                        r_, c_ = slice(64 * par, 64 * par + 64), pp * P + 64 * par
                                        ins = act.activation(state[r_, 2 * g + pp, 64 * par:64 * par + 64],
                                                             o[r_, c_:c_ + 64], ACT.Copy,
                                                             scale=carry[r_, 2 * g + pp:2 * g + pp + 1])
                                frees(ins, s, "s", w, g)
                hi_parts((s, "o", 0))
                activations(s, "rwo")
                hi_parts((s, "o", 1))

            for s in STAGES:
                if s not in DEFERRED:
                    squares(s)
                if s == "rw":
                    rwkv(s)
                elif s in ("ple0", "ple1"):
                    hi_parts((s, "p", 0))
                    take_hi(s, "turn_p", 0)
                    activations(s)
                    hi_parts((s, "p", 1))
                    squares(s)
                    hi_parts((s, "g", 0), 1)
                    for b in range(2):
                        evacuate((s, "p", b), lambda t: p_out[:, t, b * COLS:(b + 1) * COLS])
                    for b in range(2):
                        hi_parts((s, "g", b))
                        if b:
                            evacuate((s, "g", 0), lambda t: sig[:, t, 0:COLS], ACT.Sigmoid)
                    evacuate((s, "g", 1), lambda t: sig[:, t, COLS:D], ACT.Sigmoid)
                elif s == "da":
                    hi_parts((s, 0))
                    activations(s)
                    squares(s)
                    dst = [q_tok, q_tok, k_tok, k_tok, v_tok, v_tok, gate, gate]
                    for i in range(8):
                        if i < 7:
                            hi_parts((s, i + 1))
                        if i == 4:
                            act.wait_ge(event(s, "lq_dots"), 1)
                            act.activation(lam[:, 2:4], lam[:, 0:2], ACT.Exp).then_inc(event(s, "lq_exp"), 1)
                        evacuate((s, i), lambda t: dst[i][:, t, (i % 2) * COLS:(i % 2 + 1) * COLS],
                                 ACT.Silu if i >= 6 else ACT.Copy)
                    for i in range(8):
                        ready(act, s, "qk", i)
                        dst_ch = (q_ch if i < 4 else k_ch)[:, 2 * (i % 4):2 * (i % 4) + 2, :]
                        frees(act.activation(dst_ch, B(s, "qk", i)[:, :].rearrange("p (k t) -> p k t", k=2),
                                             ACT.Copy), s, "qk", i)

                    def weigh_values(hd):
                        ready(act, s, "at", hd)
                        frees(act.activation(att_ch[:, hd % 2, :, :],
                                             B(s, "at", hd)[:, 0:3 * P].rearrange("p (i q) -> p i q", i=3),
                                             ACT.Copy), s, "at", hd)
                        ready(act, s, "o", hd)
                        for t in range(TT):
                            n = 8 * (hd // 4) + 4 * t + hd % 4
                            act.activation(junk[:, 0:P], B(s, "o", hd)[:, t * P:(t + 1) * P], ACT.Square,
                                           accum_out=da_stat[:, 0, n:n + 1]).then_inc(event(s, "head_squares"), 1)
                            act.wait_ge(event(s, "head_squares"), 2 * hd + t + 1)
                        frees(act.activation(xn[:, :, hd * P:(hd + 1) * P],
                                             B(s, "o", hd)[:, 0:T].rearrange("p (t c) -> p t c", t=TT),
                                             ACT.Copy), s, "o", hd)

                    for hd in range(8):
                        for qt in range(TT):
                            u, n = hd * TT + qt, (qt + 1) * P
                            act.wait_ge(event(s, "max"), u + 1)
                            if u >= 2:
                                act.wait_ge(event(s, "att"), u - 1)
                            for c in range(2):
                                frees(act.activation(expo[:, u % 2, c, 0:n], B(s, "s", hd, qt, c)[:, 0:n], ACT.Exp,
                                                     bias=sm[:, u, 2 + c:3 + c], scale=64 ** -0.5,
                                                     accum_out=sm[:, u, 4 + c:5 + c]), s, "s", hd, qt, c)
                        if hd:
                            weigh_values(hd - 1)
                        if hd == 4:
                            hi_parts((s, "out", 0), PART_SLOTS)
                    weigh_values(7)
                    for b in range(2):
                        hi_parts((s, "out", b))
                        if b == 0:
                            activations(s, "dao")
                elif s == "ssm":
                    hi_parts((s, "dt"))
                    activations(s)
                    act.wait_ge(ld_ssm, 16 * 5)
                    act.activation(per_head_in[:, 1, :], per_head_in[:, 1, :], ACT.Exp) \
                        .then_inc(event(s, "a"), 1)
                    hi_parts((s, "z", 0))
                    act.wait_ge(event(s, "dt_minus_abs"), 1)
                    O.step(act.activation(dts[:, 2], dts[:, 1], ACT.Exp))
                    O.settle()
                    act.activation(dts[:, 3], dts[:, 2], ACT.Ln, bias=1.0).then_inc(event(s, "dt_log"), 1)
                    for i in range(4):
                        hi_parts((s, "z", i + 1) if i < 3 else (s, "xb", CONV_ORDER[0]))
                        evacuate((s, "z", i), lambda t: z_tok[:, t, i * COLS:(i + 1) * COLS], ACT.Silu)

                    def group_squares(g):
                        act.wait_ge(event(s, "y_gated"), 4 * g + 4)
                        for t in range(TT):
                            act.activation(junk[:, :], y_tok[:, t, g * COLS:(g + 1) * COLS], ACT.Square,
                                           accum_out=ss_stat[:, 0, 2 * g + t:2 * g + t + 1]) \
                                .then_inc(event(s, "group_squares"), 1)
                            act.wait_ge(event(s, "group_squares"), 2 * g + t + 1)

                    def conv_out(i, j):
                        m = 2 * i + j
                        n = CONV_ORDER.index(i) * 2 + j
                        act.wait_ge(event(s, "convolved"), n + 1)
                        for c in range(2):
                            tile_ = 4 * i + 2 * j + c
                            dst = bc[:, tile_ - 16, :] if i >= 4 else conv_sum[:, n % 2, c, :]
                            act.activation(dst, conv_sum[:, n % 2, c, :], ACT.Silu,
                                           bias=conv_b[:, tile_:tile_ + 1]).then_inc(event(s, "conv_out"), 1)

                    def take_tokens(i, j):
                        ready(act, s, "xt", i, j)
                        c = i * COLS + j * 256
                        frees(act.activation(xs_tok[:, :, c:c + 256],
                                             B(s, "xt", i, j)[:, :].rearrange("p (t c) -> p t c", t=TT),
                                             ACT.Copy), s, "xt", i, j)

                    for n, i in enumerate(CONV_ORDER):
                        for j in range(2):
                            ready(act, (s, "xb", i), j)
                            if 2 * n + j >= 2:
                                act.wait_ge(event(s, "convolved"), 2 * n + j - 1)
                            frees(act.activation(conv_in[:, j, :, 3:3 + T],
                                                 B((s, "xb", i), j)[:, :].rearrange("p (c t) -> p c t", c=2),
                                                 ACT.Copy), (s, "xb", i), j)
                            if n < 5:
                                hi_parts((s, "xb", CONV_ORDER[n + 1]), j + 1)
                            if n and CONV_ORDER[n - 1] < 4:
                                take_tokens(CONV_ORDER[n - 1], j)
                            conv_out(i, j)
                    for j in range(2):
                        take_tokens(3, j)
                    act.wait_ge(event(s, "sums_negated"), 2)
                    for u in range(SSM_H // 2):
                        ready(act, s, "seg", u, 1)
                        if u >= 3:
                            ready(act, s, "y", u - 3)
                        for lo2, n2, t in ((0, T, 0), (T, P, 1)):
                            ins = act.activation(seg_slot[u % 3][:, 1, lo2:lo2 + n2],
                                                 B(s, "seg", u, 1)[:, t * P:t * P + n2], ACT.Relu,
                                                 bias=dts[:, 4, t, 2 * u + 1:2 * u + 2], scale=-1.0)
                            if t == 0:
                                O.step(ins)
                        frees(ins, s, "seg", u, 1)
                        O.settle()
                        consumed(act, s, "seg", u, 1)
                        O.step(act.activation(seg_slot[u % 3][:, 1, :], seg_slot[u % 3][:, 1, :], ACT.Exp, scale=-1.0))
                        act.wait_ge(event(s, "seg"), u + 1)
                        act.activation(seg_slot[u % 3][:, 0, :], seg_slot[u % 3][:, 0, :], ACT.Exp) \
                            .then_inc(event(s, "seg_exp"), 1)
                        if u in (3, 5, 7):
                            hi_parts((s, "out", 0), (u - 1) // 2)
                        if u % 4 == 2 and u > 4:
                            group_squares((u - 6) // 4)
                    group_squares(3)
                    activations(s, "ssmo", 8)
                    for b in range(2):
                        hi_parts((s, "out", b))
                elif s == "kv":
                    hi_parts((s, "kv"))
                    activations(s)
                    squares(s)
                    ready(act, (s, "kv"), TT - 1)
                    ready(act, s, "vt")
                    frees(act.activation(kv_v[:, :, :], B(s, "vt")[:, 0:2 * P].rearrange("p (t c) -> p t c", t=TT),
                                         ACT.Copy), s, "vt")
                    ready(act, s, "kt")
                    frees(act.activation(kv_k[:, :, :], B(s, "kt")[:, :].rearrange("p (h t) -> p h t", h=2),
                                         ACT.Copy), s, "kt")
                elif s == "swa":
                    hi_parts((s, "q", 0))
                    activations(s)
                    squares(s)
                    for b in range(2):
                        if b == 0:
                            hi_parts((s, "q", 1))
                        evacuate((s, "q", b), lambda t: sq_tok[:, t, b * COLS:(b + 1) * COLS])
                    for i in range(4):
                        ready(act, s, "qt", i)
                        frees(act.activation(sq_ch[:, 2 * i:2 * i + 2, :],
                                             B(s, "qt", i)[:, :].rearrange("p (k t) -> p k t", k=2), ACT.Copy),
                              s, "qt", i)

                    def window_values(pr):
                        for par in range(2):
                            ready(act, s, "at", pr, par)
                            frees(act.activation(s_at[:, par, :, :],
                                                 B(s, "at", pr, par)[:, 0:3 * P].rearrange("p (i q) -> p i q", i=3),
                                                 ACT.Copy), s, "at", pr, par)
                        ready(act, s, "o", pr)
                        frees(act.activation(xn[:, :, pr * P:(pr + 1) * P],
                                             B(s, "o", pr)[:, 0:T].rearrange("p (t c) -> p t c", t=TT),
                                             ACT.Copy), s, "o", pr)

                    for pr in range(8):
                        for qt in range(TT):
                            u, n = pr * TT + qt, (qt + 1) * P
                            act.wait_ge(event(s, "max"), u + 1)
                            if pr >= 2:
                                ready(act, s, "at", pr - 2, 1)
                            for c in range(2):
                                act.activation(s_pr[:, pr % 2, qt, c, 0:n], s_sc[:, u % 2, c, 0:n], ACT.Exp,
                                               bias=s_sm[:, u, 2 + c:3 + c],
                                               accum_out=s_sm[:, u, 4 + c:5 + c]).then_inc(event(s, "exp"), 1)
                            act.activation(s_sm[:, u, 0:2], s_sm[:, u, 0:2], ACT.Exp).then_inc(event(s, "exp"), 1)
                        if pr:
                            window_values(pr - 1)
                        if pr == 4:
                            hi_parts((s, "out", 0), PART_SLOTS)
                    window_values(7)
                    hi_parts((s, "out", 0))
                    activations(s, "swao")
                    hi_parts((s, "out", 1))
                elif s.startswith("ffn"):
                    hi_parts((s, "u", 0))
                    activations(s)
                    squares(s)
                    blocks = ffn_blocks()

                    def gated_hi(b):
                        for i in range(blocks[b][1] // 256):
                            take_hi(s, "gt", b, i)

                    for b, (_, cols) in enumerate(blocks):
                        hi_parts((s, "u", b))
                        hi_parts((s, "v", b))
                        if b:
                            gated_hi(b - 1)
                            act.wait_ge(bank_free[jobs[(s, "v", b - 1), 1] % BANKS],
                                        jobs[(s, "v", b - 1), 1] // BANKS + 1)
                        evacuate((s, "u", b), lambda t: silu[:, t, 0:cols], ACT.Silu)
                    hi_parts((s, "d", 0), 2)
                    gated_hi(len(blocks) - 1)
                    for b in range(2):
                        hi_parts((s, "d", b))

        @block.vector
        def _(dve):
            O = Order(dve, vec_step)
            split = [0]

            def lo_parts(name, count=99):
                while split[0] < min(gemms[name][1], gemms[name][0] + count):
                    n = split[0]
                    dve.wait_ge(slab_hi, n + 1)
                    hi = slab_in(w_hi, n % PART_SLOTS, n)
                    dve.tensor_tensor(slab_in(w_lo, n % PART_SLOTS, n), slab_in(raw, n % RAW_SLOTS, n),
                                      hi.bitcast(F32), ALU.subtract).then_inc(slab_lo, 1)
                    split[0] += 1

            def use_row(s, r):
                n = row_at[(s, r)]
                dve.wait_ge(row_loaded[n % ROW_SLOTS], 16 * (n // ROW_SLOTS + 1))
                return row[:, n % ROW_SLOTS, :]

            def release_row():
                O.settle()
                dve.sem_inc(row_used, 1)

            def signal(ins, sem_, value):
                ins.then_inc(sem_, 1)
                O.last = (sem_, value)

            def frees_bank(ins, *name):
                frees(ins, *name)
                O.last = (bank_free[jobs[name] % BANKS], jobs[name] // BANKS + 1)

            def mean_square(s):
                dve.wait_ge(event(s, "squares"), 1)
                O.step(dve.tensor_tensor(stat[:, 4:6], stat[:, 0:2], stat[:, 2:4], ALU.add))
                O.settle()
                signal(dve.tensor_scalar(stat[:, 4:6], stat[:, 4:6], 1.0 / D, 1e-6, ALU.mult, ALU.add),
                       event(s, "norm_mean"), 1)

            def norm(s, dst, done):
                mean_square(s)
                gain = use_row(s, ROW_SOURCES[s][0])
                dve.wait_ge(event(s, "norm_rstd"), 1)
                for t in range(TT):
                    signal(dve.scalar_tensor_tensor(out=dst[:, t, :], in0=h[:, t, :],
                                                    scalar=stat[:, 6 + t:7 + t], in1=gain, op0=ALU.mult,
                                                    op1=ALU.mult), event(s, done), t + 1)
                release_row()

            def rstd(s, t):
                if s not in waited_for:
                    dve.wait_ge(event(s, "norm_rstd"), 1)
                    waited_for.add(s)
                return stat[:, 6 + t:7 + t]

            waited_for = set()

            def gain_next(s, b):
                after = STAGES[STAGES.index(s) + 1] if s in STAGES[:-1] else STAGES[0] if s is None else None
                if after not in DEFERRED:
                    return
                gain = use_row(after, ROW_SOURCES[after][0])
                O.settle()
                c = slice(b * COLS, (b + 1) * COLS)
                for t in range(TT):
                    signal(dve.tensor_tensor(xn[:, t, c], h[:, t, c], gain[:, c], ALU.mult),
                           event(after, "scaled"), 2 * b + t + 1)
                if b:
                    release_row()
                elif s not in (None, "final", "kv") and not s.startswith("ple"):
                    lo_parts(next(g for g in gemms if g[0] == after), 1)

            def take_lo(*name):
                dve.wait_ge(turned_hi, turned_no[name])
                i = name[-1]
                hi, lo_ = {"turn": (x_hi[0], x_lo[0]), "turn_p": (p_hi, p_lo), "gt": (g_hi, g_lo)}[name[1]]
                if name[0] == "ssmo":
                    hi, lo_ = y_hi, y_lo
                b_ = i if name[1] != "gt" else 2 * name[2] + i
                frees_bank(dve.tensor_tensor(lo_[:, 2 * b_:2 * b_ + 2, :],
                                             B(*name)[:, :].rearrange("p (k t) -> p k t", k=2),
                                             hi[:, 2 * b_:2 * b_ + 2, :].bitcast(F32), ALU.subtract), *name)

            def activations(s, tag=None, n=4):
                for i in range(n):
                    take_lo(tag or s, "turn", i)

            def add_to_h(name, c0, scale=1.0):
                cols = gemms[name][2]
                for t in range(TT):
                    ready(dve, name, t)
                    dst = h[:, t, c0:c0 + cols]
                    frees_bank(dve.scalar_tensor_tensor(out=dst, in0=B(name, t)[:, 0:cols], scalar=scale, in1=dst,
                                                        op0=ALU.mult, op1=ALU.add), name, t)

            def rwkv(s):
                norm(s, xn, "scaled")
                lo_parts((s, "r", 0), 1)
                O.step(dve.memset(lora_t[64:65, :, :], 1.0))
                signal(dve.memset(state[:, :, :], 0.0), event(s, "state_zeroed"), 1)
                for i in range(4):
                    consumed(dve, s, "turn", i)
                dve.wait_ge(ld_mu, 16)
                O.step(dve.tensor_scalar(dx_ch[:, :, 0:1], xn_ch[:, :, 0:1], -1.0, None, ALU.mult))
                O.step(dve.tensor_tensor(dx_ch[:, :, 1:T], xn_ch[:, :, 0:T - 1], xn_ch[:, :, 1:T], ALU.subtract))
                O.settle()

                def mix(dst, m, sem_, value):
                    for k in range(KD):
                        ins = dve.scalar_tensor_tensor(out=dst[:, k, :], in0=dx_ch[:, k, :], scalar=mu[:, m, k:k + 1],
                                                       in1=xn_ch[:, k, :], op0=ALU.mult, op1=ALU.add)
                        if k < KD - 1:
                            O.step(ins)
                    signal(ins, sem_, value)

                def mix_projection(i):
                    mix(mixes[i], i, event(s, "mixed"), i + 1)

                def mix_lo(i):
                    dve.wait_ge(event(s, "mix_hi"), i + 1)
                    signal(dve.tensor_tensor(x_lo[i % 2][:, :, :], mixes[i],
                                             x_hi[i % 2][:, :, :].bitcast(F32), ALU.subtract),
                           event(s, "mix_lo"), i + 1)

                mix_projection(0)
                lo_parts((s, "r", 0), 2)
                mix_lo(0)
                lo_parts((s, "r", 0))
                mix_projection(1)
                lo_parts((s, "r", 1))
                mix_lo(1)
                mix(mix_s, 4, event(s, "lora_mixed"), 1)
                lo_parts((s, "k", 0))
                mix(mix_v, 5, event(s, "lora_mixed"), 2)
                lo_parts((s, "k", 1))
                lo_parts((s, "v", 0), 1)
                ready(dve, s, "lora_in", "a")
                mix_projection(2)
                mix_lo(2)
                lo_parts((s, "v", 0))
                mix_projection(3)
                lo_parts((s, "v", 1))
                mix_lo(3)

                heads32 = [P, 2 * 16, 64]

                def by_head(x):
                    return x[:, :, :].rearrange("p t (h c) -> p (t h) c", c=64)

                def per_head(x):
                    return x.rearrange("p t h -> p (t h)").unsqueeze(2).broadcast_to(heads32)

                def row_op(dst, a_, r_, op):
                    for t in range(TT):
                        O.step(dve.tensor_tensor(dst[:, t, :], a_[:, t, :], r_, op))

                for b in range(2):
                    consumed(dve, (s, "k", b), TT - 1)
                ready(dve, s, "lora_out", "a", 1, 1)
                lo_parts((s, "g", 0), 2)
                dve.wait_ge(event(s, "kap_squared"), TT)
                use_row(s, "rw_k_k")
                release_row()
                O.step(dve.tensor_reduce(hstat[:, 0, :, :].rearrange("p t h -> p (t h)"), by_head(xn), X, ALU.add))
                O.settle()
                signal(dve.tensor_scalar(hstat[:, 0, :, :], hstat[:, 0, :, :], 1e-24, None, ALU.max),
                       event(s, "kap_mean"), 1)
                lo_parts((s, "g", 0))
                consumed(dve, s, "lora_out", "a", 1, 1)
                ka = use_row(s, "rw_k_a")
                for t in range(TT):
                    O.step(dve.scalar_tensor_tensor(out=xn[:, t, :], in0=rw_a[:, t, :], scalar=-1.0, in1=ka,
                                                    op0=ALU.add, op1=ALU.mult))
                release_row()
                for t in range(TT):
                    O.step(dve.scalar_tensor_tensor(out=rw_k[:, t, :], in0=xn[:, t, :], scalar=1.0, in1=rw_k[:, t, :],
                                                    op0=ALU.add, op1=ALU.mult))
                O.settle()
                dve.wait_ge(event(s, "kap_rstd"), 1)
                O.step(dve.tensor_tensor(by_head(rw_kap), by_head(rw_kap), per_head(hstat[:, 1, :, :]), ALU.mult))
                lo_parts((s, "g", 1))
                O.step(dve.tensor_tensor(xn[:, :, :], rw_r[:, :, :], rw_k[:, :, :], ALU.mult))
                O.settle()
                row_op(xn, xn, use_row(s, "rw_r_k"), ALU.mult)
                release_row()
                O.step(dve.tensor_reduce(bonus[:, :, :].rearrange("p t h -> p (t h)"), by_head(xn), X, ALU.add))
                O.step(dve.tensor_tensor(rw_a[:, :, :], rw_kap[:, :, :], rw_a[:, :, :], ALU.mult))
                O.settle()
                for b in range(2):
                    for w in range(TT):
                        consumed(dve, s, "cumx", b, w)
                        e, c = decays[(2 * b + w) % 2], slice(b * COLS, (b + 1) * COLS)
                        for x, i in ((rw_r, 0), (rw_k, 1), (rw_a, 1)):
                            O.step(dve.tensor_tensor(x[:, w, c], x[:, w, c], e[i], ALU.mult))
                        signal(dve.tensor_tensor(rw_kap[:, w, c], rw_kap[:, w, c], e[2], ALU.mult),
                               event(s, "decayed"), 2 * b + w + 1)

                O.settle()
                def finish_heads(t, b, part):
                    c, h8 = slice(b * COLS, (b + 1) * COLS), slice(8 * b, 8 * b + 8)
                    mean, rstd_, var, bon = hstat[:, 0, t, h8], hstat[:, 1, t, h8], hstat[:, 2, t, h8], bonus[:, t, h8]
                    y, tmp = xn[:, t, c], rw_r[:, t, c]
                    sq = rw_k[:, t, c] if t else tmp

                    def by_h(x):
                        return x.rearrange("p (h c) -> p h c", c=64)

                    def each(x):
                        return x.unsqueeze(2).broadcast_to([P, 8, 64])

                    def then(ins):
                        O.step(ins)
                        O.settle()

                    if part == 0:
                        for g in (2 * b, 2 * b + 1):
                            consumed(dve, s, "y", t, g)
                        then(dve.tensor_reduce(mean, by_h(y), X, ALU.add))
                        then(dve.tensor_scalar(mean, mean, 1.0 / 64, None, ALU.mult))
                        then(dve.tensor_tensor(by_h(y), by_h(y), each(mean), ALU.subtract))
                    elif part == 1:
                        then(dve.tensor_tensor(sq, y, y, ALU.mult))
                        then(dve.tensor_reduce(var, by_h(sq), X, ALU.add))
                        signal(dve.tensor_scalar(var, var, 1.0 / 64, 64e-5, ALU.mult, ALU.add),
                               event(s, "group%d%d_mean" % (t, b)), 1)
                    elif part == 2:
                        then(dve.tensor_tensor(by_h(tmp), by_h(rw_v[:, t, c]), each(bon), ALU.mult))
                    elif part == 3:
                        then(dve.tensor_tensor(tmp, tmp, use_row(s, "rw_ln_b")[:, c], ALU.add))
                    elif part == 4:
                        dve.wait_ge(event(s, "group%d%d_rstd" % (t, b)), 1)
                        then(dve.tensor_tensor(by_h(y), by_h(y), each(rstd_), ALU.mult))
                        then(dve.tensor_tensor(y, y, use_row(s, "rw_ln_w")[:, c], ALU.mult))
                    else:
                        then(dve.tensor_tensor(y, y, tmp, ALU.add))
                        signal(dve.tensor_tensor(y, y, rw_gate[:, t, c], ALU.mult),
                               event(s, "gated"), 2 * t + b + 1)

                dve.wait_ge(ld_tables, 16)
                for w in range(TT):
                    for gg in range(2):
                        pair = (2 * gg, 2 * gg + 1)
                        for g in pair:
                            a_, t_ = ab[:, g % 2], inv[:, g % 2]
                            for par in range(2):
                                it = slice(2 * par, 2 * par + 2)
                                for what, j in (("ab", 0), ("ak", 2)):
                                    ready(dve, s, what, w, g, par)
                                    frees_bank(dve.tensor_tensor(
                                        a_[:, it, j:j + 2, :].rearrange("p i j c -> p i (j c)"),
                                        B(s, what, w, g, par)[:, :].rearrange("p (i c) -> p i c", i=2),
                                        over(C("strict_incl"), 2), ALU.mult), s, what, w, g, par)
                            dve.wait_ge(event(s, "level_a"), level_no(w, g, 0))
                            signal(dve.tensor_tensor(t_[:, 1], over(ident, 4), level_a[:, g % 2, :, :], ALU.subtract),
                                   event(s, "inverse_begun"), 4 * w + g + 1)
                        for l in range(1, 7):
                            for g in pair:
                                ready(dve, s, "tx", w, g, l)
                                t_ = inv[:, g % 2, l // 6]
                                frees_bank(dve.tensor_tensor(
                                    t_, t_, B(s, "tx", w, g, l)[:, :].rearrange("p (i c) -> p i c", i=4),
                                    ALU.subtract), s, "tx", w, g, l)
                            if (w, gg, l) == (1, 1, 4):
                                lo_parts((s, "o", 0))
                            if w:
                                for t, b in (((0, 0), (0, 1)), ((1, 0),))[gg]:
                                    finish_heads(t, b, l - 1)
                for part in (2, 3, 0, 1, 4, 5):
                    finish_heads(1, 1, part)
                release_row()
                release_row()
                activations(s, "rwo")
                lo_parts((s, "o", 1))
                for b in range(2):
                    add_to_h((s, "o", b), b * COLS)
                    gain_next(s, b)

            h_done(dve, None)
            for b in range(2):
                gain_next(None, b)
            for s in STAGES:
                if s == "rw":
                    rwkv(s)
                elif s in ("ple0", "ple1"):
                    lo_parts((s, "p", 0))
                    take_lo(s, "turn_p", 0)
                    activations(s)
                    lo_parts((s, "p", 1))
                    mean_square(s)
                    lo_parts((s, "g", 0))
                    for b in range(2):
                        lo_parts((s, "g", b))
                        for t in range(TT):
                            c = slice(b * COLS, (b + 1) * COLS)
                            consumed(dve, (s, "g", b), t)
                            O.step(dve.tensor_tensor(sig[:, t, c], sig[:, t, c], p_out[:, t, c], ALU.mult))
                            O.settle()
                            signal(dve.tensor_tensor(h[:, t, c], h[:, t, c], sig[:, t, c], ALU.add),
                                   event(s, "added"), b * TT + t + 1)
                        gain_next(s, b)
                elif s == "final":
                    norm(s, h, "normed")
                    for b in range(2):
                        gain_next(s, b)
                elif s == "da":
                    lo_parts((s, 0))
                    activations(s)
                    mean_square(s)

                    def rotate(i, t):
                        x = (q_tok, k_tok)[i]
                        if t == 0:
                            for b in range(2):
                                consumed(dve, (s, 2 * i + b), TT - 1)
                        xv = x[:, t, :].rearrange("p (g c) -> p g c", c=64)
                        rv = rot[:, t, :].rearrange("p (g c) -> p g c", c=64)
                        cos = C("cos")[:, t * 64:(t + 1) * 64].unsqueeze(1).broadcast_to([P, 16, 64])
                        sin = C("sin")[:, t * 64:(t + 1) * 64].unsqueeze(1).broadcast_to([P, 16, 64])
                        O.step(dve.tensor_tensor(rv[:, :, 0:32], xv[:, :, 32:64], sin[:, :, 0:32], ALU.mult))
                        O.step(dve.tensor_tensor(rv[:, :, 32:64], xv[:, :, 0:32], sin[:, :, 32:64], ALU.mult))
                        O.settle()
                        O.step(dve.tensor_tensor(xv, xv, cos, ALU.mult))
                        O.settle()
                        signal(dve.tensor_tensor(x[:, t, :], x[:, t, :], rot[:, t, :], ALU.add),
                               event(s, "roped"), 2 * i + t + 1)

                    for i in range(3):
                        lo_parts((s, i))
                    rotate(0, 0)
                    lo_parts((s, 3))
                    rotate(0, 1)
                    lo_parts((s, 4))
                    dve.wait_ge(ld_da, 16 * 5)
                    O.step(dve.tensor_tensor(lq[:, 0:4:2, :], lq[:, 0:4:2, :], lq[:, 1:4:2, :], ALU.mult))
                    O.settle()
                    signal(dve.tensor_reduce(lam[:, 0:2], lq[:, 0:4:2, :], X, ALU.add), event(s, "lq_dots"), 1)
                    O.step(dve.tensor_scalar(subln[:, :], subln[:, :], 1.0 - LAMBDA_INIT, None, ALU.mult))
                    dve.wait_ge(event(s, "lq_exp"), 1)
                    O.step(dve.tensor_tensor(lam[:, 4:5], lam[:, 2:3], lam[:, 3:4], ALU.subtract))
                    O.settle()
                    O.step(dve.tensor_scalar(lam[:, 5:6], lam[:, 4:5], -1.0, -LAMBDA_INIT, ALU.mult, ALU.add))

                    rotate(1, 0)
                    lo_parts((s, 5))
                    rotate(1, 1)
                    lo_parts((s, 6))
                    lo_parts((s, 7))

                    consumed(dve, (s, 7), TT - 1)
                    gv = gate[:, :, :].rearrange("p t (h c) -> p (t h) c", c=P)
                    O.settle()
                    signal(dve.tensor_tensor(gv, gv, subln[:, :].unsqueeze(1).broadcast_to([P, 16, P]), ALU.mult),
                           event(s, "gate_gained"), 1)

                    def heads_mean(b):
                        dve.wait_ge(event(s, "head_squares"), 8 * (b + 1))
                        c = slice(8 * b, 8 * b + 8)
                        signal(dve.tensor_scalar(da_stat[:, 0, c], da_stat[:, 0, c], 1.0 / P, 1e-5, ALU.mult, ALU.add),
                               event(s, "head_mean"), b + 1)

                    def heads_scaled(b):
                        dve.wait_ge(event(s, "head_gated"), 4 * (b + 1))
                        dve.wait_ge(event(s, "head_rstd"), b + 1)
                        for t in range(TT):
                            xv = xn[:, t, b * COLS:(b + 1) * COLS].rearrange("p (h c) -> p h c", c=P)
                            n = 8 * b + 4 * t
                            signal(dve.tensor_tensor(xv, xv, da_stat[:, 1, n:n + 4].unsqueeze(2).broadcast_to(
                                [P, 4, P]), ALU.mult), event(s, "heads"), 2 * b + t + 1)

                    for u in range(8 * TT + 1):
                        if u < 8 * TT:
                            hd, qt = u // TT, u % TT
                            n = (qt + 1) * P
                            for c in range(2):
                                ready(dve, s, "s", hd, qt, c)
                                O.step(dve.tensor_reduce(sm[:, u, c:c + 1], B(s, "s", hd, qt, c)[:, 0:n], X, ALU.max))
                            O.settle()
                            signal(dve.tensor_scalar(sm[:, u, 2:4], sm[:, u, 0:2], -(64 ** -0.5), None, ALU.mult),
                                   event(s, "max"), u + 1)
                        if u == 12:
                            lo_parts((s, "out", 0), PART_SLOTS - 1)
                        if u == 11:
                            heads_mean(0)
                        if u:
                            v = u - 1
                            hd, qt = v // TT, v % TT
                            n = (qt + 1) * P
                            for c in range(2):
                                consumed(dve, s, "s", hd, qt, c)
                            O.step(dve.reciprocal(sm[:, v, 6:8], sm[:, v, 4:6]))
                            O.settle()
                            O.step(dve.tensor_scalar(sm[:, v, 7:8], sm[:, v, 7:8], lam[:, 5:6], None, ALU.mult))
                            O.settle()
                            O.step(dve.tensor_scalar(expo[:, v % 2, 1, 0:n], expo[:, v % 2, 1, 0:n], sm[:, v, 7:8],
                                                     None, ALU.mult))
                            O.settle()
                            if hd >= 2 and qt == 0:
                                ready(dve, s, "at", hd - 2)
                            signal(dve.scalar_tensor_tensor(out=att[:, hd % 2, qt, 0:n], in0=expo[:, v % 2, 0, 0:n],
                                                            scalar=sm[:, v, 6:7], in1=expo[:, v % 2, 1, 0:n],
                                                            op0=ALU.mult, op1=ALU.add), event(s, "att"), v + 1)
                        if u == 15:
                            heads_scaled(0)
                    heads_mean(1)
                    heads_scaled(1)
                    lo_parts((s, "out", 0))
                    activations(s, "dao")
                    lo_parts((s, "out", 1))
                    for b in range(2):
                        add_to_h((s, "out", b), b * COLS)
                        gain_next(s, b)
                elif s == "ssm":
                    norm(s, xn, "scaled")
                    lo_parts((s, "dt"))
                    activations(s)
                    signal(dve.memset(conv_in[:, :, :, 0:3], 0.0), event(s, "padded"), 1)
                    raw_, nabs, ex, lg, one_, dt, dta, nacum = (dts[:, i] for i in range(8))
                    dve.wait_ge(ld_ssm, 16 * 5)
                    for t in range(TT):
                        ready(dve, (s, "dt"), t)
                        frees_bank(dve.tensor_tensor(raw_[:, t, :], B((s, "dt"), t)[:, 0:SSM_H],
                                                     per_head_in[:, 0, :], ALU.add), (s, "dt"), t)
                    O.settle()
                    O.step(dve.tensor_scalar(lg, raw_, -1.0, None, ALU.mult))
                    O.settle()
                    signal(dve.tensor_tensor(nabs, raw_, lg, ALU.min), event(s, "dt_minus_abs"), 1)
                    lo_parts((s, "z", 0))
                    dve.wait_ge(event(s, "dt_log"), 1)
                    O.step(dve.tensor_scalar(one_, ex, 1.0, None, ALU.add))
                    O.settle()
                    O.step(dve.scalar_tensor_tensor(out=ex, in0=one_, scalar=-1.0, in1=ex, op0=ALU.add,
                                                    op1=ALU.subtract))
                    O.step(dve.reciprocal(one_, one_))
                    O.settle()
                    O.step(dve.tensor_tensor(ex, ex, one_, ALU.mult))
                    O.settle()
                    O.step(dve.tensor_tensor(lg, lg, ex, ALU.subtract))
                    O.settle()
                    O.step(dve.scalar_tensor_tensor(out=dt, in0=raw_, scalar=0.0, in1=lg, op0=ALU.max,
                                                    op1=ALU.add))
                    O.settle()
                    dve.wait_ge(event(s, "a"), 1)
                    for t in range(TT):
                        signal(dve.scalar_tensor_tensor(out=dta[:, t, :], in0=dt[:, t, :], scalar=-1.0,
                                                        in1=per_head_in[:, 1, :], op0=ALU.mult, op1=ALU.mult),
                               event(s, "dta"), t + 1)
                    for i in range(1, 4):
                        lo_parts((s, "z", i))
                    lo_parts((s, "xb", CONV_ORDER[0]))
                    ready(dve, s, "acum")
                    sums = B(s, "acum")[:, 0:TT * SSM_H].rearrange("p (t h) -> p t h", t=TT)
                    signal(dve.tensor_scalar(nacum, sums, -1.0, None, ALU.mult), event(s, "sums_negated"), 1)
                    dve.wait_ge(event(s, "sums_negated"), 1)
                    frees_bank(dve.tensor_scalar(one_, sums, 1.0, None, ALU.mult), s, "acum")
                    O.settle()
                    dve.sem_inc(event(s, "sums_negated"), 1)
                    for n, i in enumerate(CONV_ORDER):
                        for j in range(2):
                            consumed(dve, (s, "xb", i), j)
                            m = 2 * n + j
                            if m >= 2:
                                dve.wait_ge(event(s, "conv_out"), 2 * (m - 1))
                                prev = CONV_ORDER[n - 1]
                                if prev < 4:
                                    ready(dve, s, "xt", prev, j)
                            for k in range(4):
                                if k:
                                    O.settle()
                                for c in range(2):
                                    tile_ = 4 * i + 2 * j + c
                                    src, dst = conv_in[:, j, c, k:k + T], conv_sum[:, j, c, :]
                                    w_ = conv_w[:, tile_, k:k + 1]
                                    if k == 0:
                                        ins = dve.tensor_scalar(dst, src, w_, None, ALU.mult)
                                    else:
                                        ins = dve.scalar_tensor_tensor(out=dst, in0=src, scalar=w_, in1=dst,
                                                                       op0=ALU.mult, op1=ALU.add)
                                    if k < 3 or c == 0:
                                        O.step(ins)
                            signal(ins, event(s, "convolved"), m + 1)
                            if n < 5:
                                lo_parts((s, "xb", CONV_ORDER[n + 1]), j + 1)
                    for g in range(4):
                        ready(dve, s, "cb", g)
                        O.step(dve.tensor_tensor(cb[:, g, 0:T], B(s, "cb", g)[:, 0:T], C("tri"), ALU.mult))
                        frees_bank(dve.tensor_tensor(cb[:, g, T:T + P], B(s, "cb", g)[:, T:T + P],
                                                     C("tri")[:, 0:P], ALU.mult), s, "cb", g)
                    for j in range(2):
                        consumed(dve, s, "xt", 3, j)

                    def group_mean(g):
                        dve.wait_ge(event(s, "group_squares"), 2 * g + 2)
                        signal(dve.tensor_scalar(ss_stat[:, 0, 2 * g:2 * g + 2], ss_stat[:, 0, 2 * g:2 * g + 2],
                                                 1.0 / COLS, 1e-6, ALU.mult, ALU.add), event(s, "group_mean"), g + 1)

                    def group_scale(g):
                        if g % 2 == 0:
                            gain[0] = use_row(s, "gate_norm%d" % (g // 2))
                        dve.wait_ge(event(s, "group_rstd"), g + 1)
                        c = slice(g * COLS, (g + 1) * COLS)
                        half = slice(g % 2 * COLS, (g % 2 + 1) * COLS)
                        for t in range(TT):
                            signal(dve.scalar_tensor_tensor(out=y_tok[:, t, c], in0=y_tok[:, t, c],
                                                            scalar=ss_stat[:, 1, 2 * g + t:2 * g + t + 1],
                                                            in1=gain[0][:, half], op0=ALU.mult, op1=ALU.mult),
                                   event(s, "y_scaled"), 2 * g + t + 1)
                        if g % 2:
                            release_row()

                    gain = [None]
                    for u in range(SSM_H // 2 + 2):
                        if u < SSM_H // 2:
                            ready(dve, s, "seg", u, 0)
                            if u >= 3:
                                ready(dve, s, "y", u - 3)
                            for lo2, n2, t in ((0, T, 0), (T, P, 1)):
                                ins = dve.tensor_scalar(seg_slot[u % 3][:, 0, lo2:lo2 + n2],
                                                        B(s, "seg", u, 0)[:, t * P:t * P + n2],
                                                        nacum[:, t, 2 * u:2 * u + 1], 0.0, ALU.add, ALU.min)
                                if t == 0:
                                    O.step(ins)
                            frees_bank(ins, s, "seg", u, 0)
                            O.settle()
                            dve.sem_inc(event(s, "seg"), 1)
                        if u and u <= SSM_H // 2:
                            v = u - 1
                            dve.wait_ge(event(s, "seg_exp"), v + 1)
                            signal(dve.tensor_tensor(seg_slot[v % 3], seg_slot[v % 3], over(cb[:, v // 4, :], 2),
                                                     ALU.mult), event(s, "weights"), v + 1)
                        if u % 4 == 0 and u >= 8:
                            group_mean(u // 4 - 2)
                        if u >= 2:
                            v = u - 2
                            ready(dve, s, "y", v)
                            dve.wait_ge(event(s, "x_d"), 2 * (v // 4 + 1))
                            c = slice(v * P, (v + 1) * P)
                            ins = dve.tensor_tensor(y_tok[:, :, c], B(s, "y", v)[:, 0:T].rearrange(
                                "p (t c) -> p t c", t=TT), xs_tok[:, :, c], ALU.add)
                            frees_bank(ins, s, "y", v)
                            O.settle()
                            dve.sem_inc(event(s, "y_sum"), 1)
                        if u in (5, 7, 9):
                            lo_parts((s, "out", 0), (u - 3) // 2)
                        if u % 4 == 1 and u >= 9:
                            group_scale(u // 4 - 2)
                    group_mean(3)
                    group_scale(3)
                    activations(s, "ssmo", 8)
                    for b in range(2):
                        lo_parts((s, "out", b))
                    for b in range(2):
                        add_to_h((s, "out", b), b * COLS)
                        gain_next(s, b)
                elif s == "kv":
                    h_done(dve, stage_before.get(s))
                    signal(dve.memset(rel[32:33, :], 1.0), event(s, "rel_one"), 1)
                    ready(dve, s, "bias")
                    frees_bank(dve.tensor_copy(bias_rows[:, :], B(s, "bias")[0:16, 0:BIAS_N]), s, "bias")
                    lo_parts((s, "kv"))
                    activations(s)
                    mean_square(s)
                    for b in range(2):
                        gain_next(s, b)
                    dve.wait_ge(ld_kv, 16 * 3)
                    for t in range(TT):
                        ready(dve, (s, "kv"), t)
                        O.step(dve.tensor_scalar(k_tmp[:, t, :, 0, :],
                                                 B((s, "kv"), t)[:, 0:P].rearrange("p (h c) -> p h c", c=64),
                                                 rstd(s, t), None, ALU.mult))
                        frees_bank(dve.tensor_scalar(v_tmp[:, t, :], B((s, "kv"), t)[:, P:2 * P], rstd(s, t),
                                                     None, ALU.mult), (s, "kv"), t)
                    O.settle()
                    for t in range(TT):
                        O.step(dve.tensor_tensor(k_sq[:, t, :, :], k_tmp[:, t, :, 0, :], k_tmp[:, t, :, 0, :],
                                                 ALU.mult))
                    O.settle()
                    O.step(dve.tensor_reduce(sw_stat[:, 0, 0:4], k_sq[:, :, :, :].rearrange("p t h c -> p (t h) c"),
                                             X, ALU.add))
                    O.settle()
                    signal(dve.tensor_scalar(sw_stat[:, 0, 0:4], sw_stat[:, 0, 0:4], 1.0 / 64, 1e-6, ALU.mult,
                                             ALU.add), event(s, "head_mean"), 1)
                    dve.wait_ge(event(s, "head_rstd"), 1)
                    for t in range(TT):
                        for g in range(2):
                            O.step(dve.scalar_tensor_tensor(out=k_tmp[:, t, g, 0, :], in0=k_tmp[:, t, g, 0, :],
                                                            scalar=sw_stat[:, 1, 2 * t + g:2 * t + g + 1],
                                                            in1=k_norm[:, :], op0=ALU.mult, op1=ALU.mult))
                    O.settle()
                    signal(dve.tensor_copy(k_tmp[:, :, :, 1, :].rearrange("p t h c -> p (t h) c"),
                                           k_tmp[:, :, :, 0, :].rearrange("p t h c -> p (t h) c")),
                           event(s, "keys"), 1)
                elif s == "swa":
                    lo_parts((s, "q", 0))
                    activations(s)
                    mean_square(s)
                    lo_parts((s, "q", 1))
                    dve.wait_ge(ld_swa, 32)

                    def queries_scaled(b):
                        dve.wait_ge(event(s, "head_rstd"), b + 1)
                        O.settle()
                        signal(dve.tensor_tensor(per_head(sq_tok, b), per_head(sq_tok, b),
                                                 per_head(sw_stat, b)[:, 1].unsqueeze(3).broadcast_to([P, TT, 8, 64]),
                                                 ALU.mult), event(s, "queries"), b + 1)

                    def per_head(x, b):
                        if x is sw_stat:
                            return x[:, :, 16 * b:16 * b + 16].rearrange("p i (t h) -> p i t h", t=TT)
                        return x[:, :, b * COLS:(b + 1) * COLS].rearrange("p t (h c) -> p t h c", c=64)

                    for b in range(2):
                        consumed(dve, (s, "q", b), TT - 1)
                        c = slice(b * COLS, (b + 1) * COLS)
                        O.step(dve.tensor_tensor(xn[:, :, c], sq_tok[:, :, c], sq_tok[:, :, c], ALU.mult))
                        O.settle()
                        O.step(dve.tensor_reduce(per_head(sw_stat, b)[:, 0], per_head(xn, b), X, ALU.add))
                        O.settle()
                        sums = sw_stat[:, 0, 16 * b:16 * b + 16]
                        signal(dve.tensor_scalar(sums, sums, 1.0 / 64, 1e-6, ALU.mult, ALU.add),
                               event(s, "head_mean"), b + 1)
                        for t in range(TT):
                            q8 = per_head(sq_tok, b)[:, t]
                            O.step(dve.tensor_tensor(q8, q8, over(q_norm[:, :], 8), ALU.mult))
                        if b:
                            queries_scaled(b - 1)
                    queries_scaled(1)
                    dve.wait_ge(ld_bias, 32)
                    for u in range(8 * TT + 1):
                        if u < 8 * TT:
                            pr, qt = u // TT, u % TT
                            n = (qt + 1) * P
                            if u >= 2:
                                dve.wait_ge(event(s, "exp"), 3 * (u - 1))
                            for c in range(2):
                                ready(dve, s, "s", pr, qt, c)
                                frees_bank(dve.scalar_tensor_tensor(
                                    out=s_sc[:, u % 2, c, 0:n], in0=B(s, "s", pr, qt, c)[:, 0:n], scalar=64 ** -0.5,
                                    in1=bias[:, 2 * pr + c, 0:n], op0=ALU.mult, op1=ALU.add), s, "s", pr, qt, c)
                            O.settle()
                            m_, sink = s_sm[:, u, 6:8], sinks[:, 2 * pr:2 * pr + 2]
                            O.step(dve.tensor_reduce(m_, s_sc[:, u % 2, :, 0:n], X, ALU.max))
                            O.settle()
                            O.step(dve.tensor_tensor(m_, m_, sink, ALU.max))
                            O.settle()
                            O.step(dve.tensor_scalar(s_sm[:, u, 2:4], m_, -1.0, None, ALU.mult))
                            signal(dve.tensor_tensor(s_sm[:, u, 0:2], sink, m_, ALU.subtract), event(s, "max"), u + 1)
                        if u == 12:
                            lo_parts((s, "out", 0), PART_SLOTS - 1)
                        if u:
                            v = u - 1
                            pr, qt = v // TT, v % TT
                            n = (qt + 1) * P
                            dve.wait_ge(event(s, "exp"), 3 * (v + 1))
                            O.step(dve.tensor_tensor(s_sm[:, v, 4:6], s_sm[:, v, 4:6], s_sm[:, v, 0:2], ALU.add))
                            O.settle()
                            O.step(dve.reciprocal(s_sm[:, v, 6:8], s_sm[:, v, 4:6]))
                            O.settle()
                            for c in range(2):
                                w_ = s_pr[:, pr % 2, qt, c, 0:n]
                                signal(dve.tensor_scalar(w_, w_, s_sm[:, v, 6 + c:7 + c], None, ALU.mult),
                                       event(s, "att"), 2 * v + c + 1)
                    lo_parts((s, "out", 0))
                    activations(s, "swao")
                    lo_parts((s, "out", 1))
                    for b in range(2):
                        add_to_h((s, "out", b), b * COLS)
                        gain_next(s, b)
                elif s.startswith("ffn"):
                    lo_parts((s, "u", 0))
                    activations(s)
                    mean_square(s)
                    blocks = ffn_blocks()

                    def gated(b):
                        if b >= 2:
                            ready(dve, s, "gt", b - 2, blocks[b - 2][1] // 256 - 1)
                        for t in range(TT):
                            consumed(dve, (s, "u", b), t)
                            ready(dve, (s, "v", b), t)
                            cols = blocks[b][1]
                            frees_bank(dve.scalar_tensor_tensor(
                                out=g_tok[:, b % 2, t, 0:cols], in0=B((s, "v", b), t)[:, 0:cols],
                                scalar=rstd(s, t), in1=silu[:, t, 0:cols], op0=ALU.mult, op1=ALU.mult),
                                (s, "v", b), t)

                    def gated_lo(b):
                        for i in range(blocks[b][1] // 256):
                            take_lo(s, "gt", b, i)

                    for b in range(len(blocks)):
                        lo_parts((s, "u", b))
                        if b:
                            gated(b - 1)
                        lo_parts((s, "v", b))
                        if b:
                            gated_lo(b - 1)
                    lo_parts((s, "d", 0), 2)
                    gated(len(blocks) - 1)
                    gated_lo(len(blocks) - 1)
                    for b in range(2):
                        lo_parts((s, "d", b))
                    for b in range(2):
                        add_to_h((s, "d", b), b * COLS, 0.5)
                        gain_next(s, b)

        @block.tensor
        def _(pe):
            nth = [0]

            def begin(*name):
                assert jobs[name] == nth[0], (name, jobs[name], nth[0])
                nth[0] += 1
                if jobs[name] >= BANKS:
                    pe.wait_ge(bank_free[jobs[name] % BANKS], jobs[name] // BANKS)
                return B(*name)

            def end(ins):
                ins.then_inc(psum_ready, 1)

            def gemm(name, hi, lo_, need=None):
                first, last, cols = gemms[name]
                outs = [begin(name, t) for t in range(TT)]
                k_end = slabs[last - 1][1] + slabs[last - 1][2]
                for n in range(first, last):
                    _, k0, kn, _, _, release = slabs[n]
                    pe.wait_ge(slab_hi, n + 1)
                    pe.wait_ge(slab_lo, n + 1)
                    if need:
                        need(k0, kn)
                    for t in range(TT):
                        for k in range(k0, k0 + kn):
                            a_hi, a_lo = hi[:, k, t * P:(t + 1) * P], lo_[:, k, t * P:(t + 1) * P]
                            b_hi = w_hi[:, n % PART_SLOTS, k - k0, 0:cols]
                            b_lo = w_lo[:, n % PART_SLOTS, k - k0, 0:cols]
                            pe.matmul(outs[t][:, 0:cols], a_hi, b_hi, start=(k == 0), stop=False)
                            pe.matmul(outs[t][:, 0:cols], a_lo, b_hi, start=False, stop=False)
                            mm = pe.matmul(outs[t][:, 0:cols], a_hi, b_lo, start=False, stop=(k == k_end - 1))
                        if n == last - 1:
                            end(mm)
                    if n < last - 1:
                        mm.then_inc(slab_used, 1)

            def gemm_by_channel(name, hi, lo_, between):
                first = gemms[name][0]
                for j in range(2):
                    o = begin(name, j)
                    for c in range(2):
                        dst, cols = o[:, c * T:(c + 1) * T], slice(c * P, (c + 1) * P)
                        for k in range(KD):
                            n, in_slab = first + j, k
                            if c == 0 and in_slab == 0:
                                pe.wait_ge(slab_hi, n + 1)
                                pe.wait_ge(slab_lo, n + 1)
                            a = slab_in(w_hi, n % PART_SLOTS, n)[:, in_slab, cols]
                            b = slab_in(w_lo, n % PART_SLOTS, n)[:, in_slab, cols]
                            pe.matmul(dst, a, hi[:, k, :], start=(k == 0), stop=False)
                            pe.matmul(dst, a, lo_[:, k, :], start=False, stop=False)
                            mm = pe.matmul(dst, b, hi[:, k, :], start=False, stop=(k == KD - 1))
                    end(mm)
                    between(j)

            def turn(name, src, k0, nk=2):
                o = begin(*name)
                for k in range(nk):
                    for t in range(TT):
                        c = (k0 + k) * P
                        mm = pe.transpose(o[:, (k * TT + t) * P:(k * TT + t + 1) * P], src[:, t, c:c + P], ident)
                end(mm)

            def turn_activations(s, tag=None, wait=None):
                if wait:
                    wait()
                for i in range(4):
                    if wait is None and i % 2 == 0:
                        pe.wait_ge(event(s, "scaled"), 2 * (i // 2 + 1) if s in DEFERRED else TT)
                    turn((tag or s, "turn", i), xn, 2 * i)

            def turned(tag):
                def need(k0, kn):
                    for i in range(k0 // 2, (k0 + kn + 1) // 2):
                        consumed(pe, tag, "turn", i)
                return need

            def low_rank(s):
                pe.wait_ge(ld_lora, 16 * 6)
                for i, x in enumerate("wa"):
                    pe.wait_ge(event(s, "lora_mixed"), i + 1)
                    o = begin(s, "lora_in", x)
                    for k in range(KD):
                        mm = pe.matmul(o[0:64, 0:T], lora_w1[:, i, k, :], (mix_s, mix_v)[i][:, k, :],
                                       start=(k == 0), stop=(k == KD - 1))
                    end(mm)
                for i, x in enumerate("wa"):
                    consumed(pe, s, "lora_in", x)
                    for b in range(2):
                        for t in range(TT):
                            o = begin(s, "lora_out", x, b, t)
                            end(pe.matmul(o[:, :], lora_t[0:65, i, t * P:(t + 1) * P],
                                          rw_kap[0:65, i, b * COLS:(b + 1) * COLS], start=True, stop=True))

            def rwkv(s):
                turn_activations(s)
                for i, x in enumerate("rkvg"):
                    pe.wait_ge(event(s, "mix_lo"), i + 1)
                    for b in range(2):
                        gemm((s, x, b), x_hi[i % 2], x_lo[i % 2])
                    if x == "k":
                        low_rank(s)
                pe.wait_ge(ld_tables, 16)
                consumed(pe, s, "lora_out", "w", 1, 1)
                for b in range(2):
                    for w in range(TT):
                        for what in ("cum", "cumx"):
                            o = begin(s, what, b, w)
                            end(pe.matmul(o[:, :], C(what), rw_sig[:, w, b * COLS:(b + 1) * COLS],
                                          start=True, stop=True))
                o = begin(s, "carry")
                for pr in range(8):
                    for w in range(TT):
                        mm = pe.matmul(o[:, pr:pr + 1], rw_sig[:, w, pr * P:(pr + 1) * P], C("ends")[:, w:w + 1],
                                       start=(w == 0), stop=(w == 1))
                end(mm)

                def turn_four(name, src):
                    o = begin(s, *name)
                    for it in range(4):
                        mm = pe.transpose(o[:, it * P:(it + 1) * P], src[:, it, :], ident)
                    end(mm)

                for w in range(TT):
                    for gg in range(2):
                        pair = (2 * gg, 2 * gg + 1)
                        for g in pair:
                            pe.wait_ge(event(s, "decayed"), 4 if g >= 2 or w else 2)
                            for pp in range(2):
                                o = begin(s, "ct", w, g, pp)
                                c = (2 * g + pp) * P
                                for i, x in enumerate((rw_kap, rw_r, rw_a, rw_k)):
                                    mm = pe.transpose(o[:, i * P:(i + 1) * P], x[:, w, c:c + P], ident)
                                end(mm)
                            for par in range(2):
                                r_ = slice(64 * par, 64 * par + 64)
                                for what, l_ in (("ab", 2), ("ak", 3)):
                                    o = begin(s, what, w, g, par)
                                    for pp in range(2):
                                        consumed(pe, s, "ct", w, g, pp)
                                        mm = pe.matmul(o[:, pp * T:(pp + 1) * T], ct[r_, g % 2, pp, l_, :],
                                                       ct[r_, g % 2, pp, 0:2, :].rearrange("p i c -> p (i c)"),
                                                       start=True, stop=True)
                                    end(mm)
                            pe.wait_ge(event(s, "inverse_begun"), 4 * w + g + 1)
                            turn_four(("t0", w, g), inv[:, g % 2, 1])
                        for l in range(1, 7):
                            for g in pair:
                                if l == 1:
                                    consumed(pe, s, "t0", w, g)
                                else:
                                    consumed(pe, s, "tx", w, g, l - 1)
                                pe.wait_ge(event(s, "level_a"), level_no(w, g, l))
                                o = begin(s, "x", w, g, l)
                                for it in range(4):
                                    mm = pe.matmul(o[:, it * P:(it + 1) * P], level_a[:, g % 2, it, :],
                                                   inv[:, g % 2, 0, it, :], start=True, stop=True)
                                end(mm)
                            for g in pair:
                                x_, tt_ = x_sb[:, g % 2], inv[:, g % 2, 1]
                                consumed(pe, s, "x", w, g, l)
                                if l > 1:
                                    consumed(pe, s, "tt", w, g, l - 1)
                                o = begin(s, "tx", w, g, l)
                                for it in range(4):
                                    a_, b_ = (tt_[:, it, :], x_[:, it, :]) if l < 6 else (x_[:, it, :], tt_[:, it, :])
                                    mm = pe.matmul(o[:, it * P:(it + 1) * P], a_, b_, start=True, stop=True)
                                end(mm)
                            if l < 6:
                                for g in pair:
                                    consumed(pe, s, "tx", w, g, l)
                                    turn_four(("tt", w, g, l), inv[:, g % 2, 0])
                        for g in pair:
                            if w:
                                consumed(pe, s, "s", 0, g)
                            o = begin(s, "rhs", w, g)
                            for pp in range(2):
                                pr = 2 * g + pp
                                if w:
                                    pe.matmul(o[:, pp * P:(pp + 1) * P], ct[:, g % 2, pp, 0, :], state[:, pr, :],
                                              start=True, stop=False)
                                for par in range(2):
                                    c = 64 * par
                                    mm = pe.matmul(o[:, pp * P + c:pp * P + c + 64], ab[:, g % 2, 2 * par + pp, 2, :],
                                                   rw_v[:, w, pr * P + c:pr * P + c + 64], start=(w == 0),
                                                   stop=(w == 0 or par == 1))
                            end(mm)
                        for g in pair:
                            consumed(pe, s, "rhs", w, g)
                            consumed(pe, s, "tx", w, g, 6)
                            o = begin(s, "u", w, g)
                            for pp in range(2):
                                for par in range(2):
                                    c = 64 * par
                                    mm = pe.matmul(o[:, pp * P + c:pp * P + c + 64], inv[:, g % 2, 1, 2 * par + pp, :],
                                                   rhs_sb[:, g % 2, pp, c:c + 64], start=True, stop=True)
                            end(mm)
                        for g in pair:
                            consumed(pe, s, "u", w, g)
                            o = begin(s, "y", w, g)
                            for pp in range(2):
                                pr = 2 * g + pp
                                if w:
                                    pe.matmul(o[:, pp * P:(pp + 1) * P], ct[:, g % 2, pp, 1, :], state[:, pr, :],
                                              start=True, stop=False)
                                for par in range(2):
                                    c = 64 * par
                                    dst = o[:, pp * P + c:pp * P + c + 64]
                                    pe.matmul(dst, ab[:, g % 2, 2 * par + pp, 3, :],
                                              rw_v[:, w, pr * P + c:pr * P + c + 64], start=(w == 0), stop=False)
                                    mm = pe.matmul(dst, ab[:, g % 2, 2 * par + pp, 1, :],
                                                   un_sb[:, g % 2, pp, c:c + 64], start=False,
                                                   stop=(w == 0 or par == 1))
                            end(mm)
                            if w == 0:
                                o = begin(s, "s", w, g)
                                for pp in range(2):
                                    c = slice((2 * g + pp) * P, (2 * g + pp + 1) * P)
                                    pe.matmul(o[:, pp * P:(pp + 1) * P], rw_k[:, 0, c], rw_v[:, 0, c],
                                              start=True, stop=False)
                                    mm = pe.matmul(o[:, pp * P:(pp + 1) * P], rw_a[:, 0, c], un_sb[:, g % 2, pp, :],
                                                   start=False, stop=True)
                                end(mm)
                for i in range(4):
                    pe.wait_ge(event(s, "gated"), 3 + i // 2)
                    turn(("rwo", "turn", i), xn, 2 * i)
                for b in range(2):
                    gemm((s, "o", b), x_hi[0], x_lo[0], turned("rwo"))

            pe.wait_ge(ld_const, 32)
            for s in STAGES:
                if s == "rw":
                    rwkv(s)
                elif s in ("ple0", "ple1"):
                    i = int(s[-1])
                    pe.wait_ge(ld_p, 16)
                    turn((s, "turn_p", 0), p_tok[:, i], 0)
                    turn_activations(s)
                    consumed(pe, s, "turn_p", 0)
                    for b in range(2):
                        gemm((s, "p", b), p_hi, p_lo)
                    for b in range(2):
                        gemm((s, "g", b), x_hi[0], x_lo[0], turned(s))
                elif s == "da":
                    turn_activations(s)
                    for i in range(8):
                        gemm((s, i), x_hi[0], x_lo[0], turned(s))
                    for i in range(8):
                        pe.wait_ge(event(s, "roped"), 2 * (i // 4) + TT)
                        turn((s, "qk", i), q_tok if i < 4 else k_tok, 2 * (i % 4))
                    consumed(pe, s, "qk", 7)

                    def weigh_values(hd):
                        pe.wait_ge(event(s, "att"), 2 * (hd + 1))
                        o = begin(s, "at", hd)
                        for i, (qt, kt) in enumerate(((0, 0), (1, 0), (1, 1))):
                            mm = pe.transpose(o[:, i * P:(i + 1) * P], att[:, hd % 2, qt, kt * P:(kt + 1) * P], ident)
                        end(mm)
                        consumed(pe, s, "at", hd)
                        o = begin(s, "o", hd)
                        v = [v_tok[:, kt, hd * P:(hd + 1) * P] for kt in range(2)]
                        a = att_ch[:, hd % 2]
                        pe.matmul(o[:, 0:P], a[:, 0, :], v[0], start=True, stop=True)
                        pe.matmul(o[:, P:2 * P], a[:, 1, :], v[0], start=True, stop=False)
                        end(pe.matmul(o[:, P:2 * P], a[:, 2, :], v[1], start=False, stop=True))

                    for hd in range(8):
                        for qt in range(TT):
                            for c in range(2):
                                o = begin(s, "s", hd, qt, c)
                                rows_ = slice(64 * c, 64 * c + 64)
                                pe.matmul(o[:, 0:(qt + 1) * P], q_ch[rows_, hd, qt * P:(qt + 1) * P],
                                          k_ch[rows_, hd, 0:(qt + 1) * P], start=True, stop=False)
                                end(pe.matmul(o[:, qt * P:(qt + 1) * P], ident, C("causal"), start=False, stop=True))
                        if hd:
                            weigh_values(hd - 1)
                    weigh_values(7)
                    for i in range(4):
                        pe.wait_ge(event(s, "heads"), 2 * (i // 2 + 1))
                        turn(("dao", "turn", i), xn, 2 * i)
                    for b in range(2):
                        gemm((s, "out", b), x_hi[0], x_lo[0], turned("dao"))
                elif s == "ssm":
                    turn_activations(s)
                    gemm((s, "dt"), x_hi[0], x_lo[0], turned(s))
                    dta = dts[:, 6]
                    for i in range(4):
                        gemm((s, "z", i), x_hi[0], x_lo[0])
                    pe.wait_ge(event(s, "dta"), TT)
                    o = begin(s, "acum")
                    tri, ones = C("tri")[:, 0:P], C("tri")[:, P:2 * P]
                    pe.matmul(o[:, 0:SSM_H], tri, dta[:, 0, :], start=True, stop=True)
                    pe.matmul(o[:, SSM_H:2 * SSM_H], ones, dta[:, 0, :], start=True, stop=False)
                    end(pe.matmul(o[:, SSM_H:2 * SSM_H], tri, dta[:, 1, :], start=False, stop=True))

                    def turn_conv(i, j):
                        if i not in range(4):
                            return
                        pe.wait_ge(event(s, "conv_out"), 2 * (2 * CONV_ORDER.index(i) + j + 1))
                        o = begin(s, "xt", i, j)
                        for t in range(TT):
                            for c in range(2):
                                m = (2 * t + c) * P
                                mm = pe.transpose(o[:, m:m + P], conv_sum[:, j, c, t * P:(t + 1) * P], ident)
                        end(mm)

                    before = None
                    for i in CONV_ORDER:
                        gemm_by_channel((s, "xb", i), x_hi[0], x_lo[0], lambda j: turn_conv(before, j))
                        before = i
                    for j in range(2):
                        turn_conv(before, j)
                    for g in range(4):
                        o = begin(s, "cb", g)
                        pe.matmul(o[:, 0:T], bc[:, g, 0:P], bc[:, 4 + g, :], start=True, stop=True)
                        end(pe.matmul(o[:, T:T + P], bc[:, g, P:T], bc[:, 4 + g, P:T], start=True, stop=True))
                    for u in range(SSM_H // 2 + 2):
                        if u < SSM_H // 2:
                            for c in range(2):
                                o = begin(s, "seg", u, c)
                                hd = 2 * u + c
                                col = [dta[:, t, hd:hd + 1].broadcast_to([P, P]) for t in range(TT)]
                                pe.matmul(o[:, 0:T], col[0], C("tri"), start=True, stop=False)
                                end(pe.matmul(o[:, P:T], col[1], tri, start=False, stop=True))
                        if u >= 2:
                            v = u - 2
                            pe.wait_ge(event(s, "x_dt"), v // 4 + 1)
                            pe.wait_ge(event(s, "weights"), v + 1)
                            o = begin(s, "y", v)
                            for c in range(2):
                                x_ = slice((2 * v + c) * 64, (2 * v + c + 1) * 64)
                                w_ = seg_slot[v % 3][:, c, :]
                                pe.matmul(o[:, c * 64:c * 64 + 64], w_[:, 0:P], y_tok[:, 0, x_], start=True, stop=True)
                                dst = o[:, P + c * 64:P + c * 64 + 64]
                                pe.matmul(dst, w_[:, P:T], y_tok[:, 0, x_], start=True, stop=False)
                                mm = pe.matmul(dst, w_[:, T:T + P], y_tok[:, 1, x_], start=False, stop=True)
                            end(mm)
                    for i in range(8):
                        pe.wait_ge(event(s, "y_scaled"), 2 * (i // 2 + 1))
                        turn(("ssmo", "turn", i), y_tok, 2 * i)
                    for b in range(2):
                        gemm((s, "out", b), y_hi, y_lo, turned("ssmo"))
                elif s == "kv":
                    pe.wait_ge(ld_kv, 16 * 3)
                    pe.wait_ge(event(s, "rel_one"), 1)
                    o = begin(s, "bias")
                    end(pe.matmul(o[0:16, 0:BIAS_N], rel[:, :], picks[:, :], start=True, stop=True))
                    turn_activations(s)
                    gemm((s, "kv"), x_hi[0], x_lo[0], turned(s))
                    for t in range(TT):
                        consumed(pe, (s, "kv"), t)
                    o = begin(s, "vt")
                    for t in range(TT):
                        m = (1 - t) * P
                        mm = pe.matmul(o[:, m:m + P], C("flip"), v_tmp[:, t, :], start=True, stop=True)
                    end(mm)
                    pe.wait_ge(event(s, "keys"), 1)
                    o = begin(s, "kt")
                    for g in range(2):
                        for t in range(TT):
                            m = (g * TT + 1 - t) * P
                            mm = pe.matmul(o[:, m:m + P], k_tmp[:, t, g, :, :].rearrange("p a c -> p (a c)"),
                                           C("flip"), start=True, stop=True)
                    end(mm)
                elif s == "swa":
                    turn_activations(s)
                    for b in range(2):
                        gemm((s, "q", b), x_hi[0], x_lo[0], turned(s))
                    for i in range(4):
                        pe.wait_ge(event(s, "queries"), i // 2 + 1)
                        turn((s, "qt", i), sq_tok, 2 * i)
                    consumed(pe, s, "qt", 3)
                    consumed(pe, "kv", "kt")

                    def window_values(pr):
                        pe.wait_ge(event(s, "att"), 4 * (pr + 1))
                        for par in range(2):
                            o = begin(s, "at", pr, par)
                            for i, (qt, kt) in enumerate(((0, 0), (1, 0), (1, 1))):
                                mm = pe.transpose(o[:, i * P:(i + 1) * P],
                                                  s_pr[:, pr % 2, qt, par, kt * P:(kt + 1) * P], ident)
                            end(mm)
                        o = begin(s, "o", pr)
                        for par in range(2):
                            consumed(pe, s, "at", pr, par)
                            g = pr // 4
                            v = [kv_v[:, kt, 64 * g:64 * g + 64] for kt in range(2)]
                            c = 64 * par
                            pe.matmul(o[:, c:c + 64], s_at[:, par, 0, :], v[1], start=True, stop=True)
                            pe.matmul(o[:, P + c:P + c + 64], s_at[:, par, 1, :], v[0], start=True, stop=False)
                            mm = pe.matmul(o[:, P + c:P + c + 64], s_at[:, par, 2, :], v[1], start=False, stop=True)
                        end(mm)

                    for pr in range(8):
                        for qt in range(TT):
                            for par in range(2):
                                o = begin(s, "s", pr, qt, par)
                                r_ = slice(64 * par, 64 * par + 64)
                                end(pe.matmul(o[:, 0:(qt + 1) * P], sq_ch[r_, pr, qt * P:(qt + 1) * P],
                                              kv_k[r_, pr // 4, (1 - qt) * P:T], start=True, stop=True))
                        if pr:
                            window_values(pr - 1)
                    window_values(7)
                    turn_activations(s, "swao", lambda: consumed(pe, s, "o", 7))
                    for b in range(2):
                        gemm((s, "out", b), x_hi[0], x_lo[0], turned("swao"))
                elif s.startswith("ffn"):
                    turn_activations(s)
                    blocks = ffn_blocks()

                    def turn_gated(b):
                        for t in range(TT):
                            consumed(pe, (s, "v", b), t)
                        for i in range(blocks[b][1] // 256):
                            turn((s, "gt", b, i), g_tok[:, b % 2], 2 * i)

                    for b in range(len(blocks)):
                        gemm((s, "u", b), x_hi[0], x_lo[0], turned(s))
                        if b:
                            turn_gated(b - 1)
                        gemm((s, "v", b), x_hi[0], x_lo[0])
                    turn_gated(len(blocks) - 1)

                    def down(k0, kn):
                        b = min(k0 // 4, len(blocks) - 1)
                        consumed(pe, s, "gt", b, blocks[b][1] // 256 - 1)

                    for b in range(2):
                        gemm((s, "d", b), g_hi, g_lo, down)


_INS = ['x', 'p', 'rw_norm', 'rw_mu', 'rw_w_in', 'rw_w0', 'rw_w1', 'rw_w2', 'rw_a0', 'rw_a1', 'rw_a2', 'rw_k_k',
        'rw_k_a', 'rw_r_k', 'rw_ln_w', 'rw_ln_b', 'rw_w_out', 'da_norm', 'da_w_in', 'da_lq1', 'da_lk1', 'da_lq2',
        'da_lk2', 'da_subln', 'da_w_out', 'pe_norm', 'pe_w_gate', 'pe_w_proj', 'final_norm', 'ffn_norm_2',
        'ffn_w1_2', 'ffn_w3_2', 'ffn_w2_2', 'ssm_norm_2', 'ssm_w_in_2', 'ssm_conv_w_2', 'ssm_conv_b_2',
        'ssm_dt_bias_2', 'ssm_a_log_2', 'ssm_d_2', 'ssm_gate_norm_2', 'ssm_w_out_2', 'kv_norm_2', 'w_kv_2',
        'k_norm_2', 'attn_norm_2', 'w_q_2', 'q_norm_2', 'sinks_2', 'w_o_2', 'rel_bias_2']
_OUTS = [((1, T, D), 'float32')]


def kernel(**inputs):
    import numpy as _np
    import concourse.bacc as _bacc
    from concourse import mybir as _mybir
    from concourse.bass_utils import run_bass_kernel_spmd as _run

    nc = _bacc.Bacc("TRN2", target_bir_lowering=False, num_devices=1)
    arrays, args = {}, {}
    made = {"constants": constants, "bias_picks": bias_picks}
    for name in _INS + list(made):
        a = made[name]() if name in made else _np.asarray(inputs[name])
        if name == "ssm_conv_w_2":
            a = a.reshape(4, 24, P).transpose(2, 1, 0)
        if name == "ssm_conv_b_2":
            a = a.reshape(24, P).T
        if name == "rw_mu":
            a = a.reshape(6, KD, P).transpose(2, 0, 1)
        a = _np.ascontiguousarray(a)
        arrays[f"in_{name}_dram"] = a
        args[name] = nc.dram_tensor(f"in_{name}_dram", a.shape, _mybir.dt.from_np(a.dtype), kind="ExternalInput").ap()
    shape, dtype = _OUTS[0]
    out = nc.dram_tensor("out_0_dram", shape, _mybir.dt.from_np(_np.dtype(dtype)), kind="ExternalOutput").ap()
    program(nc, args, out)
    r = _run(nc, [arrays], core_ids=[0])
    return r.results[0]["out_0_dram"]
```
